# Optimizing a Trainium2 kernel written in Bass

```python
import jax, jax.numpy as jnp
from jax import lax
import numpy as np
import math
import jax
import jax.numpy as jnp

D_MODEL = 1024
BATCH = 1
SEQ = 256
DEPTH = 1

MIX_WIDTH = 512
N_BRANCH = 4
MLA_HEADS = 8
QK_NOPE = 64
QK_ROPE = 32
V_HEAD = 64
Q_LORA = 384
KV_LORA = 256
ROPE_THETA = 10000.0
Q_BLOCK = 128
POOL_WINDOWS = (2, 4, 8, 16)
POOL_GROUP = MIX_WIDTH // 4
SSD_HEADS = 8
SSD_HEADDIM = 64
SSD_GROUPS = 2
SSD_STATE = 64
SSD_CHUNK = 128
CONV_WIDTH = 4
SSD_XBC = SSD_HEADS * SSD_HEADDIM + 2 * SSD_GROUPS * SSD_STATE
LRU_BLOCKS = 8
LRU_BLOCK = MIX_WIDTH // LRU_BLOCKS
LRU_C = 8.0
D_FF = 4 * D_MODEL
PLE_DIM = 256
EPS = 1e-6

SPLIT_SIZES = (Q_LORA, KV_LORA, QK_ROPE,
               MIX_WIDTH,
               MIX_WIDTH, SSD_XBC, SSD_HEADS,
               MIX_WIDTH, MIX_WIDTH,
               N_BRANCH * D_MODEL)
IN_COLS = sum(SPLIT_SIZES)


def _split_points():
    pts, acc = [], 0
    for s in SPLIT_SIZES[:-1]:
        acc += s
        pts.append(acc)
    return pts

def rmsnorm(x, g):
    x32 = x.astype(jnp.float32)
    y = x32 * lax.rsqrt(jnp.mean(x32 * x32, axis=-1, keepdims=True) + EPS)
    return (y * g.astype(jnp.float32)).astype(x.dtype)

def causal_dwconv(x, w, b):
    c = x.shape[-1]
    y = lax.conv_general_dilated(x, w[:, None, :].astype(x.dtype), window_strides=(1,),
                                 padding=[(CONV_WIDTH - 1, 0)],
                                 dimension_numbers=('NWC', 'WIO', 'NWC'),
                                 feature_group_count=c)
    return y + b.astype(x.dtype)

def rope_tables(positions):
    inv = 1.0 / (ROPE_THETA ** (jnp.arange(0, QK_ROPE, 2, dtype=jnp.float32) / QK_ROPE))
    ang = positions.astype(jnp.float32)[..., None] * inv
    return jnp.cos(ang), jnp.sin(ang)

def apply_rope(x, cos, sin):
    x32 = x.astype(jnp.float32)
    x1, x2 = jnp.split(x32, 2, axis=-1)
    out = jnp.concatenate([x1 * cos - x2 * sin, x2 * cos + x1 * sin], axis=-1)
    return out.astype(x.dtype)

def mla_mixer(c_q, c_kv, k_r, cos, sin, q_norm, w_uq, kv_norm, w_ukv):
    b, s, _ = c_q.shape
    q = (rmsnorm(c_q, q_norm) @ w_uq).reshape(b, s, MLA_HEADS, QK_NOPE + QK_ROPE)
    q_nope = q[..., :QK_NOPE]
    q_rope = apply_rope(q[..., QK_NOPE:], cos[:, :, None], sin[:, :, None])
    kv = (rmsnorm(c_kv, kv_norm) @ w_ukv).reshape(b, s, MLA_HEADS, QK_NOPE + V_HEAD)
    k_nope, v = kv[..., :QK_NOPE], kv[..., QK_NOPE:]
    k_rope = apply_rope(k_r, cos, sin)
    scale = (QK_NOPE + QK_ROPE) ** -0.5
    outs = []
    for blk in range(s // Q_BLOCK):
        q0, kend = blk * Q_BLOCK, (blk + 1) * Q_BLOCK
        sc = (jnp.einsum('bqhd,bkhd->bhqk', q_nope[:, q0:kend], k_nope[:, :kend])
              + jnp.einsum('bqhd,bkd->bhqk', q_rope[:, q0:kend], k_rope[:, :kend]))
        sc = sc.astype(jnp.float32) * scale
        qi = q0 + jnp.arange(Q_BLOCK)[:, None]
        ki = jnp.arange(kend)[None, :]
        sc = jnp.where(ki <= qi, sc, -jnp.inf)
        pr = jax.nn.softmax(sc, axis=-1).astype(v.dtype)
        outs.append(jnp.einsum('bhqk,bkhd->bqhd', pr, v[:, :kend]))
    o = jnp.concatenate(outs, axis=1)
    return o.reshape(b, s, MLA_HEADS * V_HEAD)

def pool_mixer(u, w_pool, pool_scale):
    b, s, _ = u.shape
    u32 = u.astype(jnp.float32)
    maxw = max(POOL_WINDOWS)
    cs = jnp.pad(jnp.cumsum(u32, axis=1), ((0, 0), (maxw, 0), (0, 0)))
    t = jnp.arange(s)
    groups = []
    for g, w in enumerate(POOL_WINDOWS):
        sl = slice(g * POOL_GROUP, (g + 1) * POOL_GROUP)
        win_sum = cs[:, maxw:, sl] - cs[:, maxw - w:maxw - w + s, sl]
        count = jnp.minimum(t + 1, w).astype(jnp.float32)[None, :, None]
        groups.append(win_sum / count - u32[..., sl])
    d = jnp.stack(groups, axis=2).astype(u.dtype)
    y = jnp.einsum('bsgc,gcd->bsgd', d, w_pool).reshape(b, s, MIX_WIDTH)
    return y * pool_scale

def segsum(a):
    t = a.shape[-1]
    cs = jnp.cumsum(a, axis=-1)
    diff = cs[..., :, None] - cs[..., None, :]
    mask = jnp.tril(jnp.ones((t, t), dtype=bool))
    return jnp.where(mask, diff, -jnp.inf)

def ssd_mixer(z, xbc, dt, conv_w, conv_b, dt_bias, a_log, d_skip, norm_g):
    b, s, _ = z.shape
    nc, lc, g, r, n, hp = s // SSD_CHUNK, SSD_CHUNK, SSD_GROUPS, SSD_HEADS // SSD_GROUPS, SSD_STATE, SSD_HEADDIM
    xbc = jax.nn.silu(causal_dwconv(xbc, conv_w, conv_b)).astype(jnp.float32)
    xs = xbc[..., :MIX_WIDTH]
    bm = xbc[..., MIX_WIDTH:MIX_WIDTH + g * n].reshape(b, nc, lc, g, n)
    cm = xbc[..., MIX_WIDTH + g * n:].reshape(b, nc, lc, g, n)
    dt = jax.nn.softplus(dt.astype(jnp.float32) + dt_bias.astype(jnp.float32))
    a_head = -jnp.exp(a_log.astype(jnp.float32))
    x = xs.reshape(b, nc, lc, g, r, hp)
    xdt = x * dt.reshape(b, nc, lc, g, r)[..., None]
    a = (dt * a_head).reshape(b, nc, lc, g, r).transpose(0, 3, 4, 1, 2)
    a_cs = jnp.cumsum(a, axis=-1)
    lmat = jnp.exp(segsum(a))
    cb = jnp.einsum('bclgn,bcsgn->bgcls', cm, bm)
    y_diag = jnp.einsum('bgrcls,bcsgrp->bclgrp', cb[:, :, None] * lmat, xdt)
    decay_states = jnp.exp(a_cs[..., -1:] - a_cs)
    states = jnp.einsum('bclgn,bgrcl,bclgrp->bcgrpn', bm, decay_states, xdt)
    states = jnp.concatenate([jnp.zeros_like(states[:, :1]), states], axis=1)
    chunk_a = jnp.pad(a_cs[..., -1], ((0, 0), (0, 0), (0, 0), (1, 0)))
    decay_chunk = jnp.exp(segsum(chunk_a))
    states = jnp.einsum('bgrzc,bcgrpn->bzgrpn', decay_chunk, states)[:, :-1]
    y_off = jnp.einsum('bclgn,bcgrpn,bgrcl->bclgrp', cm, states, jnp.exp(a_cs))
    y = (y_diag + y_off).reshape(b, s, SSD_HEADS, hp) \
        + xs.reshape(b, s, SSD_HEADS, hp) * d_skip.astype(jnp.float32)[:, None]
    y = y.reshape(b, s, MIX_WIDTH) * jax.nn.silu(z.astype(jnp.float32))
    return rmsnorm(y, norm_g).astype(z.dtype)

def rglru_mixer(gate_in, x_in, conv_w, conv_b, w_a, b_a, w_i, b_i, lam):
    b, s, _ = x_in.shape
    gate = jax.nn.gelu(gate_in)
    xc = causal_dwconv(x_in, conv_w, conv_b)
    xb = xc.reshape(b, s, LRU_BLOCKS, LRU_BLOCK)
    r_t = jax.nn.sigmoid((jnp.einsum('bshi,hij->bshj', xb, w_a).reshape(b, s, MIX_WIDTH) + b_a).astype(jnp.float32))
    i_t = jax.nn.sigmoid((jnp.einsum('bshi,hij->bshj', xb, w_i).reshape(b, s, MIX_WIDTH) + b_i).astype(jnp.float32))
    log_a = -LRU_C * r_t * jax.nn.softplus(-lam.astype(jnp.float32))
    a_t = jnp.exp(log_a)
    mult = jnp.sqrt(-jnp.expm1(2.0 * log_a))
    u = xc.astype(jnp.float32) * i_t * mult

    def combine(lhs, rhs):
        a1, b1 = lhs
        a2, b2 = rhs
        return a1 * a2, a2 * b1 + b2

    _, h = lax.associative_scan(combine, (a_t, u), axis=1)
    return h.astype(x_in.dtype) * gate

def first_inputs(seed: int = 0) -> dict:
    key = jax.random.key(seed)
    ks = iter(jax.random.split(key, 48))
    f32 = jnp.float32

    def nrm(shape, fan_in):
        return jax.random.normal(next(ks), shape, f32) * (fan_in ** -0.5)

    def gain(shape):
        return 1.0 + 0.05 * jax.random.normal(next(ks), shape, f32)

    def small(shape):
        return 0.01 * jax.random.normal(next(ks), shape, f32)

    L = DEPTH
    x = jax.random.normal(next(ks), (BATCH, SEQ, D_MODEL), f32)
    p = jax.random.normal(next(ks), (DEPTH, BATCH, SEQ, PLE_DIM), f32)
    offs = jax.random.randint(next(ks), (BATCH, 1), 0, 1024, dtype=jnp.int32)
    positions = (offs + jnp.arange(SEQ, dtype=jnp.int32)[None, :]).astype(jnp.int32)
    dt0 = jnp.exp(jax.random.uniform(next(ks), (L, SSD_HEADS), f32, np.log(1e-3), np.log(1e-1)))
    dt_bias = dt0 + jnp.log(-jnp.expm1(-dt0))
    a_log = jnp.log(jax.random.uniform(next(ks), (L, SSD_HEADS), f32, 1.0, 16.0))
    a_pow = jax.random.uniform(next(ks), (L, MIX_WIDTH), f32, 0.9, 0.999) ** (1.0 / LRU_C)
    lam = jnp.log(a_pow) - jnp.log1p(-a_pow)
    return {
        "x": x,
        "p": p,
        "positions": positions,
        "g_mix": gain((L, D_MODEL)),
        "w_in": nrm((L, D_MODEL, IN_COLS), D_MODEL),
        "q_norm": gain((L, Q_LORA)),
        "w_uq": nrm((L, Q_LORA, MLA_HEADS * (QK_NOPE + QK_ROPE)), Q_LORA),
        "kv_norm": gain((L, KV_LORA)),
        "w_ukv": nrm((L, KV_LORA, MLA_HEADS * (QK_NOPE + V_HEAD)), KV_LORA),
        "w_pool": nrm((L, 4, POOL_GROUP, POOL_GROUP), POOL_GROUP),
        "pool_scale": 1.0 + 0.1 * jax.random.normal(next(ks), (L, MIX_WIDTH), f32),
        "ssd_conv_w": nrm((L, CONV_WIDTH, SSD_XBC), CONV_WIDTH),
        "ssd_conv_b": small((L, SSD_XBC)),
        "ssd_dt_bias": dt_bias,
        "ssd_a_log": a_log,
        "ssd_d": gain((L, SSD_HEADS)),
        "ssd_norm": gain((L, MIX_WIDTH)),
        "lru_conv_w": nrm((L, CONV_WIDTH, MIX_WIDTH), CONV_WIDTH),
        "lru_conv_b": small((L, MIX_WIDTH)),
        "lru_w_a": nrm((L, LRU_BLOCKS, LRU_BLOCK, LRU_BLOCK), LRU_BLOCK),
        "lru_b_a": small((L, MIX_WIDTH)),
        "lru_w_i": nrm((L, LRU_BLOCKS, LRU_BLOCK, LRU_BLOCK), LRU_BLOCK),
        "lru_b_i": small((L, MIX_WIDTH)),
        "lru_lambda": lam,
        "w_branch": nrm((L, N_BRANCH, MIX_WIDTH, D_MODEL), MIX_WIDTH),
        "w_out": nrm((L, D_MODEL, D_MODEL), D_MODEL),
        "g_mlp": gain((L, D_MODEL)),
        "w_ff1": nrm((L, D_MODEL, D_FF), D_MODEL),
        "w_ff2": nrm((L, D_FF, D_MODEL), D_FF),
        "g_ple": gain((L, D_MODEL)),
        "w_ple_gate": nrm((L, D_MODEL, D_MODEL), D_MODEL),
        "w_ple": nrm((L, PLE_DIM, D_MODEL), PLE_DIM),
        "g_final": gain((D_MODEL,)),
    }

def first_block(x, p, positions, g_mix, w_in, q_norm, w_uq, kv_norm, w_ukv, w_pool, pool_scale,
              ssd_conv_w, ssd_conv_b, ssd_dt_bias, ssd_a_log, ssd_d, ssd_norm,
              lru_conv_w, lru_conv_b, lru_w_a, lru_b_a, lru_w_i, lru_b_i, lru_lambda,
              w_branch, w_out, g_mlp, w_ff1, w_ff2, g_ple, w_ple_gate, w_ple, g_final):
    b, s, _ = x.shape
    cos, sin = rope_tables(positions)
    pts = _split_points()
    for l in range(DEPTH):
        h = rmsnorm(x, g_mix[l])
        u = h @ w_in[l]
        c_q, c_kv, k_r, u_pool, z, xbc, dt, lru_g, lru_x, gates = jnp.split(u, pts, axis=-1)
        y_a = mla_mixer(c_q, c_kv, k_r, cos, sin, q_norm[l], w_uq[l], kv_norm[l], w_ukv[l])
        y_b = pool_mixer(u_pool, w_pool[l], pool_scale[l])
        y_c = ssd_mixer(z, xbc, dt, ssd_conv_w[l], ssd_conv_b[l], ssd_dt_bias[l], ssd_a_log[l],
                        ssd_d[l], ssd_norm[l])
        y_d = rglru_mixer(lru_g, lru_x, lru_conv_w[l], lru_conv_b[l], lru_w_a[l], lru_b_a[l],
                          lru_w_i[l], lru_b_i[l], lru_lambda[l])
        gates = jax.nn.sigmoid(gates.reshape(b, s, N_BRANCH, D_MODEL))
        merged = (gates[:, :, 0] * (y_a @ w_branch[l, 0])
                  + gates[:, :, 1] * (y_b @ w_branch[l, 1])
                  + gates[:, :, 2] * (y_c @ w_branch[l, 2])
                  + gates[:, :, 3] * (y_d @ w_branch[l, 3]))
        x = x + merged @ w_out[l]
        h2 = rmsnorm(x, g_mlp[l])
        x = x + jnp.square(jax.nn.relu(h2 @ w_ff1[l])) @ w_ff2[l]
        ple_gate = jax.nn.sigmoid(rmsnorm(x, g_ple[l]) @ w_ple_gate[l])
        x = x + (p[l] @ w_ple[l]) * ple_gate
    return rmsnorm(x, g_final)


DEPTH_2 = 2

HEAD_DIM = 64
N_HEADS = D_MODEL // HEAD_DIM
ATTN_WIDTH = N_HEADS * HEAD_DIM
ATTN_SCALE = HEAD_DIM ** -0.5
N_MIXERS = 4
ROW_CHUNK = 128
REL_BUCKETS = 32
REL_MAX_DIST = 2048
DILATED_PAIRS = ((128, 1), (512, 4), (2048, 16))
SB_CLIP = 60.0
NSA_KV_HEADS = 4
NSA_GROUP = N_HEADS // NSA_KV_HEADS
NSA_KV_WIDTH = NSA_KV_HEADS * HEAD_DIM
NSA_CMP_LEN = 32
NSA_CMP_STRIDE = 16
NSA_CMP_HIDDEN = 256
NSA_SEL_BLOCK = 64
NSA_TOP_N = 16
NSA_WINDOW = 512
MOBA_BLOCK = 256
MOBA_TOP_K = 3
N_EXPERTS = 16
N_GROUPS = 4
EXPERTS_PER_GROUP = N_EXPERTS // N_GROUPS
MOE_TOP_K = 2
D_EXPERT = 256
MOE_BLOCK = 256
DEEPNORM_ALPHA = (2 * DEPTH_2) ** 0.25
DEEPNORM_BETA = (8 * DEPTH_2) ** -0.25
LN_EPS = 1e-5
NEG_INF = -1e30
FORCED_SCORE = 1e9


def layer_norm(x, g, b):
    xf = x.astype(jnp.float32)
    mu = xf.mean(-1, keepdims=True)
    var = jnp.square(xf - mu).mean(-1, keepdims=True)
    return ((xf - mu) * lax.rsqrt(var + LN_EPS) * g + b).astype(x.dtype)

def rel_bucket(dist):
    n = jnp.maximum(dist, 0)
    exact = REL_BUCKETS // 2
    logf = jnp.log(jnp.maximum(n, 1).astype(jnp.float32) / exact) / math.log(REL_MAX_DIST / exact)
    large = jnp.minimum(exact + (logf * (REL_BUCKETS - exact)).astype(jnp.int32), REL_BUCKETS - 1)
    return jnp.where(n < exact, n, large)

def rel_bias(table, dist):
    return jnp.moveaxis(table[rel_bucket(dist)], -1, 0).astype(jnp.float32)

def masked_softmax(logits, mask):
    logits = jnp.where(mask, logits.astype(jnp.float32), NEG_INF)
    m = logits.max(-1, keepdims=True)
    p = jnp.where(mask, jnp.exp(logits - m), 0.0)
    denom = jnp.maximum(p.sum(-1, keepdims=True), 1e-30)
    return p / denom, m + jnp.log(denom)

def merge_parts(o, lse):
    w = jax.nn.softmax(lse.astype(jnp.float32), axis=1)
    return jnp.einsum('npr,nprd->nrd', w, o.astype(jnp.float32))

def split_heads(t, h):
    b, s, _ = t.shape
    return t.reshape(b, s, h, HEAD_DIM).transpose(0, 2, 1, 3)

def merge_heads(t):
    b, h, s, d = t.shape
    return t.transpose(0, 2, 1, 3).reshape(b, s, h * d)

def dispatch_attention(q_src, pos_src, gid, k_groups, v_groups, kstart, bias_tbl, tbl_idx):
    n_src, n_slots = gid.shape
    n_groups, blk, _ = k_groups.shape
    R = q_src.shape[1]
    N = n_src * n_slots
    flat_g = gid.reshape(N)
    order = jnp.argsort(flat_g).astype(jnp.int32)
    sorted_g = flat_g[order]
    valid = sorted_g < n_groups
    sg = jnp.minimum(sorted_g, n_groups - 1)
    counts = jnp.zeros((n_groups + 1,), jnp.int32).at[flat_g].add(1)[:n_groups]
    padded = (counts + ROW_CHUNK - 1) // ROW_CHUNK * ROW_CHUNK
    pad_end = jnp.cumsum(padded)
    pad_start = pad_end - padded
    start = jnp.cumsum(counts) - counts
    n_chunks = -(-N // ROW_CHUNK) + n_groups
    P = n_chunks * ROW_CHUNK
    dest = jnp.where(valid, pad_start[sg] + jnp.arange(N) - start[sg], P)
    buf = jnp.full((P,), N, jnp.int32).at[dest].set(order, mode='drop')
    chunk_group = jnp.minimum(jnp.searchsorted(pad_end, jnp.arange(n_chunks) * ROW_CHUNK, side='right'),
                              n_groups - 1).astype(jnp.int32)
    q_pad = jnp.concatenate([q_src, jnp.zeros((1, R, HEAD_DIM), q_src.dtype)], axis=0)
    pos_pad = jnp.concatenate([pos_src, jnp.full((1,), -1, pos_src.dtype)], axis=0)
    off = jnp.arange(blk)

    def chunk(args):
        rows, g = args
        src = rows // n_slots
        qi = q_pad[src]
        dist = pos_pad[src][:, None] - (kstart[g] + off)[None, :]
        bias = bias_tbl[tbl_idx[g]][:, rel_bucket(dist)].astype(jnp.float32)
        logits = jnp.einsum('crd,kd->rck', qi, k_groups[g]).astype(jnp.float32) * ATTN_SCALE + bias
        p, lse = masked_softmax(logits, (dist >= 0)[None])
        o = jnp.einsum('rck,kd->crd', p, v_groups[g].astype(jnp.float32))
        return o, lse[..., 0].T

    o, lse = lax.map(chunk, (buf.reshape(n_chunks, ROW_CHUNK), chunk_group))
    o_all = jnp.zeros((N + 1, R, HEAD_DIM), jnp.float32).at[buf].set(o.reshape(P, R, HEAD_DIM))[:N]
    lse_all = jnp.full((N + 1, R), NEG_INF, jnp.float32).at[buf].set(lse.reshape(P, R))[:N]
    return o_all.reshape(n_src, n_slots, R, HEAD_DIM), lse_all.reshape(n_src, n_slots, R)

def dilated_group(q, k, v, table, window, dilation):
    Bsz, H, S_, _ = q.shape
    L = S_ // dilation
    nb = -(-L // Q_BLOCK)
    Lp = nb * Q_BLOCK
    span = window // dilation
    n_prev = -(-span // Q_BLOCK)

    def streams(t):
        t = t.reshape(Bsz, H, L, dilation, HEAD_DIM).transpose(0, 1, 3, 2, 4)
        t = jnp.pad(t, ((0, 0), (0, 0), (0, 0), (0, Lp - L), (0, 0)))
        return t.reshape(Bsz, H, dilation, nb, Q_BLOCK, HEAD_DIM)

    def band(t):
        tp = jnp.pad(t, ((0, 0), (0, 0), (0, 0), (n_prev, 0), (0, 0), (0, 0)))
        return jnp.concatenate([tp[:, :, :, o:o + nb] for o in range(n_prev + 1)], axis=4)

    qs = streams(q)
    kb, vb = band(streams(k)), band(streams(v))
    a = jnp.arange(Q_BLOCK)
    c = jnp.arange((n_prev + 1) * Q_BLOCK)
    steps = n_prev * Q_BLOCK + a[:, None] - c[None, :]
    key_idx = jnp.arange(nb)[:, None] * Q_BLOCK - n_prev * Q_BLOCK + c[None, :]
    mask = ((steps >= 0) & (steps <= span))[None] & (key_idx >= 0)[:, None, :]
    bias = rel_bias(table, steps * dilation)
    logits = jnp.einsum('bhrnqd,bhrnkd->bhrnqk', qs, kb).astype(jnp.float32) * ATTN_SCALE + bias[:, None, None]
    p, lse = masked_softmax(logits, mask)
    o = jnp.einsum('bhrnqk,bhrnkd->bhrnqd', p.astype(v.dtype), vb)
    o = o.reshape(Bsz, H, dilation, Lp, HEAD_DIM)[:, :, :, :L].transpose(0, 1, 3, 2, 4).reshape(Bsz, H, S_, HEAD_DIM)
    lse = lse[..., 0].reshape(Bsz, H, dilation, Lp)[..., :L].transpose(0, 1, 3, 2).reshape(Bsz, H, S_)
    return o, lse

def mixer_dilated(x, w_in, w_out, table):
    proj = x @ w_in
    gw = 3 * ATTN_WIDTH
    outs, lses = [], []
    for g, (window, dilation) in enumerate(DILATED_PAIRS):
        q, k, v = [split_heads(t, N_HEADS) for t in jnp.split(proj[..., g * gw:(g + 1) * gw], 3, axis=-1)]
        o, lse = dilated_group(q, k, v, table, window, dilation)
        outs.append(o)
        lses.append(lse)
    wts = jax.nn.softmax(jnp.stack(lses), axis=0)
    o = jnp.einsum('gbhs,gbhsd->bhsd', wts, jnp.stack(outs).astype(jnp.float32))
    return merge_heads(o.astype(x.dtype)) @ w_out

def mixer_stick_breaking(x, w_in, w_out):
    q, k, v = [split_heads(t, N_HEADS) for t in jnp.split(x @ w_in, 3, axis=-1)]
    Bsz, H, S_, _ = q.shape
    nb = S_ // Q_BLOCK
    nbp = nb + nb % 2
    pad = ((0, 0), (0, 0), (0, (nbp - nb) * Q_BLOCK), (0, 0))

    def blocks(t):
        return jnp.pad(t, pad).reshape(Bsz, H, nbp, Q_BLOCK, HEAD_DIM)

    qb, kb, vb = blocks(q * ATTN_SCALE), blocks(k), blocks(v)
    a = jnp.arange(Q_BLOCK)
    strict = a[None, :] < a[:, None]
    suffix = (a[:, None] >= a[None, :]).astype(jnp.float32)

    z = jnp.clip(jnp.einsum('bhnqd,bhnkd->bhnqk', qb, kb).astype(jnp.float32), -SB_CLIP, SB_CLIP)
    sp = jnp.where(strict, jnp.log1p(jnp.exp(z)), 0.0)
    r_in = jnp.einsum('bhnqj,js->bhnqs', sp, suffix)
    att = jnp.where(strict, jnp.exp(z - r_in), 0.0)
    acc_d = jnp.einsum('bhnqs,bhnsd->bhnqd', att, vb.astype(jnp.float32))
    r_d = r_in[..., 0]

    def pair(p):
        qb2 = nbp - 1 - p
        init_r2 = lax.dynamic_index_in_dim(r_d, qb2, axis=2, keepdims=False)
        init_a2 = lax.dynamic_index_in_dim(acc_d, qb2, axis=2, keepdims=False)

        def step(carry, kstep):
            r_sum, acc, acc_first = carry
            start2 = kstep == p
            acc_first = jnp.where(start2, acc, acc_first)
            r_sum = jnp.where(start2, init_r2, r_sum)
            acc = jnp.where(start2, init_a2, acc)
            first = kstep < p
            qi = jnp.where(first, p, qb2)
            kj = jnp.where(first, p - 1 - kstep, nbp - 2 - kstep)
            qblk = lax.dynamic_index_in_dim(qb, qi, axis=2, keepdims=False)
            kblk = lax.dynamic_index_in_dim(kb, kj, axis=2, keepdims=False)
            vblk = lax.dynamic_index_in_dim(vb, kj, axis=2, keepdims=False)
            zz = jnp.clip(jnp.einsum('bhqd,bhkd->bhqk', qblk, kblk).astype(jnp.float32), -SB_CLIP, SB_CLIP)
            rr = jnp.einsum('bhqj,js->bhqs', jnp.log1p(jnp.exp(zz)), suffix)
            pv = jnp.einsum('bhqs,bhsd->bhqd', jnp.exp(zz - rr), vblk.astype(jnp.float32))
            acc = acc + jnp.exp(-r_sum)[..., None] * pv
            r_sum = r_sum + rr[..., 0]
            return (r_sum, acc, acc_first), None

        init = (lax.dynamic_index_in_dim(r_d, p, axis=2, keepdims=False),
                lax.dynamic_index_in_dim(acc_d, p, axis=2, keepdims=False),
                jnp.zeros((Bsz, H, Q_BLOCK, HEAD_DIM), jnp.float32))
        (_, acc_b, acc_a), _ = lax.scan(step, init, jnp.arange(nbp - 1))
        return acc_a, acc_b

    out_a, out_b = lax.map(pair, jnp.arange(nbp // 2))
    o = jnp.concatenate([out_a, out_b[::-1]], axis=0)
    o = o.transpose(1, 2, 0, 3, 4).reshape(Bsz, H, nbp * Q_BLOCK, HEAD_DIM)[:, :, :S_]
    return merge_heads(o.astype(x.dtype)) @ w_out

def compress_blocks(t, pos, w1, w2):
    Bsz, G, S_, _ = t.shape
    halves = t.reshape(Bsz, G, S_ // NSA_CMP_STRIDE, NSA_CMP_STRIDE, HEAD_DIM)
    blocks = jnp.concatenate([halves[:, :, :-1], halves[:, :, 1:]], axis=3) + pos
    n_cmp = blocks.shape[2]
    flat = blocks.reshape(Bsz, G, n_cmp, NSA_CMP_LEN * HEAD_DIM)
    return jax.nn.gelu(flat @ w1) @ w2

def mixer_nsa(x, w_in, w_out, table, pos_k, w1_k, w2_k, pos_v, w1_v, w2_v):
    Bsz, S_, _ = x.shape
    G, R = NSA_KV_HEADS, NSA_GROUP
    proj = x @ w_in
    q = proj[..., :ATTN_WIDTH].reshape(Bsz, S_, G, R, HEAD_DIM).transpose(0, 2, 3, 1, 4)
    kv = jnp.split(proj[..., ATTN_WIDTH:ATTN_WIDTH + 6 * NSA_KV_WIDTH], 6, axis=-1)
    k_cmp, v_cmp, k_sel, v_sel, k_win, v_win = [split_heads(t, G) for t in kv]
    gates = jax.nn.sigmoid(proj[..., ATTN_WIDTH + 6 * NSA_KV_WIDTH:].astype(jnp.float32))
    gates = gates.reshape(Bsz, S_, 3, G, R).transpose(2, 0, 3, 4, 1)

    kc = compress_blocks(k_cmp, pos_k, w1_k, w2_k)
    vc = compress_blocks(v_cmp, pos_v, w1_v, w2_v)
    n_cmp = kc.shape[2]
    cmp_end = jnp.arange(n_cmp) * NSA_CMP_STRIDE + NSA_CMP_LEN - 1
    n_sel_blocks = S_ // NSA_SEL_BLOCK
    n_top = min(NSA_TOP_N, n_sel_blocks)
    offs = np.arange(1 - NSA_CMP_LEN // NSA_CMP_STRIDE, NSA_SEL_BLOCK // NSA_CMP_STRIDE)
    ov = np.arange(n_sel_blocks)[:, None] * (NSA_SEL_BLOCK // NSA_CMP_STRIDE) + offs[None]
    ov_valid = jnp.asarray((ov >= 0) & (ov < n_cmp))
    ov_idx = jnp.asarray(np.clip(ov, 0, n_cmp - 1))
    kwin = jnp.pad(k_win, ((0, 0), (0, 0), (NSA_WINDOW, 0), (0, 0)))
    vwin = jnp.pad(v_win, ((0, 0), (0, 0), (NSA_WINDOW, 0), (0, 0)))
    table_gr = table.T.reshape(G, R, REL_BUCKETS)
    nb = S_ // Q_BLOCK
    win_len = NSA_WINDOW + Q_BLOCK
    a = jnp.arange(Q_BLOCK)
    win_steps = NSA_WINDOW + a[:, None] - jnp.arange(win_len)[None, :]
    win_bias = rel_bias(table, win_steps).reshape(G, R, Q_BLOCK, win_len)
    sel_j = jnp.arange(n_sel_blocks)
    qb = q.reshape(Bsz, G, R, nb, Q_BLOCK, HEAD_DIM).transpose(3, 0, 1, 2, 4, 5)

    def block(args):
        qi, i = args
        qpos = i * Q_BLOCK + a
        cdist = qpos[:, None] - cmp_end[None, :]
        lc = jnp.einsum('bgrqd,bgcd->bgrqc', qi, kc).astype(jnp.float32) * ATTN_SCALE
        lc = lc + rel_bias(table, cdist).reshape(G, R, Q_BLOCK, n_cmp)
        pc, _ = masked_softmax(lc, cdist >= 0)
        o_cmp = jnp.einsum('bgrqc,bgcd->bgrqd', pc, vc.astype(jnp.float32))
        imp = (pc.sum(2)[..., ov_idx] * ov_valid).sum(-1)
        cur = qpos // NSA_SEL_BLOCK
        forced = (sel_j[None] == 0) | (sel_j[None] == cur[:, None]) | (sel_j[None] == cur[:, None] - 1)
        causal = sel_j[None] * NSA_SEL_BLOCK <= qpos[:, None]
        score = jnp.where(forced, FORCED_SCORE, jnp.where(causal, imp, NEG_INF))
        sel = lax.top_k(score, n_top)[1]
        kw = lax.dynamic_slice_in_dim(kwin, i * Q_BLOCK, win_len, axis=2)
        vw = lax.dynamic_slice_in_dim(vwin, i * Q_BLOCK, win_len, axis=2)
        wmask = (win_steps < NSA_WINDOW) & (win_steps >= 0) & (qpos[:, None] - win_steps >= 0)
        lw = jnp.einsum('bgrqd,bgkd->bgrqk', qi, kw).astype(jnp.float32) * ATTN_SCALE + win_bias
        pw, _ = masked_softmax(lw, wmask)
        o_win = jnp.einsum('bgrqk,bgkd->bgrqd', pw, vw.astype(jnp.float32))
        return o_cmp, o_win, sel

    o_cmp, o_win, sel = lax.map(block, (qb, jnp.arange(nb)))

    def unblock(t):
        return t.transpose(1, 2, 3, 0, 4, 5).reshape(Bsz, G, R, S_, HEAD_DIM)

    o_cmp, o_win = unblock(o_cmp), unblock(o_win)
    sel = sel.transpose(1, 2, 0, 3, 4).reshape(Bsz, G, S_, n_top)
    qpos_all = jnp.arange(S_)
    valid = sel * NSA_SEL_BLOCK <= qpos_all[:, None]
    n_groups = Bsz * G * n_sel_blocks
    bg = jnp.arange(Bsz * G).reshape(Bsz, G, 1, 1)
    gid = jnp.where(valid, bg * n_sel_blocks + sel, n_groups).reshape(Bsz * G * S_, n_top)
    q_src = q.transpose(0, 1, 3, 2, 4).reshape(Bsz * G * S_, R, HEAD_DIM)
    o_s, lse_s = dispatch_attention(
        q_src, jnp.tile(qpos_all, Bsz * G), gid,
        k_sel.reshape(n_groups, NSA_SEL_BLOCK, HEAD_DIM), v_sel.reshape(n_groups, NSA_SEL_BLOCK, HEAD_DIM),
        jnp.tile(jnp.arange(n_sel_blocks) * NSA_SEL_BLOCK, Bsz * G), table_gr,
        (jnp.arange(n_groups) // n_sel_blocks) % G)
    o_sel = merge_parts(o_s, lse_s).reshape(Bsz, G, S_, R, HEAD_DIM).transpose(0, 1, 3, 2, 4)
    out = gates[0][..., None] * o_cmp + gates[1][..., None] * o_sel + gates[2][..., None] * o_win
    return out.transpose(0, 3, 1, 2, 4).reshape(Bsz, S_, ATTN_WIDTH).astype(x.dtype) @ w_out

def mixer_moba(x, w_in, w_out, table):
    Bsz, S_, _ = x.shape
    H = N_HEADS
    q, k, v = [split_heads(t, H) for t in jnp.split(x @ w_in, 3, axis=-1)]
    nblk = -(-S_ // MOBA_BLOCK)
    Sp = nblk * MOBA_BLOCK
    pad = ((0, 0), (0, 0), (0, Sp - S_), (0, 0))
    qblk = jnp.pad(q, pad).reshape(Bsz, H, nblk, MOBA_BLOCK, HEAD_DIM)
    kblk = jnp.pad(k, pad).reshape(Bsz, H, nblk, MOBA_BLOCK, HEAD_DIM)
    vblk = jnp.pad(v, pad).reshape(Bsz, H, nblk, MOBA_BLOCK, HEAD_DIM)
    c = jnp.arange(MOBA_BLOCK)
    own_dist = c[:, None] - c[None, :]
    lo = jnp.einsum('bhnqd,bhnkd->bhnqk', qblk, kblk).astype(jnp.float32) * ATTN_SCALE + rel_bias(table, own_dist)[:, None]
    p_own, lse_own = masked_softmax(lo, own_dist >= 0)
    o_own = jnp.einsum('bhnqk,bhnkd->bhnqd', p_own, vblk.astype(jnp.float32)).reshape(Bsz, H, Sp, HEAD_DIM)[:, :, :S_]
    lse_own = lse_own[..., 0].reshape(Bsz, H, Sp)[:, :, :S_]
    kmean = kblk.mean(axis=3)
    n_top = max(1, min(MOBA_TOP_K, nblk - 1))
    cur = jnp.arange(S_) // MOBA_BLOCK
    gate = jnp.einsum('bhsd,bhnd->bhsn', q, kmean).astype(jnp.float32)
    gate = jnp.where(jnp.arange(nblk)[None, :] < cur[:, None], gate, NEG_INF)
    sel = lax.top_k(gate, n_top)[1]
    valid = sel < cur[:, None]
    n_groups = Bsz * H * nblk
    bh = jnp.arange(Bsz * H).reshape(Bsz, H, 1, 1)
    gid = jnp.where(valid, bh * nblk + sel, n_groups).reshape(Bsz * H * S_, n_top)
    o_sel, lse_sel = dispatch_attention(
        q.reshape(Bsz * H * S_, 1, HEAD_DIM), jnp.tile(jnp.arange(S_), Bsz * H), gid,
        kblk.reshape(n_groups, MOBA_BLOCK, HEAD_DIM), vblk.reshape(n_groups, MOBA_BLOCK, HEAD_DIM),
        jnp.tile(jnp.arange(nblk) * MOBA_BLOCK, Bsz * H), table.T[:, None, :],
        (jnp.arange(n_groups) // nblk) % H)
    o_all = jnp.concatenate([o_own.reshape(Bsz * H * S_, 1, 1, HEAD_DIM), o_sel], axis=1)
    lse_all = jnp.concatenate([lse_own.reshape(Bsz * H * S_, 1, 1), lse_sel], axis=1)
    o = merge_parts(o_all, lse_all).reshape(Bsz, H, S_, HEAD_DIM)
    return merge_heads(o.astype(x.dtype)) @ w_out

def moe_ffn(x, router_w, router_b, w_gate, w_up, w_down):
    Bsz, S_, D_ = x.shape
    T = Bsz * S_
    xt = x.reshape(T, D_)
    scores = jax.nn.sigmoid((xt @ router_w).astype(jnp.float32))
    biased = (scores + router_b.astype(jnp.float32)).reshape(T, N_GROUPS, EXPERTS_PER_GROUP)
    group_score = lax.top_k(biased, MOE_TOP_K)[0].sum(-1)
    best_group = jnp.argmax(group_score, axis=-1).astype(jnp.int32)
    in_group = jnp.take_along_axis(biased, best_group[:, None, None], axis=1)[:, 0]
    local = lax.top_k(in_group, MOE_TOP_K)[1]
    expert_idx = best_group[:, None] * EXPERTS_PER_GROUP + local
    gate = jnp.take_along_axis(scores, expert_idx, axis=1)
    gate = gate / gate.sum(-1, keepdims=True)
    n_assign = T * MOE_TOP_K
    flat_e = expert_idx.reshape(n_assign)
    order = jnp.argsort(flat_e)
    sorted_e = flat_e[order]
    sorted_tok = (order // MOE_TOP_K).astype(jnp.int32)
    sorted_w = gate.reshape(n_assign)[order]
    counts = jnp.zeros((N_EXPERTS,), jnp.int32).at[flat_e].add(1)
    padded = (counts + MOE_BLOCK - 1) // MOE_BLOCK * MOE_BLOCK
    pad_end = jnp.cumsum(padded)
    pad_start = pad_end - padded
    start = jnp.cumsum(counts) - counts
    dest = pad_start[sorted_e] + jnp.arange(n_assign) - start[sorted_e]
    n_blocks = -(-n_assign // MOE_BLOCK) + N_EXPERTS
    P = n_blocks * MOE_BLOCK
    buf_tok = jnp.full((P,), T, jnp.int32).at[dest].set(sorted_tok)
    buf_w = jnp.zeros((P,), x.dtype).at[dest].set(sorted_w.astype(x.dtype))
    block_expert = jnp.minimum(jnp.searchsorted(pad_end, jnp.arange(n_blocks) * MOE_BLOCK, side='right'), N_EXPERTS - 1)
    x_pad = jnp.concatenate([xt, jnp.zeros((1, D_), xt.dtype)], axis=0)
    xb = x_pad[buf_tok].reshape(n_blocks, MOE_BLOCK, D_)

    def expert_block(args):
        xi, e = args
        return (jax.nn.silu(xi @ w_gate[e]) * (xi @ w_up[e])) @ w_down[e]

    yb = lax.map(expert_block, (xb, block_expert)).reshape(P, D_) * buf_w[:, None]
    y = jnp.zeros((T + 1, D_), yb.dtype).at[buf_tok].add(yb)[:T]
    return y.reshape(Bsz, S_, D_)

def second_inputs(seed: int = 0) -> dict:
    key = jax.random.key(seed)
    ks = jax.random.split(key, 26)
    n_occ = [len(range(m, DEPTH_2, N_MIXERS)) for m in range(N_MIXERS)]
    beta = DEEPNORM_BETA

    def normal(k, shape, scale):
        return jax.random.normal(k, shape, jnp.float32) * scale

    def col_scale(pieces):
        return jnp.asarray(np.concatenate([np.full((w,), s, np.float32) for w, s in pieces]))

    qkv_pieces = [(ATTN_WIDTH, 1.0), (ATTN_WIDTH, 1.0), (ATTN_WIDTH, beta)]
    dil_scale = col_scale(qkv_pieces * len(DILATED_PAIRS))
    qkv_scale = col_scale(qkv_pieces)
    nsa_scale = col_scale([(ATTN_WIDTH, 1.0)] + [(NSA_KV_WIDTH, 1.0), (NSA_KV_WIDTH, beta)] * 3 + [(3 * N_HEADS, 1.0)])
    din = D_MODEL ** -0.5
    out_scale = ATTN_WIDTH ** -0.5 * beta
    cmp_in = NSA_CMP_LEN * HEAD_DIM
    return {
        'x': normal(ks[0], (BATCH, SEQ, D_MODEL), 1.0),
        'rel_table': normal(ks[1], (REL_BUCKETS, N_HEADS), 0.1),
        'router_w': normal(ks[2], (D_MODEL, N_EXPERTS), din),
        'router_b': normal(ks[3], (N_EXPERTS,), 0.01),
        'ln1_g': 1.0 + normal(ks[4], (DEPTH_2, D_MODEL), 0.01),
        'ln1_b': normal(ks[5], (DEPTH_2, D_MODEL), 0.01),
        'ln2_g': 1.0 + normal(ks[6], (DEPTH_2, D_MODEL), 0.01),
        'ln2_b': normal(ks[7], (DEPTH_2, D_MODEL), 0.01),
        'exp_w_gate': normal(ks[8], (DEPTH_2, N_EXPERTS, D_MODEL, D_EXPERT), din),
        'exp_w_up': normal(ks[9], (DEPTH_2, N_EXPERTS, D_MODEL, D_EXPERT), din),
        'exp_w_down': normal(ks[10], (DEPTH_2, N_EXPERTS, D_EXPERT, D_MODEL), D_EXPERT ** -0.5 * beta),
        'dil_w_in': normal(ks[11], (n_occ[0], D_MODEL, 3 * len(DILATED_PAIRS) * ATTN_WIDTH), din) * dil_scale,
        'dil_w_out': normal(ks[12], (n_occ[0], ATTN_WIDTH, D_MODEL), out_scale),
        'sb_w_in': normal(ks[13], (n_occ[1], D_MODEL, 3 * ATTN_WIDTH), din) * qkv_scale,
        'sb_w_out': normal(ks[14], (n_occ[1], ATTN_WIDTH, D_MODEL), out_scale),
        'nsa_w_in': normal(ks[15], (n_occ[2], D_MODEL, ATTN_WIDTH + 6 * NSA_KV_WIDTH + 3 * N_HEADS), din) * nsa_scale,
        'nsa_w_out': normal(ks[16], (n_occ[2], ATTN_WIDTH, D_MODEL), out_scale),
        'nsa_cmp_pos_k': normal(ks[17], (n_occ[2], NSA_CMP_LEN, HEAD_DIM), 0.1),
        'nsa_cmp_w1_k': normal(ks[18], (n_occ[2], cmp_in, NSA_CMP_HIDDEN), cmp_in ** -0.5),
        'nsa_cmp_w2_k': normal(ks[19], (n_occ[2], NSA_CMP_HIDDEN, HEAD_DIM), NSA_CMP_HIDDEN ** -0.5),
        'nsa_cmp_pos_v': normal(ks[20], (n_occ[2], NSA_CMP_LEN, HEAD_DIM), 0.1),
        'nsa_cmp_w1_v': normal(ks[21], (n_occ[2], cmp_in, NSA_CMP_HIDDEN), cmp_in ** -0.5),
        'nsa_cmp_w2_v': normal(ks[22], (n_occ[2], NSA_CMP_HIDDEN, HEAD_DIM), NSA_CMP_HIDDEN ** -0.5),
        'moba_w_in': normal(ks[23], (n_occ[3], D_MODEL, 3 * ATTN_WIDTH), din) * qkv_scale,
        'moba_w_out': normal(ks[24], (n_occ[3], ATTN_WIDTH, D_MODEL), out_scale),
    }

def second_block(x, rel_table, router_w, router_b, ln1_g, ln1_b, ln2_g, ln2_b,
              exp_w_gate, exp_w_up, exp_w_down, dil_w_in, dil_w_out, sb_w_in, sb_w_out,
              nsa_w_in, nsa_w_out, nsa_cmp_pos_k, nsa_cmp_w1_k, nsa_cmp_w2_k,
              nsa_cmp_pos_v, nsa_cmp_w1_v, nsa_cmp_w2_v, moba_w_in, moba_w_out):
    for layer in range(DEPTH_2):
        kind, occ = layer % N_MIXERS, layer // N_MIXERS
        if kind == 0:
            mixed = mixer_dilated(x, dil_w_in[occ], dil_w_out[occ], rel_table)
        elif kind == 1:
            mixed = mixer_stick_breaking(x, sb_w_in[occ], sb_w_out[occ])
        elif kind == 2:
            mixed = mixer_nsa(x, nsa_w_in[occ], nsa_w_out[occ], rel_table,
                              nsa_cmp_pos_k[occ], nsa_cmp_w1_k[occ], nsa_cmp_w2_k[occ],
                              nsa_cmp_pos_v[occ], nsa_cmp_w1_v[occ], nsa_cmp_w2_v[occ])
        else:
            mixed = mixer_moba(x, moba_w_in[occ], moba_w_out[occ], rel_table)
        x = layer_norm(DEEPNORM_ALPHA * x + mixed, ln1_g[layer], ln1_b[layer])
        ffn = moe_ffn(x, router_w, router_b, exp_w_gate[layer], exp_w_up[layer], exp_w_down[layer])
        x = layer_norm(DEEPNORM_ALPHA * x + ffn, ln2_g[layer], ln2_b[layer])
    return x


def setup_inputs(seed=0):
    out = dict(first_inputs(seed))
    for name, value in second_inputs(seed + 1).items():
        if name != "x":
            out[name + "_2"] = value
    return out


def reference(
    x, p, positions, g_mix, w_in, q_norm, w_uq, kv_norm, w_ukv, w_pool, pool_scale, ssd_conv_w,
    ssd_conv_b, ssd_dt_bias, ssd_a_log, ssd_d, ssd_norm, lru_conv_w, lru_conv_b, lru_w_a,
    lru_b_a, lru_w_i, lru_b_i, lru_lambda, w_branch, w_out, g_mlp, w_ff1, w_ff2, g_ple,
    w_ple_gate, w_ple, g_final, rel_table_2, router_w_2, router_b_2, ln1_g_2, ln1_b_2, ln2_g_2,
    ln2_b_2, exp_w_gate_2, exp_w_up_2, exp_w_down_2, dil_w_in_2, dil_w_out_2, sb_w_in_2,
    sb_w_out_2, nsa_w_in_2, nsa_w_out_2, nsa_cmp_pos_k_2, nsa_cmp_w1_k_2, nsa_cmp_w2_k_2,
    nsa_cmp_pos_v_2, nsa_cmp_w1_v_2, nsa_cmp_w2_v_2, moba_w_in_2, moba_w_out_2,
):
    x = first_block(
        x, p, positions, g_mix, w_in, q_norm, w_uq, kv_norm, w_ukv, w_pool, pool_scale,
        ssd_conv_w, ssd_conv_b, ssd_dt_bias, ssd_a_log, ssd_d, ssd_norm, lru_conv_w, lru_conv_b,
        lru_w_a, lru_b_a, lru_w_i, lru_b_i, lru_lambda, w_branch, w_out, g_mlp, w_ff1, w_ff2,
        g_ple, w_ple_gate, w_ple, g_final,
    )
    return second_block(
        x, rel_table_2, router_w_2, router_b_2, ln1_g_2, ln1_b_2, ln2_g_2, ln2_b_2,
        exp_w_gate_2, exp_w_up_2, exp_w_down_2, dil_w_in_2, dil_w_out_2, sb_w_in_2, sb_w_out_2,
        nsa_w_in_2, nsa_w_out_2, nsa_cmp_pos_k_2, nsa_cmp_w1_k_2, nsa_cmp_w2_k_2,
        nsa_cmp_pos_v_2, nsa_cmp_w1_v_2, nsa_cmp_w2_v_2, moba_w_in_2, moba_w_out_2,
    )


_drawn_inputs = setup_inputs


def setup_inputs(seed=0):
    import zlib

    import numpy as np

    out = dict(_drawn_inputs(seed))
    spreads = {}
    factors = {'q_norm': 8.0,
     'kv_norm': 2.879,
     'lru_b_a': 60.42,
     'lru_b_i': 30.833,
     'g_ple': 4.548,
     'rel_table_2': 6.982,
     'ln2_g_2': 8.77,
     'ln2_b_2': 11.67,
     'ssd_conv_b': 4.332}
    for name, (base, spread) in spreads.items():
        noise = np.random.default_rng([zlib.crc32(name.encode()), seed]).standard_normal(out[name].shape)
        drawn = base * np.exp(spread * noise) if base else spread * noise
        out[name] = jnp.asarray(drawn.astype(out[name].dtype))
    for name, factor in factors.items():
        out[name] = (out[name] * factor).astype(out[name].dtype)
    return out
```

```python
from contextlib import ExitStack

import numpy as np
import concourse.bass as bass
from concourse import mybir

F32 = mybir.dt.float32
BF16 = mybir.dt.bfloat16
F16 = mybir.dt.float16
I32 = mybir.dt.int32
ALU = mybir.AluOpType
ACT = mybir.ActivationFunctionType
AX = mybir.AxisListType

P = 128
S = 256
T = S // P
D = 1024
KD = D // P
MIX = 512
KM = MIX // P
EPS = 1e-6
LN_EPS = 1e-5
QL, KVL, ROPE, NOPE = 384, 256, 32, 64
MH = 8
QKD = NOPE + ROPE
MLA_SCALE = float(QKD) ** -0.5
XBC = 768
KX = XBC // P
CONV = 4
NE = 16
DE = 256
H2 = 16
HD = 64
ALPHA = 4.0 ** 0.25
SB_CLIP = 60.0
LN_TOP = 40.0
NEG = -1e30
W_POW, A_POW = 2.0 ** 8, 2.0 ** 3
SUM_POW = W_POW * A_POW
RING = 3
SLOT = 4096

DIL0, DOUT0, MOE0, SBI0, SBO0, MOE1 = 43, 61, 63, 87, 93, 95

C_Q, C_KV, C_POOL, C_Z, C_XBC, C_DT, C_LG, C_LX, C_GATE = 0, 384, 672, 1184, 1696, 2464, 2472, 2984, 3496

PARAM_ROWS = (("g_mix", 8), ("q_norm", 3), ("kv_norm", 2), ("pool_scale", 4), ("ssd_conv_w", 24),
              ("ssd_conv_b", 6), ("ssd_norm", 4), ("lru_conv_w", 16), ("lru_conv_b", 4),
              ("lru_b_a", 4), ("lru_b_i", 4), ("lru_lambda", 4), ("g_mlp", 8), ("g_ple", 8))
PROW = {}
_at = 0
for _name, _n in PARAM_ROWS:
    PROW[_name] = _at
    _at += _n
NPROW = _at


def constants():
    i = np.arange(P)
    f = np.float32
    eye = np.eye(P, dtype=f)
    flip = eye[::-1].copy()
    tri = (i[:, None] <= i[None, :]).astype(f)
    ones = np.ones((P, P), f)
    strict = (i[:, None] < i[None, :]).astype(f)
    low = (i[:, None] >= i[None, :]).astype(f)
    cmask = np.where(i[None, :] <= i[:, None], f(0), f(NEG)).astype(f)
    mats = np.concatenate([eye, flip, tri, ones, tri, strict, ones, strict, low, cmask], axis=1)
    t = np.arange(S)
    band = []
    for w in (2, 4, 8, 16):
        cnt = np.minimum(t + 1, w)
        m = ((t[:, None] <= t[None, :]) & (t[:, None] > t[None, :] - w)) / cnt[None, :] - np.eye(S)
        band.append(np.concatenate([m[:P, :], m[P:, P:]], axis=1).astype(f))
    band = np.concatenate(band, axis=1)
    dist = 255 - np.arange(384)
    n = np.maximum(dist, 0)
    logf = (np.log(np.maximum(n, 1).astype(f) / f(16)) / f(np.log(2048 / 16))).astype(f)
    large = np.minimum(16 + (logf * f(16)).astype(np.int32), 31)
    bucket = np.where(n < 16, n, large)
    onehot = (np.arange(32)[:, None] == bucket[None, :]).astype(f)
    d = 128 + i[:, None] - np.arange(S)[None, :]
    rel = np.stack([(d >= 0) & (d <= 128), (d >= 0) & (d % 4 == 0), (d >= 0) & (d % 16 == 0)], 1)
    relmask = np.where(rel, f(0), f(NEG)).astype(f)
    inv = (f(1) / (f(10000.0) ** (np.arange(0, ROPE, 2).astype(f) / f(ROPE)))).astype(f)
    rank0 = np.tile(np.array([3, 2, 1, 0], f), 8)
    rows = np.concatenate([inv, rank0]).reshape(1, 48).repeat(P, 0).astype(f)
    return {"c_mats": mats, "c_band": band.astype(f), "c_onehot": onehot,
            "c_relmask": relmask.reshape(P, 3 * S), "c_rows": rows}


def build(nc, a, out):
    ctx = ExitStack()
    with ctx:
        sems = {}

        def sig(name):
            if name not in sems:
                sems[name] = ctx.enter_context(nc.semaphore(name))
            return sems[name]

        def sb(name, shape, dt=F32):
            return ctx.enter_context(nc.sbuf_tensor(name, shape, dt))

        w_ring = sb("w_ring", [P, RING, SLOT])
        x_tok = sb("x_tok", [P, T, D])
        x_norm = sb("x_norm", [P, T, D])
        actT = sb("actT", [P, KD, S])
        ln_gb = sb("ln_gb", [P, 2, D])
        mats = sb("mats", [P, 10, P])
        crow = sb("crow", [P, 48])
        brow = sb("brow", [P, 24 + NE])
        pcol = sb("pcol", [P, NPROW])
        stats = sb("stats", [P, 64])
        lru_w = sb("lru_w", [P, 2, KM, P])
        pool_w = sb("pool_w", [P, KM, P])
        ARENA = 28350
        arena = sb("arena", [P, ARENA])
        ps = ctx.enter_context(nc.psum_tensor("ps", [P, 8, 512], F32))

        ident, flip = mats[:, 0, :], mats[:, 1, :]
        tri3 = mats[:, 2:5, :].rearrange("p a b -> p (a b)")
        tri, ones = mats[:, 2, :], mats[:, 3, :]
        strict3 = mats[:, 5:8, :].rearrange("p a b -> p (a b)")
        low, cmask = mats[:, 8, :], mats[:, 9, :]
        inv_freq, rank0 = crow[:, 0:16], crow[:, 16:48].rearrange("p (g e) -> p g e", e=4)

        at = [0]

        def take(n):
            at[0] += n
            assert at[0] <= ARENA, at[0]
            return arena[:, at[0] - n:at[0]]

        gates = take(T * 4 * D).rearrange("p (t n) -> p t n", t=T)
        hidT = gates.rearrange("p t n -> p (t n)").rearrange("p (k s) -> p k s", s=S)
        u_cqkv = take(T * 672)
        cq = u_cqkv[:, 0:T * QL].rearrange("p (t n) -> p t n", t=T)
        ckv = u_cqkv[:, T * QL:T * 672].rearrange("p (t n) -> p t n", t=T)
        y_ssd = u_cqkv[:, 0:T * MIX].rearrange("p (t n) -> p t n", t=T)
        u_up = take(T * MIX)
        up = u_up.rearrange("p (t n) -> p t n", t=T)
        lru_i = u_up.rearrange("p (c s) -> p c s", c=KM)
        z_silu = take(T * MIX).rearrange("p (t n) -> p t n", t=T)
        u_xb = take(KX * (S + 3))
        xbT = u_xb.rearrange("p (c s) -> p c s", c=KX)
        lru_a = u_xb[:, 0:KM * S].rearrange("p (c s) -> p c s", c=KM)
        u_xbS = take(KX * S)
        xbS = u_xbS.rearrange("p (c s) -> p c s", c=KX)
        xdt = u_xbS[:, 0:T * MIX].rearrange("p (t n) -> p t n", t=T)
        lru_g = take(KM * S).rearrange("p (c s) -> p c s", c=KM)
        u_lx = take(KM * (S + 3))
        lxT = u_lx.rearrange("p (c s) -> p c s", c=KM)
        lru_r = u_lx[:, 0:KM * S].rearrange("p (c s) -> p c s", c=KM)
        xcT = take(KM * S).rearrange("p (c s) -> p c s", c=KM)
        ycT = xcT
        u_cT = take(5 * S)
        cT = u_cT.rearrange("p (c s) -> p c s", c=5)
        cbm = u_cT[:, 0:2 * 384].rearrange("p (g s) -> p g s", g=2)
        lru_t = u_cT[:, 0:KM * S].rearrange("p (c s) -> p c s", c=KM)
        u_qk = take(2 * T * MH * QKD)
        q_tok = u_qk[:, 0:T * MH * QKD].rearrange("p (t h d) -> p t h d", t=T, h=MH)
        k_tok = u_qk[:, T * MH * QKD:].rearrange("p (t h d) -> p t h d", t=T, h=MH)
        dm = u_qk.rearrange("p (h s) -> p h s", h=MH)
        u_v = take(T * MIX)
        v_tok = u_v.rearrange("p (t h d) -> p t h d", t=T, h=MH)
        yaT = u_v.rearrange("p (c s) -> p c s", c=KM)
        probs = take(384)
        probsT = take(384)
        o_mla = take(T * MIX).rearrange("p (t n) -> p t n", t=T)
        u_dT = take(KM * S)
        dT = u_dT.rearrange("p (c s) -> p c s", c=KM)
        ybT = dT
        xs_tok = take(T * MIX).rearrange("p (t n) -> p t n", t=T)
        rope_cs = take(2 * T * 16).rearrange("p (a t f) -> p a t f", a=2, t=T)
        rope_tmp = take(4 * T * MH * 16).rearrange("p (a n) -> p a n", a=4)
        qT = x_norm[:, :, :].rearrange("p t n -> p (t n)").rearrange("p (h s) -> p h s", h=MH)
        kT = x_tok[:, :, :].rearrange("p t n -> p (t n)").rearrange("p (h s) -> p h s", h=MH)
        band = ln_gb[:, :, :].rearrange("p a n -> p (a n)")[:, 0:4 * 384].rearrange("p (g s) -> p g s", g=4)
        prow = probs
        dt_tok = stats[:, 0:16].rearrange("p (t h) -> p t h", t=T)
        a_tok = stats[:, 16:32].rearrange("p (t h) -> p t h", t=T)
        acs = stats[:, 32:48].rearrange("p (t h) -> p t h", t=T)
        ms, rstd, neghalf = stats[:, 48:52], stats[:, 52:56], stats[:, 56:60]
        mx = stats[:, 60:62]
        p_tok = o_mla.rearrange("p t n -> p (t n)")[:, 0:T * DE].rearrange("p (t n) -> p t n", t=T)
        pT = o_mla.rearrange("p t n -> p (t n)")[:, T * DE:2 * T * DE].rearrange("p (c s) -> p c s", c=2)
        pos_i = sb("pos_i", [P, T], I32)
        router_w = sb("router_w", [P, KD, NE])
        bn_part = sb("bn_part", [P, T, 2, 6])
        bn_mv = sb("bn_mv", [P, T, 2])
        mx4 = sb("mx4", [P, 4])
        pos_f = sb("pos_f", [P, T])
        zero16 = sb("zero16", [P, 640], BF16)
        den = sb("den", [P, 8])
        sp_v, sp_a, sp_e = (sb(f"softplus_{n}", [P, 20]) for n in "vae")
        decay8 = sb("decay8", [P, 4])
        a_head = sb("a_head", [P, MH])
        zc_mask = sb("zc_mask", [P, S])

        at[0] = 0
        u_q2 = take(3 * KD * S)
        q2T = u_q2.rearrange("p (g c s) -> p g c s", g=3, c=KD)
        k2T = take(3 * KD * S).rearrange("p (g c s) -> p g c s", g=3, c=KD)
        v2 = take(3 * T * D).rearrange("p (g t n) -> p g t n", g=3, t=T)
        bias_h = take(H2 * S).rearrange("p (h s) -> p h s", h=H2)
        relmask = take(3 * S).rearrange("p (g s) -> p g s", g=3)
        bm = take(2 * 3 * S).rearrange("p (b g s) -> p b g s", b=2, g=3)
        u_e = take(2 * 1152)
        e_dil = u_e.rearrange("p (b n) -> p b n", b=2)
        eT_dil = take(1152)
        rel_row = u_e[0:H2, 1152:1536]
        rel_tab = eT_dil[0:32, 0:H2]
        rel_spread = v2.rearrange("p g t n -> p (g t n)")[:, 0:H2 * S].rearrange("p (h s) -> p h s", h=H2)
        onehot = eT_dil[0:32, 16:400]
        sb_sets = (arena[:, 2048:2048 + 4 * 768], arena[:, 8192:8192 + 4 * 768])
        sb_zt, sb_e, sb_l, sb_h = ([u[:, 768 * i:768 * i + 768].rearrange("p (h s) -> p h s", h=2) for u in sb_sets]
                                   for i in range(4))
        at[0] = 0
        half = lambda v: v.bitcast(F16)
        aT_hi, aT_lo = (half(take(KD * S // 2)).rearrange("p (k s) -> p k s", k=KD) for _ in range(2))
        e_silu = take(2 * T * DE).rearrange("p (b t n) -> p b t n", b=2, t=T)
        h_tok = take(2 * T * DE).rearrange("p (b t n) -> p b t n", b=2, t=T)
        hT_hi, hT_lo = (half(take(S * DE // P)).rearrange("p (b n) -> p b n", b=2) for _ in range(2))
        score = take(T * NE)
        r_v, r_rank, r_cmp, r_sel, r_gate = (take(T * NE) for _ in range(5))
        r_gs = take(8)
        r_gr = take(8)
        r_best = take(8)
        r_den = take(4)
        at[0] = 14400
        w_hi, w_lo = (half(take(3 * SLOT // 2)).rearrange("p (b n) -> p b n", b=3) for _ in range(2))
        rel_dram = nc.dram_tensor("rel_rows_dram", [H2, 384], F32, kind="Internal").ap()
        block = ctx.enter_context(nc.Block())

        EVAC, _n = [], {"A": 0, "D": 0}
        for e in "ADAADDAD" + "A" * 8:
            _n[e] += 1
            EVAC.append((sig("out_by_act" if e == "A" else "out_by_dve"), _n[e]))

        w_in = a["w_in"].rearrange("o (k p) n -> (o p) k n", p=P)

        def landed(eng, n):
            eng.wait_ge(sig(f"w_landed{n % RING}"), 32 * (n // RING + 1))

        def moe_index(n):
            if MOE0 <= n < SBI0:
                return n - MOE0
            return n - MOE1 + 3 * NE // 2 if n >= MOE1 else None

        def bcast(ap, n, offset=0):
            return bass.AP(tensor=ap.tensor, offset=offset, ap=[[0, P], [1, n]])

        @block.sync
        def _(sp):
            def slot_free(n):
                m = n - RING
                if m >= 0:
                    q = moe_index(m)
                    if q is None:
                        sp.wait_ge(sig("w_used"), m + 1)
                    else:
                        sp.wait_ge(sig("w_lo"), q + 1)

            def slot(n, pairs):
                slot_free(n)
                for o, k, c, src in pairs:
                    sp.dma_start(w_ring[:, n % RING, o:o + k * c].rearrange("p (k n) -> p k n", k=k), src)\
                        .then_inc(sig(f"w_landed{n % RING}"), 16)

            def halves(n, w, c0, c):
                h = KD // 2
                slot(n, [(0, h, c, w[:, 0:h, c0:c0 + c]), (h * c, h, c, w[:, h:KD, c0:c0 + c])])

            def rows4(n, w):
                slot(n, [(0, 2, D, w[:, 0:2, :]), (2 * D, 2, D, w[:, 2:4, :])])

            sp.dma_start(x_norm[:, :, :], a["x"].rearrange("o (t p) d -> (o p) t d", p=P)).then_inc(sig("ld_x"), 16)
            sp.dma_start(mats[:, :, :].rearrange("p a b -> p (a b)"), a["c_mats"]).then_inc(sig("ld_mats"), 16)
            halves(0, w_in, C_Q, 384)
            for name, n in PARAM_ROWS:
                v = a[name]
                flat = bass.AP(tensor=v.tensor, offset=0, ap=[[P, n], [1, P]])
                sp.dma_start(prow[PROW[name]:PROW[name] + n, 0:P], flat).then_inc(sig("ld_params"), 16)
            sp.dma_start(crow[:, :], a["c_rows"]).then_inc(sig("ld_rows"), 16)
            for i, (name, n) in enumerate((("ssd_dt_bias", 8), ("ssd_a_log", 8), ("ssd_d", 8), ("router_b_2", NE))):
                sp.dma_start(brow[:, 8 * i:8 * i + n], bcast(a[name], n)).then_inc(sig("ld_rows"), 16)
            sp.dma_start(pos_i[:, :], a["positions"]).then_inc(sig("ld_rows"), 16)
            halves(1, w_in, C_KV, 288)
            halves(2, w_in, C_POOL, 512)
            sp.dma_start(band, a["c_band"].rearrange("p (g s) -> p g s", g=4)).then_inc(sig("ld_pool"), 16)
            sp.dma_start(pool_w[:, :, :], a["w_pool"].rearrange("o g c d -> (o c) g d")).then_inc(sig("ld_pool"), 16)
            sp.wait_ge(sig("lru_zeroed"), 1)
            for i, name in enumerate(("lru_w_a", "lru_w_i")):
                w = a[name].rearrange("o (c b) i j -> (o b) i c j", b=2)
                for b in range(2):
                    sp.dma_start(lru_w[64 * b:64 * b + 64, i, :, 64 * b:64 * b + 64], w[b])\
                        .then_inc(sig("ld_lru"), 16)
            halves(3, w_in, C_Z, 512)
            halves(4, w_in, C_XBC, 384)
            w = a["w_uq"].rearrange("o (k p) n -> (o p) k n", p=P)
            slot(5, [(0, 2, 768, w[:, 0:2, :]), (1536, 1, 768, w[:, 2:3, :])])
            halves(6, w_in, C_XBC + 384, 392)
            w = a["w_ukv"].rearrange("o (k p) n -> (o p) k n", p=P)
            slot(7, [(0, 1, D, w[:, 0:1, :]), (D, 1, D, w[:, 1:2, :])])
            halves(8, w_in, C_LG, 512)
            halves(9, w_in, C_LX, 512)
            for i in range(8):
                halves(10 + i, w_in, C_GATE + 512 * i, 512)
            for i, b in enumerate((1, 0, 3, 2)):
                rows4(18 + i, a["w_branch"][0, b].rearrange("(k p) n -> p k n", p=P))
            sp.wait_ge(sig("mla_scores"), MH)
            sp.dma_start(x_tok[:, :, :], a["x"].rearrange("o (t p) d -> (o p) t d", p=P)).then_inc(sig("ld_x"), 16)
            sp.wait_ge(sig("pool_d"), 1)
            sp.dma_start(ln_gb[:, 0, :], bcast(a["g_final"], D)).then_inc(sig("ld_gb"), 16)
            w = a["w_out"].rearrange("o (k p) n -> (o p) k n", p=P)
            halves(22, w, 0, 512)
            halves(23, w, 512, 512)
            sp.wait_ge(sig("mla_oT_pe"), KM)
            sp.dma_start(p_tok, a["p"].rearrange("l o (t p) d -> (l o p) t d", p=P)).then_inc(sig("ld_p"), 16)
            w = a["w_ff1"].rearrange("o (k p) n -> (o p) k n", p=P)
            for i in range(8):
                halves(24 + i, w, 512 * i, 512)
            sp.wait_ge(sig("branch"), 4)
            sp.dma_start(relmask, a["c_relmask"].rearrange("p (g s) -> p g s", g=3)).then_inc(sig("ld_rel"), 16)
            sp.dma_start(rel_tab, a["rel_table_2"]).then_inc(sig("ld_rel"), 16)
            sp.dma_start(onehot, a["c_onehot"]).then_inc(sig("ld_rel"), 16)
            sp.dma_start(router_w[:, :, :], a["router_w_2"].rearrange("(k p) e -> p k e", p=P)).then_inc(sig("ld_router"), 16)
            for i in range(8):
                rows4(32 + i, a["w_ff2"][0, 512 * i:512 * i + 512, :].rearrange("(k p) n -> p k n", p=P))
            sp.wait_ge(sig("rel_row"), 1)
            sp.dma_start(rel_dram, rel_row).then_inc(sig("st_rel"), 16)
            sp.wait_ge(sig("st_rel"), 16)
            spread = bass.AP(tensor=rel_dram.tensor, offset=0, ap=[[1, P], [384, H2], [1, S]])
            sp.dma_start(rel_spread, spread).then_inc(sig("ld_spread"), 16)

            w = a["w_ple"].rearrange("o (k p) n -> (o p) k n", p=P)
            slot(40, [(0, 1, D, w[:, 0:1, :]), (D, 1, D, w[:, 1:2, :])])
            w = a["w_ple_gate"].rearrange("o (k p) n -> (o p) k n", p=P)
            halves(41, w, 0, 512)
            halves(42, w, 512, 512)
            def slot_g(n, pairs):
                for dst, src in pairs:
                    sp.dma_start(dst, src).then_inc(sig(f"w_landed{n % RING}"), 16)

            w = a["dil_w_in_2"].rearrange("o (k p) n -> (o p) k n", p=P)
            with sp.Fori(0, 3) as g:
                for s in range(6):
                    dst = w_ring[:, (DIL0 + s) % RING, :].rearrange("p (k n) -> p k n", k=KD)
                    sp.wait_ge(sig("w_used"), DIL0 + s - RING + 1 + g * 6)
                    slot_g(DIL0 + s, [(dst[:, kk:kk + 4, :], w[:, kk:kk + 4, bass.ds(g * 3 * D + 512 * s, 512)])
                                      for kk in (0, 4)])

            def gb(m):
                layer, name = m // 2, ("ln1", "ln2")[m % 2]
                sp.wait_ge(sig("gb_free"), m + 1)
                sp.dma_start(ln_gb[:, 0, :], bcast(a[name + "_g_2"], D, layer * D)).then_inc(sig("ld_gb"), 16)
                sp.dma_start(ln_gb[:, 1, :], bcast(a[name + "_b_2"], D, layer * D)).then_inc(sig("ld_gb"), 16)

            def experts(layer, n0):
                wg = a["exp_w_gate_2"][layer].rearrange("e (k p) n -> p e k n", p=P)
                wu = a["exp_w_up_2"][layer].rearrange("e (k p) n -> p e k n", p=P)
                wd = a["exp_w_down_2"][layer].rearrange("e (k p) n -> p e k n", p=P)

                def pair(j):
                    for b in range(3):
                        n = n0 + b
                        if isinstance(j, int):
                            slot_free(n)
                        else:
                            sp.wait_ge(sig("w_lo"), moe_index(n0) + b - 2 + j * 3)
                        if b < 2:
                            dst = w_ring[:, n % RING, :].rearrange("p (o k n) -> p o k n", o=1, k=KD)
                            slot_g(n, [(dst[:, :, :, 0:DE], wg[:, bass.ds(2 * j + b, 1), :, :]),
                                       (dst[:, :, :, DE:2 * DE], wu[:, bass.ds(2 * j + b, 1), :, :])])
                        else:
                            dst = w_ring[:, n % RING, :].rearrange("p (o k n) -> p o k n", o=2, k=2)
                            slot_g(n, [(dst[:, i:i + 1, :, :], wd[:, bass.ds(2 * j + i, 1), :, :]) for i in range(2)])

                pair(0)
                with sp.Fori(1, NE // 2) as j:
                    pair(j)

            gb(0)
            w = a["dil_w_out_2"].rearrange("o (k p) n -> (o p) k n", p=P)
            halves(DOUT0, w, 0, 512)
            halves(DOUT0 + 1, w, 512, 512)
            experts(0, MOE0)
            gb(1)
            w = a["sb_w_in_2"].rearrange("o (k p) n -> (o p) k n", p=P)
            for s in range(6):
                halves(SBI0 + s, w, 512 * s, 512)
            gb(2)
            w = a["sb_w_out_2"].rearrange("o (k p) n -> (o p) k n", p=P)
            halves(SBO0, w, 0, 512)
            halves(SBO0 + 1, w, 512, 512)
            experts(1, MOE1)
            gb(3)
            for t in range(T):
                sp.wait_ge(sig("out_ready"), t + 1)
                sp.dma_start(out[0, t * P:(t + 1) * P, :], x_tok[:, t, :]).then_inc(sig("stored"), 16)
            sp.wait_ge(sig("stored"), 16 * T)

        @block.gpsimd
        def _(pool):
            pool.memset(neghalf, -0.5)
            pool.memset(zero16[:, :], 0.0)
            pool.memset(lru_w[:, :, :, :], 0.0)
            pool.drain()
            pool.memset(xbT[:, :, 0:CONV - 1], 0.0)
            pool.memset(lxT[:, :, 0:CONV - 1], 0.0).then_inc(sig("lru_zeroed"), 1)

            def rsqrt(i, n):
                pool.wait_ge(sig("ms_ready"), i + 1)
                pool.tensor_tensor(rstd[:, 0:n], ms[:, 0:n], neghalf[:, 0:n], ALU.pow).then_inc(sig("rstd_ready"), 1)

            rsqrt(0, 2)
            rsqrt(1, 4)
            for i in range(2, 6):
                rsqrt(i, 2)
            pool.wait_ge(sig("bias_h"), 2)
            pool.wait_ge(sig("ld_rel"), 16 * 3)
            for h in range(H2):
                if h >= 2:
                    pool.wait_ge(sig("dil_max"), h - 1)
                pool.tensor_tensor(bm[:, h % 2, :, :], relmask, bias_h[:, h:h + 1, :].broadcast_to([P, 3, S]), ALU.add)\
                    .then_inc(sig("bm"), 1)
            for i in range(6, 10):
                rsqrt(i, 2)

        def pcols(name, i):
            c = PROW[name] + i
            return pcol[:, c:c + 1]

        @block.tensor
        def _(pe):
            def w_slot(n, k):
                return w_ring[:, n % RING, :].rearrange("p (k n) -> p k n", k=k) if k else w_ring[:, n % RING, :]

            def transposes(i, src, chunks, sem_name, first_bank=4):
                for k in range(chunks):
                    for t in range(T):
                        o = (k % 2) * 256 + t * P
                        ins = pe.transpose(ps[:, first_bank + k // 2, o:o + P], src[:, t, k * P:(k + 1) * P], ident)
                    ins.then_inc(sig(sem_name), 1)

            def act_transposes(i, src=x_norm):
                pe.wait_ge(sig("xn_ready"), i + 1)
                if i:
                    pe.wait_ge(sig("xp_act"), 4 * i)
                    pe.wait_ge(sig("xp_dve"), 4 * i)
                transposes(i, src, KD, "xp_pe")

            def act_ready(i):
                pe.wait_ge(sig("xp_act"), 4 * i + 4)
                pe.wait_ge(sig("xp_dve"), 4 * i + 4)

            def gemm_tok(n, bank, cols):
                landed(pe, n)
                w = w_ring[:, n % RING, 0:KD * cols].rearrange("p (k n) -> p k n", k=KD)
                for t in range(T):
                    for k in range(KD):
                        ins = pe.matmul(ps[:, bank + t, 0:cols], actT[:, k, t * P:(t + 1) * P], w[:, k, :],
                                        start=(k == 0), stop=(k == KD - 1))
                return ins

            def gemm_T(n, bank, cols, chunks):
                landed(pe, n)
                w = w_ring[:, n % RING, 0:KD * cols].rearrange("p (k n) -> p k n", k=KD)
                for c in range(chunks):
                    o = (c % 2) * S
                    for k in range(KD):
                        ins = pe.matmul(ps[:, bank + c // 2, o:o + S], w[:, k, c * P:(c + 1) * P], actT[:, k, :],
                                        start=(k == 0), stop=(k == KD - 1))
                return ins

            def evacuated(g):
                if g >= 2:
                    pe.wait_ge(*EVAC[g - 2])

            pe.wait_ge(sig("ld_mats"), 16)
            pe.wait_ge(sig("ld_params"), 16 * len(PARAM_ROWS))
            pe.transpose(ps[:, 0, 0:NPROW], prow[0:NPROW, 0:P], ident[0:NPROW, 0:NPROW]).then_inc(sig("params_T"), 1)
            act_transposes(0)
            act_ready(0)
            pe.wait_ge(sig("pcol"), 1)
            g = 0
            for n, cols in ((0, 384), (1, 288), (2, 512), (3, 512)):
                evacuated(g)
                gemm_tok(n, (g % 2) * 2, cols).then_inc(sig("w_used"), 1)
                g += 1
            pe.wait_ge(sig("ld_pool"), 32)
            pe.wait_ge(*EVAC[2])
            for c in range(KM):
                o = (c % 2) * S
                pe.matmul(ps[:, 4 + c // 2, o:o + S], up[:, 0, c * P:(c + 1) * P], band[:, c, 0:S],
                          start=True, stop=False, skip_group_check=True)
                ins = pe.matmul(ps[:, 4 + c // 2, o + P:o + S], up[:, 1, c * P:(c + 1) * P], band[:, c, S:384],
                                start=False, stop=True, skip_group_check=True)
            ins.then_inc(sig("pool_d"), 1)
            evacuated(g)
            gemm_T(4, (g % 2) * 2, 384, 3).then_inc(sig("w_used"), 1)
            g += 1
            pe.wait_ge(sig("dT"), 1)
            pe.wait_ge(sig("mla_normed"), 1)
            for k in range(5):
                src, kk = (cq, k) if k < 3 else (ckv, k - 3)
                for t in range(T):
                    o = (k % 2) * S + t * P
                    ins = pe.transpose(ps[:, 4 + k // 2, o:o + P], src[:, t, kk * P:(kk + 1) * P], ident)
            ins.then_inc(sig("cT_pe"), 1)
            landed(pe, 5)
            pe.wait_ge(sig("cT"), 1)
            w = w_ring[:, 5 % RING, 0:3 * 768].rearrange("p (k n) -> p k n", k=3)
            for t in range(T):
                for h in range(2):
                    for k in range(3):
                        ins = pe.matmul(ps[:, 4 + 2 * t + h, 0:384], cT[:, k, t * P:(t + 1) * P],
                                        w[:, k, h * 384:(h + 1) * 384], start=(k == 0), stop=(k == 2))
            ins.then_inc(sig("w_used"), 1)
            evacuated(g)
            gemm_T(6, (g % 2) * 2, 392, 3)
            w = w_ring[:, 6 % RING, 0:KD * 392].rearrange("p (k n) -> p k n", k=KD)
            for t in range(T):
                for k in range(KD):
                    ins = pe.matmul(ps[:, (g % 2) * 2 + 1, S + 8 * t:S + 8 * t + 8], actT[:, k, t * P:(t + 1) * P],
                                    w[:, k, 384:392], start=(k == 0), stop=(k == KD - 1))
            ins.then_inc(sig("w_used"), 1)
            g += 1
            landed(pe, 7)
            pe.wait_ge(sig("q_out"), 1)
            w = w_ring[:, 7 % RING, 0:2 * D].rearrange("p (k n) -> p k n", k=2)
            for t in range(T):
                for h in range(2):
                    for k in range(2):
                        ins = pe.matmul(ps[:, 4 + 2 * t + h, :], cT[:, 3 + k, t * P:(t + 1) * P],
                                        w[:, k, h * 512:(h + 1) * 512], start=(k == 0), stop=(k == 1))
            ins.then_inc(sig("w_used"), 1)
            evacuated(g)
            gemm_T(8, (g % 2) * 2, 512, 4).then_inc(sig("w_used"), 1)
            g += 1

            def head_turns(src, done):
                for h in range(MH):
                    for t in range(T):
                        o = (h % 2) * S + t * P
                        ins = pe.transpose(ps[0:QKD, 4 + h // 2, o:o + P], src[:, t, h, :], ident)
                ins.then_inc(sig(done), 1)

            pe.wait_ge(sig("q_roped"), 1)
            pe.wait_ge(sig("kv_out"), 1)
            head_turns(q_tok, "qT_pe")
            evacuated(g)
            gemm_T(9, (g % 2) * 2, 512, 4).then_inc(sig("w_used"), 1)
            g += 1
            pe.wait_ge(sig("k_roped"), 1)
            pe.wait_ge(sig("qT"), 1)
            head_turns(k_tok, "kT_pe")

            def mla_score(h):
                if h == 0:
                    pe.wait_ge(sig("kT"), 1)
                else:
                    pe.wait_ge(sig("mla_max"), h)
                pe.matmul(ps[:, 4, 0:P], qT[0:QKD, h, 0:P], kT[0:QKD, h, 0:P], start=True, stop=True)
                pe.matmul(ps[:, 4, P:384], qT[0:QKD, h, P:S], kT[0:QKD, h, :], start=True, stop=True)\
                    .then_inc(sig("mla_scores"), 1)

            def mla_out(h):
                pe.wait_ge(sig("mla_exp"), h + 1)
                if h == 0:
                    pe.wait_ge(sig("kT"), 1)
                else:
                    pe.wait_ge(sig("mla_o"), h)
                for j in range(3):
                    ins = pe.transpose(ps[:, 5, j * P:(j + 1) * P], probs[:, j * P:(j + 1) * P], ident)
                ins.then_inc(sig("mla_pT_pe"), 1)
                pe.wait_ge(sig("mla_pT"), h + 1)
                pe.matmul(ps[:, 5, 384:448], probsT[:, 0:P], v_tok[:, 0, h, :], start=True, stop=True)
                pe.matmul(ps[:, 5, 448:512], probsT[:, P:2 * P], v_tok[:, 0, h, :], start=True, stop=False)
                pe.matmul(ps[:, 5, 448:512], probsT[:, 2 * P:3 * P], v_tok[:, 1, h, :], start=False, stop=True)\
                    .then_inc(sig("mla_pv"), 1)

            def ssd_cb():
                pe.wait_ge(sig("xbS"), 1)
                pe.wait_ge(sig("kT"), 1)
                for gr in range(2):
                    r = slice(64 * gr, 64 * gr + 64)
                    pe.matmul(ps[:, 6 + gr, 0:S], xbS[r, 4, 0:P], xbS[r, 5, :], start=True, stop=True)
                    ins = pe.matmul(ps[:, 6 + gr, S:384], xbS[r, 4, P:S], xbS[r, 5, P:S], start=True, stop=True)
                ins.then_inc(sig("cb_pe"), 1)

            def ssd_xs():
                pe.wait_ge(sig("cbm"), 1)
                for t in range(T):
                    for c in range(KM):
                        ins = pe.transpose(ps[:, 6 + t, c * P:(c + 1) * P], xbS[:, c, t * P:(t + 1) * P], ident)
                ins.then_inc(sig("xs_pe"), 1)

            def ssd_cumsum(half):
                if half == 0:
                    pe.wait_ge(sig("acs"), 1)
                else:
                    pe.wait_ge(sig("dm"), 1)
                for j in range(4):
                    h = 4 * half + j
                    o = (j % 2) * S
                    b = 6 + j // 2
                    pe.matmul(ps[:, b, o:o + S], a_tok[:, 0, h:h + 1].broadcast_to([P, P]), tri3[:, 0:S],
                              start=True, stop=False, skip_group_check=True)
                    ins = pe.matmul(ps[:, b, o + P:o + S], a_tok[:, 1, h:h + 1].broadcast_to([P, P]), tri,
                                    start=False, stop=True, skip_group_check=True)
                ins.then_inc(sig("cum_pe"), 1)

            def ssd_cumcol():
                pe.wait_ge(sig("a_tok"), 1)
                pe.wait_ge(sig("xs_tok"), 1)
                pe.matmul(ps[:, 6, 0:8], tri, a_tok[:, 0, :], start=True, stop=True)
                pe.matmul(ps[:, 6, 8:16], ones, a_tok[:, 0, :], start=True, stop=False)
                pe.matmul(ps[:, 6, 8:16], tri, a_tok[:, 1, :], start=False, stop=True).then_inc(sig("acs_pe"), 1)

            def lru_gate(i):
                pe.wait_ge(sig("ld_lru"), 64)
                pe.wait_ge(sig("xcT"), 1)
                if i == 0:
                    pe.wait_ge(sig("dm"), 2)
                else:
                    pe.wait_ge(sig("lru_r"), 1)
                for c in range(KM):
                    o = (c % 2) * S
                    ins = pe.matmul(ps[:, 6 + c // 2, o:o + S], lru_w[:, i, c, :], xcT[:, c, :], start=True, stop=True)
                ins.then_inc(sig("lru_pe"), 1)

            def ssd_y():
                pe.wait_ge(sig("lru_i"), 1)
                pe.wait_ge(sig("dm_cb"), 1)
                pe.wait_ge(sig("xdt"), 1)
                for h in range(MH):
                    c = slice(64 * h, 64 * h + 64)
                    pe.matmul(ps[:, 6, c], dm[:, h, 0:P], xdt[:, 0, c], start=True, stop=True)
                    pe.matmul(ps[:, 7, c], dm[:, h, P:S], xdt[:, 0, c], start=True, stop=False)
                    ins = pe.matmul(ps[:, 7, c], dm[:, h, S:384], xdt[:, 1, c], start=False, stop=True)
                ins.then_inc(sig("ssd_y_pe"), 1)

            def pool_y():
                pe.wait_ge(sig("ssd_y"), 1)
                for c in range(KM):
                    o = (c % 2) * S
                    ins = pe.matmul(ps[:, 6 + c // 2, o:o + S], pool_w[:, c, :], dT[:, c, :], start=True, stop=True)
                ins.then_inc(sig("pool_y"), 1)

            def ssd_turn():
                pe.wait_ge(sig("ybT"), 1)
                pe.wait_ge(sig("ssd_normed"), 1)
                transposes(0, y_ssd, KM, "ycT_pe", 6)

            extra = {0: [ssd_cb], 1: [ssd_xs, ssd_cumcol], 2: [lambda: ssd_cumsum(0)], 3: [lambda: ssd_cumsum(1)],
                     4: [lambda: lru_gate(0)], 5: [lambda: lru_gate(1), ssd_y], 6: [pool_y], 7: [ssd_turn]}
            for i in range(8):
                evacuated(g)
                gemm_tok(10 + i, (g % 2) * 2, 512).then_inc(sig("w_used"), 1)
                g += 1
                mla_score(i)
                if i:
                    mla_out(i - 1)
                for f in extra[i]:
                    f()
            mla_out(MH - 1)
            pe.wait_ge(sig("mla_o"), MH)
            transposes(0, o_mla, KM, "mla_oT_pe", 4)
            for i, (b, yT) in enumerate(((1, ybT), (0, yaT), (3, lru_g), (2, ycT))):
                n = 18 + i
                landed(pe, n)
                pe.wait_ge(sig(("ybT", "yaT", "ydT", "ycT")[i]), 1)
                if i == 0:
                    pe.wait_ge(*EVAC[15])
                    pe.wait_ge(*EVAC[14])
                elif i == 1:
                    pe.wait_ge(sig("ycT"), 1)
                else:
                    pe.wait_ge(sig("branch"), i - 1)
                w = w_ring[:, n % RING, :].rearrange("p (k n) -> p k n", k=KM)
                for t in range(T):
                    for h in range(2):
                        for k in range(KM):
                            ins = pe.matmul(ps[:, 4 * (i % 2) + 2 * t + h, :], yT[:, k, t * P:(t + 1) * P],
                                            w[:, k, h * 512:(h + 1) * 512], start=(k == 0), stop=(k == KM - 1))
                ins.then_inc(sig("w_used"), 1)
            pe.wait_ge(sig("branch"), 4)
            act_transposes(1)
            act_ready(1)
            gemm_tok(22, 0, 512).then_inc(sig("w_used"), 1)
            gemm_tok(23, 2, 512).then_inc(sig("w_used"), 1)
            act_transposes(2)
            act_ready(2)
            for i in range(8):
                if i >= 2:
                    pe.wait_ge(sig("ff1_relu"), i - 1)
                elif i == 0:
                    pe.wait_ge(sig("x_res"), 1)
                gemm_T(24 + i, (i % 2) * 2, 512, 4).then_inc(sig("w_used"), 1)
            pe.wait_ge(sig("ld_rel"), 48)
            pe.matmul(ps[0:H2, 5, 0:384], rel_tab, onehot, start=True, stop=True).then_inc(sig("rel_pe"), 1)
            pe.wait_ge(sig("ld_p"), 16)
            transposes(0, p_tok, 2, "pT_pe", 4)
            pe.wait_ge(sig("ff1_square"), 8)
            for i in range(8):
                landed(pe, 32 + i)
                w = w_ring[:, (32 + i) % RING, :].rearrange("p (k n) -> p k n", k=KM)
                for t in range(T):
                    for h in range(2):
                        for k in range(KM):
                            kk = KM * i + k
                            ins = pe.matmul(ps[:, 2 * t + h, :], hidT[:, kk, t * P:(t + 1) * P],
                                            w[:, k, h * 512:(h + 1) * 512], start=(kk == 0), stop=(kk == 31),
                                            skip_group_check=True)
                ins.then_inc(sig("w_used"), 1)
            pe.wait_ge(sig("ld_spread"), 16)
            pe.wait_ge(sig("pT"), 1)
            pe.wait_ge(sig("rel_row"), 1)
            for i in range(8):
                if i == 4:
                    pe.wait_ge(sig("bias_h"), 1)
                ins = pe.matmul(ps[:, 4 + i % 4, :], flip, rel_spread[:, 2 * i:2 * i + 2, :], start=True, stop=True)
                if i % 4 == 3:
                    ins.then_inc(sig("flip_pe"), 1)
            pe.wait_ge(sig("x_res"), 2)
            pe.wait_ge(sig("pT"), 1)
            landed(pe, 40)
            w = w_ring[:, 40 % RING, 0:2 * D].rearrange("p (k n) -> p k n", k=2)
            for t in range(T):
                for h in range(2):
                    for k in range(2):
                        ins = pe.matmul(ps[:, 2 * t + h, :], pT[:, k, t * P:(t + 1) * P],
                                        w[:, k, h * 512:(h + 1) * 512], start=(k == 0), stop=(k == 1))
            ins.then_inc(sig("w_used"), 1)
            pe.wait_ge(sig("bias_h"), 2)
            act_transposes(3)
            act_ready(3)
            for i in range(2):
                gemm_tok(41 + i, 4 + 2 * i, 512).then_inc(sig("w_used"), 1)

            def qkv(n0, g, base):
                for s in range(6):
                    n = n0 + s
                    pe.wait_ge(sig(f"w_landed{n % RING}"), 32 * (n // RING + 1) + g * 64)
                    if s >= 2:
                        pe.wait_ge(sig("qkv_act" if s % 2 == 0 else "qkv_dve"), base + s // 2 + g * 3)
                    w = w_ring[:, n % RING, :].rearrange("p (k n) -> p k n", k=KD)
                    for c in range(4 if s < 4 else T):
                        for k in range(KD):
                            if s < 4:
                                o = (c % 2) * S
                                ins = pe.matmul(ps[:, (s % 2) * 2 + c // 2, o:o + S], w[:, k, c * P:(c + 1) * P],
                                                actT[:, k, :], start=(k == 0), stop=(k == KD - 1))
                            else:
                                ins = pe.matmul(ps[:, (s % 2) * 2 + c, :], actT[:, k, c * P:(c + 1) * P], w[:, k, :],
                                                start=(k == 0), stop=(k == KD - 1))
                    ins.then_inc(sig("w_used"), 1)
                pe.wait_ge(sig("qkv_act"), base + 3 + g * 3)
                pe.wait_ge(sig("qkv_dve"), base + 3 + g * 3)

            act_transposes(4, x_tok)
            act_ready(4)
            with pe.Fori(0, 3) as g:
                qkv(DIL0, g, 0)

            def dil_scores(h):
                if h:
                    pe.wait_ge(sig("dil_max"), h)
                c, r = h // 2, slice(64 * (h % 2), 64 * (h % 2) + 64)
                for g in range(3):
                    pe.matmul(ps[:, 0, g * P:(g + 1) * P], q2T[r, g, c, 0:P], k2T[r, g, c, 0:P], start=True, stop=True)
                for g in range(3):
                    o = (g % 2) * S
                    ins = pe.matmul(ps[:, 1 + g // 2, o:o + S], q2T[r, g, c, P:S], k2T[r, g, c, :], start=True, stop=True)
                ins.then_inc(sig("dil_scores"), 1)

            def dil_out(h):
                pe.wait_ge(sig("dil_exp"), h + 1)
                if h == 0:
                    pe.wait_ge(sig("xp_act"), 20)
                for j in range(9):
                    b, o = (3, j * P) if j < 3 else (4 + (j - 3) // 4, ((j - 3) % 4) * P)
                    ins = pe.transpose(ps[:, b, o:o + P], e_dil[:, h % 2, j * P:(j + 1) * P], ident)
                ins.then_inc(sig("dil_pT_pe"), 1)
                pe.wait_ge(sig("dil_pT_act"), h + 1)
                pe.wait_ge(sig("dil_pT_dve"), h + 1)
                if h >= 2:
                    pe.wait_ge(sig("dil_o"), h - 1)
                cols = slice(64 * h, 64 * h + 64)
                for g in range(3):
                    pe.matmul(ps[:, 6 + h % 2, 0:64], eT_dil[:, g * P:(g + 1) * P], v2[:, g, 0, cols],
                              start=(g == 0), stop=(g == 2))
                for g in range(3):
                    for kt in range(2):
                        o = 384 + g * S + kt * P
                        ins = pe.matmul(ps[:, 6 + h % 2, 64:128], eT_dil[:, o:o + P], v2[:, g, kt, cols],
                                        start=(g + kt == 0), stop=(g + kt == 3))
                ins.then_inc(sig("dil_pv"), 1)

            dil_scores(0)
            for h in range(H2):
                if h + 1 < H2:
                    dil_scores(h + 1)
                dil_out(h)
            act_transposes(5)
            act_ready(5)
            gemm_tok(DOUT0, 0, 512).then_inc(sig("w_used"), 1)
            gemm_tok(DOUT0 + 1, 2, 512).then_inc(sig("w_used"), 1)

            def experts(layer, n0, turn):
                q0 = moe_index(n0)
                act_transposes(turn, x_tok)
                act_ready(turn)
                pe.wait_ge(sig("ld_router"), 16)
                for t in range(T):
                    for k in range(KD):
                        ins = pe.matmul(ps[:, 0, t * NE:(t + 1) * NE], actT[:, k, t * P:(t + 1) * P], router_w[:, k, :],
                                        start=(k == 0), stop=(k == KD - 1))
                ins.then_inc(sig("logits"), 1)

                def gate_up(b, t):
                    w_h, w_l = (v[:, (n0 + b) % 3, :].rearrange("p (k n) -> p k n", k=KD) for v in (w_hi, w_lo))
                    for k in range(KD):
                        c = slice(t * P, (t + 1) * P)
                        for i, (u, v) in enumerate(((aT_hi, w_h), (aT_hi, w_l), (aT_lo, w_h))):
                            ins = pe.matmul(ps[:, 4 + 2 * b + t, :], u[:, k, c], v[:, k, :],
                                            start=(k + i == 0), stop=(k == KD - 1 and i == 2))
                    return ins

                def turn_h(b, j):
                    pe.wait_ge(sig("moe_h"), NE * layer + 1 + b + j * 2)
                    for f in range(2):
                        for t in range(T):
                            o = f * S + t * P
                            ins = pe.transpose(ps[:, 4 + 2 * b, o:o + P], h_tok[:, b, t, f * P:(f + 1) * P], ident)
                    ins.then_inc(sig("moe_hT_pe"), 1)

                def down(b, j):
                    pe.wait_ge(sig("moe_hT"), NE * layer + 1 + b + j * 2)
                    o = b * 2048
                    w_h, w_l = (v[:, (n0 + 2) % 3, o:o + 2048].rearrange("p (k n) -> p k n", k=2) for v in (w_hi, w_lo))
                    for t in range(T):
                        for f in range(2):
                            c = slice(f * S + t * P, f * S + (t + 1) * P)
                            for u, v in ((hT_hi, w_h), (hT_hi, w_l), (hT_lo, w_h)):
                                for h in range(2):
                                    ins = pe.matmul(ps[:, 2 * t + h, :], u[:, b, c], v[:, f, h * 512:(h + 1) * 512],
                                                    start=False, stop=False, skip_group_check=True)
                    return ins

                def pair(j, last):
                    gate_up(0, 1).then_inc(sig("w_used"), 1)
                    pe.wait_ge(sig("w_lo"), q0 + 2 + j * 3)
                    gate_up(1, 0)
                    turn_h(0, j)
                    gate_up(1, 1).then_inc(sig("w_used"), 1)
                    pe.wait_ge(sig("w_lo"), q0 + 3 + j * 3)
                    down(0, j)
                    turn_h(1, j)
                    if not last:
                        pe.wait_ge(sig("w_lo"), q0 + 4 + j * 3)
                        gate_up(0, 0)
                    down(1, j).then_inc(sig("w_used"), 1)

                pe.wait_ge(sig("w_lo"), q0 + 1)
                pe.wait_ge(sig("aT_lo"), 2 * layer + 1)
                gate_up(0, 0)
                pe.wait_ge(sig("router_exp"), layer + 1)
                for b in range(4):
                    pe.matmul(ps[:, b, :], zero16[:, 0:P], zero16[:, P:640], start=True, stop=False,
                              skip_group_check=True)
                pe.wait_ge(sig("aT_lo"), 2 * layer + 2)
                with pe.Fori(0, NE // 2 - 1) as j:
                    pair(j, False)
                pair(NE // 2 - 1, True)
                for b in range(4):
                    ins = pe.matmul(ps[:, b, :], zero16[:, 0:P], zero16[:, P:640], start=False, stop=True,
                                    skip_group_check=True)
                ins.then_inc(sig("moe_done"), 1)

            experts(0, MOE0, 6)
            act_transposes(7, x_tok)
            act_ready(7)
            qkv(SBI0, 0, 9)

            def sb_z(m):
                if m >= 2:
                    pe.wait_ge(sig("sb_zc"), m - 1)
                for j in range(2):
                    r, b = slice(64 * j, 64 * j + 64), 2 * (m % 2) + j
                    pe.matmul(ps[:, b, 0:S], k2T[r, 0, m, 0:P], q2T[r, 0, m, :], start=True, stop=True)
                    ins = pe.matmul(ps[:, b, S:384], k2T[r, 0, m, P:S], q2T[r, 0, m, P:S], start=True, stop=True)
                ins.then_inc(sig("sb_z"), 1)

            def sb_r(m):
                pe.wait_ge(sig("sb_sp"), m + 1)
                if m:
                    pe.wait_ge(sig("sb_d"), m)
                for j in range(2):
                    pe.matmul(ps[:, 4 + j, 0:384], low, sb_l[m % 2][:, j, :], start=True, stop=False,
                              skip_group_check=True)
                    ins = pe.matmul(ps[:, 4 + j, P:S], ones, sb_l[m % 2][:, j, S:384], start=False, stop=True,
                                    skip_group_check=True)
                ins.then_inc(sig("sb_r"), 1)

            def sb_pv(m):
                pe.wait_ge(sig("sb_att"), m + 1)
                if m >= 2:
                    pe.wait_ge(sig("sb_o"), m - 1)
                for j in range(2):
                    att, cols = sb_e[m % 2][:, j, :], slice(64 * (2 * m + j), 64 * (2 * m + j) + 64)
                    pe.matmul(ps[:, 6 + m % 2, j * 64:j * 64 + 64], att[:, 0:P], v2[:, 0, 0, cols], start=True, stop=True)
                    o = 128 + j * 64
                    pe.matmul(ps[:, 6 + m % 2, o:o + 64], att[:, P:S], v2[:, 0, 0, cols], start=True, stop=False)
                    ins = pe.matmul(ps[:, 6 + m % 2, o:o + 64], att[:, S:384], v2[:, 0, 1, cols], start=False, stop=True)
                ins.then_inc(sig("sb_pv"), 1)

            sb_z(0)
            for m in range(H2 // 2):
                if m + 1 < H2 // 2:
                    sb_z(m + 1)
                sb_r(m)
                if m:
                    sb_pv(m - 1)
            sb_pv(H2 // 2 - 1)
            act_transposes(8)
            act_ready(8)
            gemm_tok(SBO0, 0, 512).then_inc(sig("w_used"), 1)
            gemm_tok(SBO0 + 1, 2, 512).then_inc(sig("w_used"), 1)
            experts(1, MOE1, 9)

        def turned(eng, copy, i, gains, done, first):
            for b in range(first, KD // 2, 2):
                eng.wait_ge(sig("xp_pe"), KD * i + 2 * b + 2)
                for k in (2 * b, 2 * b + 1):
                    eng_out = copy(actT[:, k, :], ps[:, 4 + b, (k % 2) * S:(k % 2) * S + S],
                                   pcols(gains, k) if gains else 1.0)
                    eng_out.then_inc(sig(done), 1)

        @block.scalar
        def _(act):
            def copy(dst, src, scale=1.0):
                return act.activation(dst, src, ACT.Copy, scale=scale)

            def bank_pair(g, cols):
                return ps[:, (g % 2) * 2:(g % 2) * 2 + 2, 0:cols]

            act.wait_ge(sig("angle"), 1)
            act.activation(rope_cs[:, 1, :, :], rope_tmp[:, 0, 0:32].rearrange("p (t f) -> p t f", t=T), ACT.Sin)
            act.activation(rope_cs[:, 0, :, :], rope_tmp[:, 0, 0:32].rearrange("p (t f) -> p t f", t=T), ACT.Sin,
                           scale=0.5).then_inc(sig("sines"), 1)
            act.wait_ge(sig("pcol"), 1)
            turned(act, copy, 0, "g_mix", "xp_act", 0)
            act.wait_ge(sig("w_used"), 1)
            copy(cq, bank_pair(0, 384)).then_inc(sig("out_by_act"), 1)
            act.wait_ge(sig("w_used"), 3)
            copy(up, bank_pair(2, 512)).then_inc(sig("out_by_act"), 1)
            act.wait_ge(sig("w_used"), 4)
            act.activation(z_silu, bank_pair(3, 512), ACT.Silu).then_inc(sig("out_by_act"), 1)
            act.wait_ge(sig("w_used"), 6)
            for t in range(T):
                ins = copy(q_tok[:, t, :, :].rearrange("p (b h) d -> p b (h d)", b=2), ps[:, 4 + 2 * t:6 + 2 * t, 0:384])
            ins.then_inc(sig("q_out"), 1)
            act.wait_ge(sig("w_used"), 8)
            for t in range(T):
                src = ps[:, 4 + 2 * t:6 + 2 * t, :].rearrange("p b (h d) -> p (b h) d", h=4)
                copy(k_tok[:, t, :, 0:NOPE], src[:, :, 0:NOPE])
                ins = copy(v_tok[:, t, :, :], src[:, :, NOPE:])
            ins.then_inc(sig("kv_out"), 1)
            act.wait_ge(sig("w_used"), 9)
            act.activation(lru_g, ps[:, 0:2, :].rearrange("p b (c s) -> p (b c) s", c=2), ACT.Gelu_apprx_tanh)\
                .then_inc(sig("out_by_act"), 1)
            act.wait_ge(sig("qT_pe"), 1)
            copy(qT[0:QKD, :, :], ps[0:QKD, 4:8, :].rearrange("p b (h s) -> p (b h) s", h=2)).then_inc(sig("qT"), 1)
            act.wait_ge(sig("x_conv"), 1)
            act.activation(xbS, xbS, ACT.Silu).then_inc(sig("xbS"), 1)
            act.wait_ge(sig("sp_abs"), 1)
            act.activation(sp_e[:, :], sp_a[:, :], ACT.Exp, scale=-1.0)
            act.activation(a_head[:, :], brow[:, 8:16], ACT.Exp)
            act.drain()
            act.activation(sp_e[:, :], sp_e[:, :], ACT.Ln, bias=1.0).then_inc(sig("sp_ln"), 1)
            act.wait_ge(sig("kT_pe"), 1)
            copy(kT[0:QKD, :, :], ps[0:QKD, 4:8, :].rearrange("p b (h s) -> p (b h) s", h=2)).then_inc(sig("kT"), 1)

            def gate(i):
                g = 8 + i
                act.wait_ge(sig("w_used"), 11 + i)
                act.activation(gates[:, :, 512 * i:512 * i + 512], bank_pair(g, 512), ACT.Sigmoid)\
                    .then_inc(sig("out_by_act"), 1)

            def mla_exp(h):
                act.wait_ge(sig("mla_max"), h + 1)
                d = 2 * (h % 2)
                act.activation(probs[:, 0:P], probs[:, 0:P], ACT.Exp, bias=mx[:, 0:1], accum_out=den[:, d:d + 1])
                act.activation(probs[:, P:384], probs[:, P:384], ACT.Exp, bias=mx[:, 1:2],
                               accum_out=den[:, d + 1:d + 2]).then_inc(sig("mla_exp"), 1)

            def xs_out():
                act.wait_ge(sig("xs_pe"), 1)
                copy(xs_tok, ps[:, 6:8, :]).then_inc(sig("xs_tok"), 1)

            def dm_exp(half):
                act.wait_ge(sig("dm"), half + 1)
                v = dm[:, 4 * half:4 * half + 4, :]
                act.activation(v, v, ACT.Exp).then_inc(sig("dm_exp"), 1)

            def lru_sigmoid(i):
                act.wait_ge(sig("lru_pe"), i + 1)
                dst, bias = ((lru_r, "lru_b_a"), (lru_i, "lru_b_i"))[i]
                for c in range(KM):
                    ins = act.activation(dst[:, c, :], ps[:, 6 + c // 2, (c % 2) * S:(c % 2) * S + S], ACT.Sigmoid,
                                         bias=pcols(bias, c))
                ins.then_inc(sig(("lru_r", "lru_i")[i]), 1)

            def lru_decay():
                act.wait_ge(sig("lru_nl"), 1)
                act.activation(lru_a, lru_r, ACT.Exp, scale=-1.0)
                act.activation(lru_t, lru_r, ACT.Tanh).then_inc(sig("lru_at"), 1)

            def lru_root():
                act.wait_ge(sig("lru_sq"), 1)
                act.activation(lru_t, lru_t, ACT.Sqrt).then_inc(sig("lru_root"), 1)

            extra = {1: [xs_out], 2: [lambda: dm_exp(0)], 3: [lambda: dm_exp(1)], 4: [lambda: lru_sigmoid(0)],
                     5: [lambda: lru_sigmoid(1), lru_decay], 6: [lru_root]}
            for i in range(8):
                gate(i)
                mla_exp(i)
                for f in extra.get(i, []):
                    f()
            act.wait_ge(sig("mla_oT_pe"), KM)
            copy(yaT, ps[:, 4:6, :].rearrange("p b (c s) -> p (b c) s", c=2)).then_inc(sig("yaT"), 1)
            turned(act, copy, 1, None, "xp_act", 0)
            turned(act, copy, 2, "g_mlp", "xp_act", 0)
            for i in range(8):
                act.wait_ge(sig("w_used"), 25 + i)
                act.activation(hidT[:, 4 * i:4 * i + 4, :],
                               ps[:, (i % 2) * 2:(i % 2) * 2 + 2, :].rearrange("p b (c s) -> p (b c) s", c=2),
                               ACT.Relu).then_inc(sig("ff1_relu"), 1)
            act.wait_ge(sig("pT_pe"), 2)
            copy(pT, ps[:, 4, :].rearrange("p (c s) -> p c s", c=2)).then_inc(sig("pT"), 1)
            for i in range(2):
                act.wait_ge(sig("flip_pe"), i + 1)
                copy(bias_h[:, 8 * i:8 * i + 8, :], ps[:, 4:8, :].rearrange("p b (h s) -> p (b h) s", h=2))\
                    .then_inc(sig("bias_h"), 1)
            turned(act, copy, 3, "g_ple", "xp_act", 0)
            for h in range(2):
                act.wait_ge(sig("w_used"), 42 + h)
                act.activation(x_norm[:, :, 512 * h:512 * h + 512], ps[:, 4 + 2 * h:6 + 2 * h, :], ACT.Sigmoid)\
                    .then_inc(sig("ple_gate"), 1)
            turned(act, copy, 4, None, "xp_act", 0)

            def qkv(n0, g, step):
                for i, (dst, scale) in enumerate(((q2T, 0.125), (k2T, 1.0), (v2, 1.0))):
                    act.wait_ge(sig("w_used"), n0 + 2 * i + 1 + g * step)
                    d = dst[:, bass.ds(g, 1), 0:4, :] if i < 2 else dst[:, bass.ds(g, 1), :, 0:512]
                    src = ps[:, 0:2, :].rearrange("p b (c s) -> p (b c) s", c=2) if i < 2 else ps[:, 0:2, :]
                    copy(d.rearrange("p o c s -> p (o c) s"), src, scale).then_inc(sig("qkv_act"), 1)

            with act.Fori(0, 3) as g:
                qkv(DIL0, g, 6)

            def dil_exp(h):
                act.wait_ge(sig("dil_max"), h + 1)
                d = 2 * (h % 2)
                e, m = e_dil[:, h % 2, :], mx4[:, d:d + 2]
                act.activation(e[:, 0:384], e[:, 0:384], ACT.Exp, bias=m[:, 0:1], accum_out=den[:, d:d + 1])
                act.activation(e[:, 384:], e[:, 384:], ACT.Exp, bias=m[:, 1:2], accum_out=den[:, d + 1:d + 2])\
                    .then_inc(sig("dil_exp"), 1)

            dil_exp(0)
            for h in range(H2):
                if h + 1 < H2:
                    dil_exp(h + 1)
                act.wait_ge(sig("dil_pT_pe"), h + 1)
                copy(eT_dil[:, 0:384], ps[:, 3, 0:384]).then_inc(sig("dil_pT_act"), 1)
            turned(act, copy, 5, None, "xp_act", 0)

            def w_split(n0, b, j):
                n = n0 + b
                act.wait_ge(sig(f"w_landed{n % RING}"), 32 * (n // RING + 1) + j * 32)
                act.wait_ge(sig("w_used"), n - 2 + j * 3)
                copy(w_hi[:, n % 3, :], w_ring[:, n % RING, :], W_POW).then_inc(sig("w_hi"), 1)

            def experts(layer, n0, turn):
                for b in range(2):
                    w_split(n0, b, 0)
                turned(act, copy, turn, None, "xp_act", 0)
                act.wait_ge(sig("xp_dve"), 4 * turn + 4)
                act.drain()
                for t in range(T):
                    copy(aT_hi[:, :, t * P:(t + 1) * P], actT[:, :, t * P:(t + 1) * P], A_POW).then_inc(sig("aT_hi"), 1)
                act.wait_ge(sig("logits"), layer + 1)
                act.activation(score, ps[:, 0, 0:T * NE], ACT.Exp, scale=-1.0).then_inc(sig("router_exp"), 1)

                def silu(b, j):
                    act.wait_ge(sig("w_used"), n0 + b + 1 + j * 3)
                    act.activation(e_silu[:, b, :, :], ps[:, 4 + 2 * b:6 + 2 * b, 0:DE], ACT.Silu, scale=1.0 / SUM_POW)\
                        .then_inc(sig("moe_silu"), 1)

                def h_high(b, j):
                    act.wait_ge(sig("moe_hT_pe"), NE * layer + 1 + b + j * 2)
                    copy(hT_hi[:, b, :], ps[:, 4 + 2 * b, :]).then_inc(sig("moe_hT_hi"), 1)

                def pair(j, last):
                    silu(0, j)
                    w_split(n0, 2, j)
                    if not last:
                        w_split(n0 + 3, 0, j)
                    h_high(0, j)
                    silu(1, j)
                    if not last:
                        w_split(n0 + 3, 1, j)
                    h_high(1, j)

                with act.Fori(0, NE // 2 - 1) as j:
                    pair(j, False)
                pair(NE // 2 - 1, True)

            act.wait_ge(sig("dil_pv"), H2)
            experts(0, MOE0, 6)
            turned(act, copy, 7, None, "xp_act", 0)
            for i, (dst, scale) in enumerate(((q2T, 0.125), (k2T, 1.0), (v2, 1.0))):
                act.wait_ge(sig("w_used"), SBI0 + 2 * i + 1)
                d = dst[:, 0, 0:4, :] if i < 2 else dst[:, 0, :, 0:512]
                src = ps[:, 0:2, :].rearrange("p b (c s) -> p (b c) s", c=2) if i < 2 else ps[:, 0:2, :]
                copy(d, src, scale).then_inc(sig("qkv_act"), 1)

            def sb_softplus(m):
                act.wait_ge(sig("sb_zc"), m + 1)
                act.activation(sb_l[m % 2], sb_e[m % 2], ACT.Exp)
                act.drain()
                act.activation(sb_l[m % 2], sb_l[m % 2], ACT.Ln, bias=1.0).then_inc(sig("sb_ln"), 1)

            def sb_exp(m):
                act.wait_ge(sig("sb_d"), m + 1)
                act.activation(sb_e[m % 2], sb_e[m % 2], ACT.Exp).then_inc(sig("sb_exp"), 1)

            sb_softplus(0)
            for m in range(H2 // 2):
                if m + 1 < H2 // 2:
                    sb_softplus(m + 1)
                sb_exp(m)
            turned(act, copy, 8, None, "xp_act", 0)
            experts(1, MOE1, 9)

        @block.vector
        def _(dve):
            def scaled(dst, src, scale):
                return dve.tensor_scalar(dst, src, scale, None, ALU.mult)

            def bank_pair(g, cols, o=0):
                return ps[:, (g % 2) * 2:(g % 2) * 2 + 2, o:o + cols]

            def mean_square(src, cols, i, junk):
                for t in range(T):
                    dve.tensor_tensor_reduce(junk[:, t, 0:cols], src[:, t, :], src[:, t, :], 1.0, 0.0, ALU.mult, ALU.add,
                                             ms[:, i + t:i + t + 1])
                dve.drain()
                return dve.tensor_scalar(ms[:, i:i + T], ms[:, i:i + T], 1.0 / cols, EPS, ALU.mult, ALU.add)

            def rmsnorm_x(n, i):
                mean_square(x_tok, D, 0, x_norm).then_inc(sig("ms_ready"), 1)
                dve.wait_ge(sig("rstd_ready"), n + 1)
                for t in range(T):
                    ins = scaled(x_norm[:, t, :], x_tok[:, t, :], rstd[:, t:t + 1])
                ins.then_inc(sig("xn_ready"), 1)

            junk = gates[:, :, 0:D]
            dve.wait_ge(sig("ld_x"), 16)
            mean_square(x_norm, D, 0, junk).then_inc(sig("ms_ready"), 1)
            dve.wait_ge(sig("rstd_ready"), 1)
            for t in range(T):
                ins = scaled(x_norm[:, t, :], x_norm[:, t, :], rstd[:, t:t + 1])
            ins.then_inc(sig("xn_ready"), 1)
            dve.wait_ge(sig("ld_rows"), 16 * 6)
            dve.tensor_copy(pos_f[:, :], pos_i[:, :])
            dve.drain()
            ang, turns, tmp = (rope_tmp[:, 0, 32 * i:32 * i + 32] for i in range(3))
            for t in range(T):
                dve.tensor_scalar(ang[:, 16 * t:16 * t + 16], inv_freq, pos_f[:, t:t + 1], None, ALU.mult)
            dve.drain()
            dve.tensor_scalar(turns, ang, float(1 / (2 * np.pi)), None, ALU.mult)
            dve.drain()
            dve.tensor_scalar(turns, turns, 12582912.0, None, ALU.add)
            dve.drain()
            dve.tensor_scalar(turns, turns, -12582912.0, None, ALU.add)
            dve.drain()
            c1 = 6.28125
            c2 = round((2 * np.pi - c1) * 2 ** 19) / 2 ** 19
            c3 = 2 * np.pi - c1 - c2
            for c in (c1, c2, c3):
                dve.scalar_tensor_tensor(out=ang, in0=turns, scalar=-c, in1=ang, op0=ALU.mult, op1=ALU.add)
                dve.drain()
            dve.tensor_scalar(ang, ang, 3.1415925, -3.1415925, ALU.min, ALU.max).then_inc(sig("angle"), 1)
            dve.wait_ge(sig("params_T"), 1)
            dve.tensor_copy(pcol[:, :], ps[:, 0, 0:NPROW]).then_inc(sig("pcol"), 1)
            dve.drain()
            turned(dve, scaled, 0, "g_mix", "xp_dve", 1)
            dve.wait_ge(sig("sines"), 1)
            cos, sin = rope_cs[:, 0, :, :], rope_cs[:, 1, :, :]
            dve.tensor_tensor(cos, cos, cos, ALU.mult)
            dve.drain()
            dve.tensor_scalar(cos, cos, -2.0, 1.0, ALU.mult, ALU.add)
            dve.wait_ge(sig("w_used"), 2)
            for t in range(T):
                ins = dve.tensor_copy(u_cqkv[:, T * QL + 288 * t:T * QL + 288 * t + 288], ps[:, 2 + t, 0:288])
            ins.then_inc(sig("out_by_dve"), 1)
            dve.drain()
            dve.wait_ge(sig("out_by_act"), 1)
            mean_square(cq, QL, 0, junk)
            mean_square(ckv[:, :, 0:KVL], KVL, 2, junk).then_inc(sig("ms_ready"), 1)
            dve.wait_ge(sig("rstd_ready"), 2)
            for t in range(T):
                scaled(cq[:, t, :], cq[:, t, :], rstd[:, t:t + 1])
                ins = scaled(ckv[:, t, 0:KVL], ckv[:, t, 0:KVL], rstd[:, 2 + t:3 + t])
            ins.then_inc(sig("mla_normed"), 1)
            dve.wait_ge(sig("pool_d"), 1)
            dve.tensor_copy(u_dT, ps[:, 4:6, :].rearrange("p b s -> p (b s)")).then_inc(sig("dT"), 1)
            dve.wait_ge(sig("w_used"), 5)
            xb_in = xbT[:, :, CONV - 1:]
            dve.tensor_copy(xb_in[:, 0:2, :], ps[:, 0, :].rearrange("p (c s) -> p c s", c=2))
            dve.tensor_copy(xb_in[:, 2, :], ps[:, 1, 0:S]).then_inc(sig("out_by_dve"), 1)
            dve.wait_ge(sig("cT_pe"), 1)
            for k in range(5):
                gain = pcols("q_norm", k) if k < 3 else pcols("kv_norm", k - 3)
                ins = scaled(cT[:, k, :], ps[:, 4 + k // 2, (k % 2) * S:(k % 2) * S + S], gain)
            ins.then_inc(sig("cT"), 1)

            def rope(x, heads, t4):
                def cs(c):
                    return c.unsqueeze(2).broadcast_to([P, T, heads, 16]) if heads > 1 else c
                lo, hi = (x[:, :, :, 0:16], x[:, :, :, 16:32]) if heads > 1 else (x[:, :, 0:16], x[:, :, 16:32])
                dve.tensor_tensor(t4[0], lo, cs(cos), ALU.mult)
                dve.tensor_tensor(t4[1], hi, cs(sin), ALU.mult)
                dve.tensor_tensor(t4[2], hi, cs(cos), ALU.mult)
                dve.tensor_tensor(t4[3], lo, cs(sin), ALU.mult)
                dve.drain()
                dve.tensor_tensor(lo, t4[0], t4[1], ALU.subtract)
                return dve.tensor_tensor(hi, t4[2], t4[3], ALU.add)

            dve.wait_ge(sig("q_out"), 1)
            rope(q_tok[:, :, :, NOPE:], MH, [rope_tmp[:, i, :].rearrange("p (t h f) -> p t h f", t=T, h=MH)
                                             for i in range(4)]).then_inc(sig("q_roped"), 1)
            dve.wait_ge(sig("w_used"), 7)
            dve.tensor_copy(xb_in[:, 3:5, :], ps[:, 2, :].rearrange("p (c s) -> p c s", c=2))
            dve.tensor_copy(xb_in[:, 5, :], ps[:, 3, 0:S])
            dve.tensor_tensor(sp_v[:, 0:16].rearrange("p (t h) -> p t h", t=T),
                              ps[:, 3, S:S + 16].rearrange("p (t h) -> p t h", t=T),
                              brow[:, 0:8].unsqueeze(1).broadcast_to([P, T, MH]), ALU.add)\
                .then_inc(sig("out_by_dve"), 1)
            dve.tensor_scalar(sp_v[:, 16:20], pcol[:, PROW["lru_lambda"]:PROW["lru_lambda"] + 4], -1.0, None, ALU.mult)
            dve.drain()
            dve.scalar_tensor_tensor(out=sp_a[:, :], in0=sp_v[:, :], scalar=-1.0, in1=sp_v[:, :], op0=ALU.mult, op1=ALU.max)\
                .then_inc(sig("sp_abs"), 1)
            rope(ckv[:, :, KVL:288], 1, [rope_tmp[:, i, 0:32].rearrange("p (t f) -> p t f", t=T) for i in range(4)])
            dve.drain()
            dve.wait_ge(sig("kv_out"), 1)
            for t in range(T):
                ins = dve.tensor_copy(k_tok[:, t, :, NOPE:], ckv[:, t:t + 1, KVL:288].broadcast_to([P, MH, ROPE]))
            ins.then_inc(sig("k_roped"), 1)

            def conv(dst, src, chunks, w, b):
                for j in range(CONV):
                    for c in range(chunks):
                        win = src[:, c, j:j + S]
                        if j == 0:
                            ins = dve.tensor_scalar(dst[:, c, :], win, pcols(w, c), pcols(b, c), ALU.mult, ALU.add)
                        else:
                            ins = dve.scalar_tensor_tensor(out=dst[:, c, :], in0=win, scalar=pcols(w, j * chunks + c),
                                                           in1=dst[:, c, :], op0=ALU.mult, op1=ALU.add)
                    if j < CONV - 1:
                        dve.drain()
                return ins

            dve.wait_ge(sig("lru_zeroed"), 1)
            conv(xbS, xbT, KX, "ssd_conv_w", "ssd_conv_b").then_inc(sig("x_conv"), 1)
            dve.wait_ge(sig("w_used"), 10)
            dve.tensor_copy(lxT[:, :, CONV - 1:], ps[:, 2:4, :].rearrange("p b (c s) -> p (b c) s", c=2))\
                .then_inc(sig("out_by_dve"), 1)
            dve.wait_ge(sig("sp_ln"), 1)
            dve.scalar_tensor_tensor(out=sp_v[:, :], in0=sp_v[:, :], scalar=0.0, in1=sp_e[:, :], op0=ALU.max, op1=ALU.add)
            dve.drain()
            dve.tensor_copy(stats[:, 0:16], sp_v[:, 0:16])
            dve.tensor_scalar(decay8[:, :], sp_v[:, 16:20], 8.0, None, ALU.mult)
            dve.drain()
            dve.scalar_tensor_tensor(out=a_tok, in0=dt_tok, scalar=-1.0,
                                     in1=a_head[:, :].unsqueeze(1).broadcast_to([P, T, MH]),
                                     op0=ALU.mult, op1=ALU.mult).then_inc(sig("a_tok"), 1)
            conv(xcT, lxT, KM, "lru_conv_w", "lru_conv_b").then_inc(sig("xcT"), 1)

            def mla_max(h):
                dve.wait_ge(sig("mla_scores"), h + 1)
                if h:
                    dve.wait_ge(sig("mla_pT_pe"), h)
                dve.tensor_tensor_reduce(probs[:, 0:P], ps[:, 4, 0:P], cmask, MLA_SCALE, -3e38, ALU.add, ALU.max,
                                         mx[:, 0:1])
                dve.tensor_tensor_reduce(probs[:, P:384], ps[:, 4, P:384], zc_mask[:, :], MLA_SCALE, -3e38,
                                         ALU.add, ALU.max, mx[:, 1:2])
                dve.drain()
                dve.tensor_scalar(mx, mx, -1.0, None, ALU.mult).then_inc(sig("mla_max"), 1)

            def mla_o(h):
                dve.wait_ge(sig("mla_pT_pe"), h + 1)
                dve.tensor_copy(probsT, ps[:, 5, 0:384]).then_inc(sig("mla_pT"), 1)
                d = 2 * (h % 2)
                dve.reciprocal(den[:, 4 + d:6 + d], den[:, d:d + 2])
                dve.drain()
                dve.wait_ge(sig("mla_pv"), h + 1)
                for t in range(T):
                    ins = scaled(o_mla[:, t, 64 * h:64 * h + 64], ps[:, 5, 384 + 64 * t:448 + 64 * t],
                                 den[:, 4 + d + t:5 + d + t])
                ins.then_inc(sig("mla_o"), 1)

            def cb_mask():
                dve.wait_ge(sig("cb_pe"), 1)
                for gr in range(2):
                    ins = dve.tensor_tensor(cbm[:, gr, :], ps[:, 6 + gr, 0:384], tri3, ALU.mult)
                ins.then_inc(sig("cbm"), 1)

            def ssd_xdt():
                dve.wait_ge(sig("acs_pe"), 1)
                dve.tensor_copy(stats[:, 32:48], ps[:, 6, 0:16]).then_inc(sig("acs"), 1)
                dve.wait_ge(sig("xs_tok"), 1)
                dve.tensor_tensor(xdt.rearrange("p t (h d) -> p (t h) d", d=64),
                                  xs_tok.rearrange("p t (h d) -> p (t h) d", d=64),
                                  stats[:, 0:16].unsqueeze(2).broadcast_to([P, 16, 64]), ALU.mult).then_inc(sig("xdt"), 1)

            def decay(half):
                dve.wait_ge(sig("cum_pe"), half + 1)
                dve.drain()
                for j in range(4):
                    h = 4 * half + j
                    src = ps[:, 6 + j // 2, (j % 2) * S:(j % 2) * S + S]
                    dve.tensor_scalar(dm[:, h, 0:S], src, acs[:, 0, h:h + 1], 0.0, ALU.subtract, ALU.min)
                    ins = dve.tensor_scalar(dm[:, h, S:384], src[:, P:S], acs[:, 1, h:h + 1], 0.0, ALU.subtract, ALU.min)
                ins.then_inc(sig("dm"), 1)

            def decay_cb():
                for half in range(2):
                    dve.wait_ge(sig("dm_exp"), half + 1)
                    for j in range(4):
                        ins = dve.tensor_tensor(dm[:, 4 * half + j, :], dm[:, 4 * half + j, :], cbm[:, half, :], ALU.mult)
                ins.then_inc(sig("dm_cb"), 1)

            def lru_log():
                dve.wait_ge(sig("lru_r"), 1)
                for c in range(KM):
                    ins = scaled(lru_r[:, c, :], lru_r[:, c, :], decay8[:, c:c + 1])
                ins.then_inc(sig("lru_nl"), 1)

            def ssd_out():
                dv = y_ssd.rearrange("p t (h d) -> p t h d", h=MH)
                for t in range(T):
                    dve.tensor_tensor(dv[:, t, :, :], xs_tok[:, t, :].rearrange("p (h d) -> p h d", h=MH),
                                      brow[:, 16:24].unsqueeze(2).broadcast_to([P, MH, 64]), ALU.mult)
                dve.drain()
                dve.wait_ge(sig("ssd_y_pe"), 1)
                dve.tensor_tensor(y_ssd, y_ssd, ps[:, 6:8, :], ALU.add).then_inc(sig("ssd_y"), 1)
                dve.drain()
                dve.tensor_tensor(y_ssd, y_ssd, z_silu, ALU.mult)
                dve.drain()
                mean_square(y_ssd, MIX, 0, xs_tok).then_inc(sig("ms_ready"), 1)
                dve.wait_ge(sig("rstd_ready"), 3)
                for t in range(T):
                    ins = scaled(y_ssd[:, t, :], y_ssd[:, t, :], rstd[:, t:t + 1])
                ins.then_inc(sig("ssd_normed"), 1)

            def lru_input():
                dve.wait_ge(sig("lru_at"), 1)
                sq = xs_tok.rearrange("p t n -> p (t n)").rearrange("p (c s) -> p c s", c=KM)
                dve.drain()
                dve.tensor_tensor(sq, lru_a, lru_a, ALU.mult)
                dve.drain()
                dve.scalar_tensor_tensor(out=lru_t, in0=sq, scalar=1.0, in1=lru_t, op0=ALU.add, op1=ALU.mult)\
                    .then_inc(sig("lru_sq"), 1)
                dve.wait_ge(sig("lru_i"), 1)
                dve.tensor_tensor(lru_i, lru_i, xcT, ALU.mult)

            def pool_out():
                dve.wait_ge(sig("pool_y"), 1)
                for c in range(KM):
                    ins = scaled(ybT[:, c, :], ps[:, 6 + c // 2, (c % 2) * S:(c % 2) * S + S], pcols("pool_scale", c))
                ins.then_inc(sig("ybT"), 1)

            def lru_scan():
                dve.wait_ge(sig("lru_root"), 1)
                dve.drain()
                dve.tensor_tensor(lru_i, lru_i, lru_t, ALU.mult)
                dve.drain()
                for c in range(KM):
                    dve.tensor_tensor_scan(lru_r[:, c, :], lru_a[:, c, :], lru_i[:, c, :], 0.0, ALU.mult, ALU.add)
                dve.drain()
                dve.tensor_tensor(lru_g, lru_g, lru_r, ALU.mult).then_inc(sig("ydT"), 1)

            def ssd_turned():
                dve.wait_ge(sig("ycT_pe"), KM)
                for c in range(KM):
                    ins = scaled(ycT[:, c, :], ps[:, 6 + c // 2, (c % 2) * S:(c % 2) * S + S], pcols("ssd_norm", c))
                ins.then_inc(sig("ycT"), 1)

            extra = {0: [cb_mask], 1: [ssd_xdt], 2: [lambda: decay(0)], 3: [lambda: decay(1), decay_cb],
                     4: [lru_log], 5: [ssd_out], 6: [lru_input, pool_out], 7: [lru_scan, ssd_turned]}
            dve.memset(zc_mask[:, 0:P], 0.0)
            dve.tensor_copy(zc_mask[:, P:S], cmask)
            dve.drain()
            for i in range(8):
                mla_max(i)
                if i:
                    mla_o(i - 1)
                for f in extra[i]:
                    f()
            mla_o(MH - 1)
            for i, b in enumerate((1, 0, 3, 2)):
                dve.wait_ge(sig("w_used"), 19 + i)
                if i == 0:
                    dve.wait_ge(sig("out_by_act"), 12)
                for t in range(T):
                    y = ps[:, 4 * (i % 2) + 2 * t:4 * (i % 2) + 2 * t + 2, :].rearrange("p b n -> p (b n)")
                    gt = gates[:, t, D * b:D * b + D]
                    if i == 0:
                        ins = dve.tensor_tensor(x_norm[:, t, :], y, gt, ALU.mult)
                    else:
                        ins = dve.tensor_tensor(gt, y, gt, ALU.mult)
                ins.then_inc(sig("branch"), 1)
                if i:
                    dve.drain()
                    for t in range(T):
                        ins = dve.tensor_tensor(x_norm[:, t, :], x_norm[:, t, :], gates[:, t, D * b:D * b + D], ALU.add)
                if i < 3:
                    dve.drain()
            ins.then_inc(sig("xn_ready"), 1)
            turned(dve, scaled, 1, None, "xp_dve", 1)
            dve.wait_ge(sig("ld_x"), 32)
            for h in range(2):
                dve.wait_ge(sig("w_used"), 23 + h)
                ins = dve.tensor_tensor(x_tok[:, :, 512 * h:512 * h + 512], x_tok[:, :, 512 * h:512 * h + 512],
                                        ps[:, 2 * h:2 * h + 2, :], ALU.add)
            ins.then_inc(sig("x_res"), 1)
            dve.drain()
            rmsnorm_x(3, 2)
            turned(dve, scaled, 2, "g_mlp", "xp_dve", 1)
            for i in range(8):
                dve.wait_ge(sig("ff1_relu"), i + 1)
                h4 = hidT[:, 4 * i:4 * i + 4, :]
                dve.tensor_tensor(h4, h4, h4, ALU.mult).then_inc(sig("ff1_square"), 1)
            dve.wait_ge(sig("rel_pe"), 1)
            dve.tensor_copy(rel_row, ps[0:H2, 5, 0:384]).then_inc(sig("rel_row"), 1)
            dve.wait_ge(sig("w_used"), 40)
            ins = dve.tensor_tensor(x_tok[:, :, :].rearrange("p t n -> p (t n)"), x_tok[:, :, :].rearrange("p t n -> p (t n)"),
                                    ps[:, 0:4, :].rearrange("p b n -> p (b n)"), ALU.add)
            ins.then_inc(sig("x_res"), 1)
            dve.drain()
            rmsnorm_x(4, 3)
            turned(dve, scaled, 3, "g_ple", "xp_dve", 1)
            dve.wait_ge(sig("ple_gate"), 2)
            xn, xt = (v[:, :, :].rearrange("p t n -> p (t n)") for v in (x_norm, x_tok))
            dve.tensor_tensor(xn, xn, ps[:, 0:4, :].rearrange("p b n -> p (b n)"), ALU.mult).then_inc(sig("x_res"), 1)
            dve.drain()
            dve.tensor_tensor(xt, xt, xn, ALU.add)
            dve.drain()
            mean_square(x_tok, D, 0, x_norm).then_inc(sig("ms_ready"), 1)
            dve.wait_ge(sig("rstd_ready"), 6)
            dve.wait_ge(sig("ld_gb"), 16)
            for t in range(T):
                ins = dve.scalar_tensor_tensor(out=x_tok[:, t, :], in0=x_tok[:, t, :], scalar=rstd[:, t:t + 1],
                                               in1=ln_gb[:, 0, :], op0=ALU.mult, op1=ALU.mult)
            ins.then_inc(sig("xn_ready"), 1)
            dve.drain()
            dve.engine_nop().then_inc(sig("gb_free"), 1)
            turned(dve, scaled, 4, None, "xp_dve", 1)

            def qkv(n0, g, step):
                for i, (dst, scale) in enumerate(((q2T, 0.125), (k2T, 1.0), (v2, 1.0))):
                    dve.wait_ge(sig("w_used"), n0 + 2 * i + 2 + g * step)
                    d = dst[:, bass.ds(g, 1), 4:8, :] if i < 2 else dst[:, bass.ds(g, 1), :, 512:]
                    src = ps[:, 2:4, :].rearrange("p b (c s) -> p (b c) s", c=2) if i < 2 else ps[:, 2:4, :]
                    scaled(d.rearrange("p o c s -> p (o c) s"), src, scale).then_inc(sig("qkv_dve"), 1)

            with dve.Fori(0, 3) as g:
                qkv(DIL0, g, 6)

            def dil_max(h):
                dve.wait_ge(sig("dil_scores"), h + 1)
                dve.wait_ge(sig("bm"), h + 1)
                if h >= 2:
                    dve.wait_ge(sig("dil_pT_pe"), h - 1)
                e, m = e_dil[:, h % 2, :], mx4[:, 2 * (h % 2):2 * (h % 2) + 2]
                dve.tensor_tensor_reduce(e[:, 0:384].rearrange("p (g s) -> p g s", g=3),
                                         ps[:, 0, 0:384].rearrange("p (g s) -> p g s", g=3), bm[:, h % 2, :, P:S],
                                         1.0, -3e38, ALU.add, ALU.max, m[:, 0:1])
                dve.tensor_tensor_reduce(e[:, 384:], ps[:, 1:3, :].rearrange("p b n -> p (b n)")[:, 0:768],
                                         bm[:, h % 2, :, :].rearrange("p g s -> p (g s)"),
                                         1.0, -3e38, ALU.add, ALU.max, m[:, 1:2])
                dve.drain()
                dve.tensor_scalar(m, m, -1.0, None, ALU.mult).then_inc(sig("dil_max"), 1)

            dil_max(0)
            for h in range(H2):
                if h + 1 < H2:
                    dil_max(h + 1)
                dve.wait_ge(sig("dil_pT_pe"), h + 1)
                dve.tensor_copy(eT_dil[:, 384:], ps[:, 4:6, :].rearrange("p b n -> p (b n)")[:, 0:768])\
                    .then_inc(sig("dil_pT_dve"), 1)
                d = 2 * (h % 2)
                dve.reciprocal(den[:, 4 + d:6 + d], den[:, d:d + 2])
                dve.drain()
                dve.wait_ge(sig("dil_pv"), h + 1)
                for t in range(T):
                    ins = scaled(x_norm[:, t, 64 * h:64 * h + 64], ps[:, 6 + h % 2, 64 * t:64 * t + 64],
                                 den[:, 4 + d + t:5 + d + t])
                ins.then_inc(sig("dil_o"), 1)
            dve.drain()
            dve.engine_nop().then_inc(sig("xn_ready"), 1)
            turned(dve, scaled, 5, None, "xp_dve", 1)

            def w_split(n0, b, j):
                n = n0 + b
                dve.wait_ge(sig("w_hi"), moe_index(n0) + b + 1 + j * 3)
                dve.scalar_tensor_tensor(out=w_lo[:, n % 3, :], in0=w_ring[:, n % RING, :], scalar=W_POW,
                                         in1=w_hi[:, n % 3, :], op0=ALU.mult, op1=ALU.subtract).then_inc(sig("w_lo"), 1)

            def layer_norm(m, halves_first, done):
                pow2 = 1.0 if halves_first else SUM_POW
                for h in range(2):
                    if halves_first:
                        src = ps[:, 2 * h:2 * h + 2, :]
                    else:
                        src = ps[:, 0:4, :].rearrange("p (t h) n -> p t h n", h=2)[:, :, h, :]
                    xh = x_tok[:, :, 512 * h:512 * h + 512]
                    dve.scalar_tensor_tensor(out=xh, in0=xh, scalar=ALPHA * pow2, in1=src, op0=ALU.mult, op1=ALU.add)
                dve.drain()
                for t in range(T):
                    for h in range(2):
                        dve.bn_stats(bn_part[:, t, h, :], x_tok[:, t, 512 * h:512 * h + 512])
                dve.drain()
                for t in range(T):
                    dve.bn_aggr(bn_mv[:, t, :], bn_part[:, t, :, :])
                dve.drain()
                dve.tensor_scalar(ms[:, 0:T], bn_mv[:, :, 1], LN_EPS * pow2 * pow2, None, ALU.add).then_inc(sig("ms_ready"), 1)
                dve.wait_ge(sig("rstd_ready"), 7 + m)
                for t in range(T):
                    dve.tensor_scalar(x_tok[:, t, :], x_tok[:, t, :], bn_mv[:, t, 0:1], rstd[:, t:t + 1],
                                      ALU.subtract, ALU.mult)
                dve.wait_ge(sig("ld_gb"), 16 + 32 * (m + 1))
                dve.drain()
                for t in range(T):
                    dve.tensor_tensor(x_tok[:, t, :], x_tok[:, t, :], ln_gb[:, 0, :], ALU.mult)
                dve.drain()
                for t in range(T):
                    ins = dve.tensor_tensor(x_tok[:, t, :], x_tok[:, t, :], ln_gb[:, 1, :], ALU.add)
                    if done != "xn_ready" or t == T - 1:
                        ins.then_inc(sig(done), 1)
                dve.drain()
                dve.engine_nop().then_inc(sig("gb_free"), 1)

            def rank_of_four(v, rank, tmp, init):
                dve.tensor_copy(rank, init)
                dve.drain()
                for s in (1, 2, 3):
                    c = tmp[:, :, 0:4 - s]
                    dve.tensor_tensor(c, v[:, :, 0:4 - s], v[:, :, s:4], ALU.is_ge)
                    dve.drain()
                    dve.tensor_tensor(rank[:, :, s:4], rank[:, :, s:4], c, ALU.add)
                    dve.drain()
                    dve.tensor_tensor(rank[:, :, 0:4 - s], rank[:, :, 0:4 - s], c, ALU.subtract)
                    dve.drain()

            def experts(layer, n0, turn):
                turned(dve, scaled, turn, None, "xp_dve", 1)
                dve.wait_ge(sig("xp_act"), 4 * turn + 4)
                dve.drain()
                for t in range(T):
                    c = slice(t * P, (t + 1) * P)
                    dve.wait_ge(sig("aT_hi"), 2 * layer + t + 1)
                    dve.scalar_tensor_tensor(out=aT_lo[:, :, c], in0=actT[:, :, c], scalar=A_POW, in1=aT_hi[:, :, c],
                                             op0=ALU.mult, op1=ALU.subtract).then_inc(sig("aT_lo"), 1)
                g4 = lambda v: v.rearrange("p (g e) -> p g e", e=4)
                tg = lambda v: v.rearrange("p (t e) -> p t e", t=T)
                dve.wait_ge(sig("router_exp"), layer + 1)
                dve.tensor_scalar(score, score, 1.0, None, ALU.add)
                dve.drain()
                dve.reciprocal(score, score)
                dve.drain()
                dve.tensor_tensor(tg(r_v), tg(score), brow[:, 24:40].unsqueeze(1).broadcast_to([P, T, NE]), ALU.add)
                dve.drain()
                rank_of_four(g4(r_v), g4(r_rank), g4(r_cmp), rank0)
                dve.tensor_scalar(r_sel, r_rank, 2.0, None, ALU.is_lt)
                dve.drain()
                dve.tensor_tensor(r_cmp, r_sel, r_v, ALU.mult)
                dve.drain()
                dve.tensor_reduce(r_gs, g4(r_cmp), AX.X, ALU.add)
                dve.drain()
                rank_of_four(g4(r_gs), g4(r_gr), g4(r_best), rank0[:, 0:T, :])
                dve.tensor_scalar(r_best, r_gr, 1.0, None, ALU.is_lt)
                dve.drain()
                dve.tensor_tensor(g4(r_sel), g4(r_sel), r_best.unsqueeze(2).broadcast_to([P, 8, 4]), ALU.mult)
                dve.drain()
                dve.tensor_tensor(r_sel, r_sel, score, ALU.mult)
                dve.drain()
                dve.tensor_reduce(r_den[:, 0:T], tg(r_sel), AX.X, ALU.add)
                dve.drain()
                dve.reciprocal(r_den[:, 2:2 + T], r_den[:, 0:T])
                dve.drain()
                dve.scalar_tensor_tensor(out=tg(r_gate), in0=tg(r_sel), scalar=A_POW / SUM_POW,
                                         in1=r_den[:, 2:2 + T].unsqueeze(2).broadcast_to([P, T, NE]),
                                         op0=ALU.mult, op1=ALU.mult)
                dve.drain()

                def weigh(b, j):
                    dve.wait_ge(sig("moe_silu"), NE * layer + b + 1 + j * 2)
                    for t in range(T):
                        ins = dve.scalar_tensor_tensor(out=h_tok[:, b, t, :], in0=ps[:, 4 + 2 * b + t, DE:2 * DE],
                                                       scalar=r_gate[:, bass.ds(2 * j + b + t * NE, 1)],
                                                       in1=e_silu[:, b, t, :], op0=ALU.mult, op1=ALU.mult)
                    ins.then_inc(sig("moe_h"), 1)

                def h_low(b, j):
                    dve.wait_ge(sig("moe_hT_hi"), NE * layer + 1 + b + j * 2)
                    dve.tensor_tensor(hT_lo[:, b, :], ps[:, 4 + 2 * b, :], hT_hi[:, b, :], ALU.subtract)\
                        .then_inc(sig("moe_hT"), 1)

                def pair(j, last):
                    weigh(0, j)
                    w_split(n0, 2, j)
                    h_low(0, j)
                    if not last:
                        w_split(n0 + 3, 0, j)
                    weigh(1, j)
                    if not last:
                        w_split(n0 + 3, 1, j)
                    h_low(1, j)

                with dve.Fori(0, NE // 2 - 1) as j:
                    pair(j, False)
                pair(NE // 2 - 1, True)
                dve.wait_ge(sig("moe_done"), layer + 1)

            for b in range(2):
                w_split(MOE0, b, 0)
            dve.wait_ge(sig("w_used"), DOUT0 + 2)
            layer_norm(0, True, "xn_ready")
            experts(0, MOE0, 6)
            layer_norm(1, False, "xn_ready")
            turned(dve, scaled, 7, None, "xp_dve", 1)
            for i, (dst, scale) in enumerate(((q2T, 0.125), (k2T, 1.0), (v2, 1.0))):
                dve.wait_ge(sig("w_used"), SBI0 + 2 * i + 2)
                d = dst[:, 0, 4:8, :] if i < 2 else dst[:, 0, :, 512:]
                src = ps[:, 2:4, :].rearrange("p b (c s) -> p (b c) s", c=2) if i < 2 else ps[:, 2:4, :]
                scaled(d, src, scale).then_inc(sig("qkv_dve"), 1)

            mask2 = strict3.unsqueeze(1).broadcast_to([P, 2, 384])

            def sb_clip(m):
                dve.wait_ge(sig("sb_z"), m + 1)
                if m >= 2:
                    dve.wait_ge(sig("sb_pv"), m - 1)
                z, b = sb_zt[m % 2], 2 * (m % 2)
                dve.tensor_scalar(z, ps[:, b:b + 2, 0:384], SB_CLIP, -SB_CLIP, ALU.min, ALU.max)
                dve.drain()
                dve.tensor_scalar(sb_e[m % 2], z, LN_TOP, None, ALU.min).then_inc(sig("sb_zc"), 1)
                dve.tensor_scalar(sb_h[m % 2], z, -LN_TOP, 0.0, ALU.add, ALU.max)

            def sb_sp(m):
                dve.wait_ge(sig("sb_ln"), m + 1)
                v = sb_l[m % 2]
                dve.drain()
                dve.tensor_tensor(v, v, sb_h[m % 2], ALU.add)
                dve.drain()
                dve.tensor_tensor(v, v, mask2, ALU.mult).then_inc(sig("sb_sp"), 1)

            def sb_att(m):
                dve.wait_ge(sig("sb_r"), m + 1)
                v = sb_e[m % 2]
                dve.tensor_tensor(v, sb_zt[m % 2], ps[:, 4:6, 0:384], ALU.subtract).then_inc(sig("sb_d"), 1)

            def sb_mask(m):
                dve.wait_ge(sig("sb_exp"), m + 1)
                v = sb_e[m % 2]
                dve.tensor_tensor(v, v, mask2, ALU.mult).then_inc(sig("sb_att"), 1)

            def sb_o(m):
                dve.wait_ge(sig("sb_pv"), m + 1)
                dve.tensor_copy(x_norm[:, :, P * m:P * m + P], ps[:, 6 + m % 2, 0:S].rearrange("p (t n) -> p t n", t=T))\
                    .then_inc(sig("sb_o"), 1)

            sb_clip(0)
            for m in range(H2 // 2):
                sb_sp(m)
                if m >= 1:
                    sb_o(m - 1)
                if m + 1 < H2 // 2:
                    sb_clip(m + 1)
                sb_att(m)
                sb_mask(m)
            sb_o(H2 // 2 - 1)
            dve.drain()
            dve.engine_nop().then_inc(sig("xn_ready"), 1)
            turned(dve, scaled, 8, None, "xp_dve", 1)
            for b in range(2):
                w_split(MOE1, b, 0)
            dve.wait_ge(sig("w_used"), SBO0 + 2)
            layer_norm(2, True, "xn_ready")
            experts(1, MOE1, 9)
            layer_norm(3, False, "out_ready")

_SHAPES_IN = ("x", "p", "positions", "w_in", "w_uq", "w_ukv", "w_pool", "ssd_dt_bias", "ssd_a_log", "ssd_d",
              "lru_w_a", "lru_w_i", "w_branch", "w_out", "w_ff1", "w_ff2", "w_ple_gate", "w_ple", "g_final",
              "rel_table_2", "router_w_2", "router_b_2", "ln1_g_2", "ln1_b_2", "ln2_g_2", "ln2_b_2",
              "exp_w_gate_2", "exp_w_up_2", "exp_w_down_2", "dil_w_in_2", "dil_w_out_2", "sb_w_in_2",
              "sb_w_out_2") + tuple(n for n, _ in PARAM_ROWS)


def kernel(**inputs):
    import concourse.bacc as bacc
    from concourse.bass_utils import run_bass_kernel_spmd

    nc = bacc.Bacc("TRN2", target_bir_lowering=False, num_devices=1)
    arrays, aps = {}, {}
    named = [(n, inputs[n]) for n in _SHAPES_IN] + list(constants().items())
    for name, value in named:
        if name == "positions":
            value = np.asarray(value).reshape(T, P).T
        v = np.ascontiguousarray(value)
        arrays["in_" + name] = v
        aps[name] = nc.dram_tensor("in_" + name, v.shape, mybir.dt.from_np(v.dtype), kind="ExternalInput").ap()
    out = nc.dram_tensor("out_0", (1, S, D), F32, kind="ExternalOutput").ap()
    build(nc, aps, out)
    r = run_bass_kernel_spmd(nc, [arrays], core_ids=[0])
    return r.results[0]["out_0"]
```

```python
from contextlib import ExitStack

import numpy as np
import concourse.bass as bass
from concourse import mybir

F32 = mybir.dt.float32
BF16 = mybir.dt.bfloat16
F16 = mybir.dt.float16
I32 = mybir.dt.int32
ALU = mybir.AluOpType
ACT = mybir.ActivationFunctionType
AX = mybir.AxisListType

P = 128
S = 256
T = S // P
D = 1024
KD = D // P
MIX = 512
KM = MIX // P
EPS = 1e-6
LN_EPS = 1e-5
QL, KVL, ROPE, NOPE = 384, 256, 32, 64
MH = 8
QKD = NOPE + ROPE
MLA_SCALE = float(QKD) ** -0.5
XBC = 768
KX = XBC // P
CONV = 4
NE = 16
DE = 256
H2 = 16
HD = 64
ALPHA = 4.0 ** 0.25
SB_CLIP = 60.0
LN_TOP = 40.0
NEG = -1e30
W_POW, A_POW = 2.0 ** 8, 2.0 ** 3
SUM_POW = W_POW * A_POW
RING = 3
SLOT = 4096

DIL0, DOUT0, MOE0, SBI0, SBO0, MOE1 = 43, 61, 63, 87, 93, 95

C_Q, C_KV, C_POOL, C_Z, C_XBC, C_DT, C_LG, C_LX, C_GATE = 0, 384, 672, 1184, 1696, 2464, 2472, 2984, 3496

PARAM_ROWS = (("g_mix", 8), ("q_norm", 3), ("kv_norm", 2), ("pool_scale", 4), ("ssd_conv_w", 24),
              ("ssd_conv_b", 6), ("ssd_norm", 4), ("lru_conv_w", 16), ("lru_conv_b", 4),
              ("lru_b_a", 4), ("lru_b_i", 4), ("lru_lambda", 4), ("g_mlp", 8), ("g_ple", 8), ("g_final", 8))
LN_ROWS = (("ln1_g_2", 0), ("ln1_b_2", 0), ("ln2_g_2", 0), ("ln2_b_2", 0), ("ln1_g_2", 1), ("ln1_b_2", 1))
PROW = {}
_at = 0
for _name, _n in PARAM_ROWS:
    PROW[_name] = _at
    _at += _n
NPROW = _at
NCOL = NPROW + 8 * len(LN_ROWS)


def constants():
    i = np.arange(P)
    f = np.float32
    eye = np.eye(P, dtype=f)
    flip = eye[::-1].copy()
    tri = (i[:, None] <= i[None, :]).astype(f)
    ones = np.ones((P, P), f)
    strict = (i[:, None] < i[None, :]).astype(f)
    low = (i[:, None] >= i[None, :]).astype(f)
    cmask = np.where(i[None, :] <= i[:, None], f(0), f(NEG)).astype(f)
    mats = np.concatenate([eye, flip, tri, ones, tri, strict, ones, strict, low, cmask], axis=1)
    t = np.arange(S)
    band = []
    for w in (2, 4, 8, 16):
        cnt = np.minimum(t + 1, w)
        m = ((t[:, None] <= t[None, :]) & (t[:, None] > t[None, :] - w)) / cnt[None, :] - np.eye(S)
        band.append(np.concatenate([m[:P, :], m[P:, P:]], axis=1).astype(f))
    band = np.concatenate(band, axis=1)
    dist = 255 - np.arange(384)
    n = np.maximum(dist, 0)
    logf = (np.log(np.maximum(n, 1).astype(f) / f(16)) / f(np.log(2048 / 16))).astype(f)
    large = np.minimum(16 + (logf * f(16)).astype(np.int32), 31)
    bucket = np.where(n < 16, n, large)
    onehot = (np.arange(32)[:, None] == bucket[None, :]).astype(f)
    d = 128 + i[:, None] - np.arange(S)[None, :]
    rel = np.stack([(d >= 0) & (d <= 128), (d >= 0) & (d % 4 == 0), (d >= 0) & (d % 16 == 0)], 1)
    relmask = np.where(rel, f(0), f(NEG)).astype(f)
    inv = (f(1) / (f(10000.0) ** (np.arange(0, ROPE, 2).astype(f) / f(ROPE)))).astype(f)
    rank0 = np.tile(np.array([3, 2, 1, 0], f), 8)
    rows = np.concatenate([inv, rank0]).reshape(1, 48).repeat(P, 0).astype(f)
    return {"c_mats": mats, "c_band": band.astype(f), "c_onehot": onehot,
            "c_relmask": relmask.reshape(P, 3 * S), "c_rows": rows}


def build(nc, a, out):
    ctx = ExitStack()
    with ctx:
        sems = {}

        def sig(name):
            if name not in sems:
                sems[name] = ctx.enter_context(nc.semaphore(name))
            return sems[name]

        def sb(name, shape, dt=F32):
            return ctx.enter_context(nc.sbuf_tensor(name, shape, dt))

        w_ring = sb("w_ring", [P, RING, SLOT])
        x_tok = sb("x_tok", [P, T, D])
        x_norm = sb("x_norm", [P, T, D])
        actT = sb("actT", [P, KD, S])
        ln_gb = sb("ln_gb", [P, 2, D])
        mats = sb("mats", [P, 10, P])
        crow = sb("crow", [P, 48])
        brow = sb("brow", [P, 24 + NE])
        pcol = sb("pcol", [P, NCOL])
        stats = sb("stats", [P, 64])
        lru_w = sb("lru_w", [P, 2, KM, P])
        pool_w = sb("pool_w", [P, KM, P])
        ARENA = 28350
        arena = sb("arena", [P, ARENA])
        ps = ctx.enter_context(nc.psum_tensor("ps", [P, 8, 512], F32))

        ident, flip = mats[:, 0, :], mats[:, 1, :]
        tri3 = mats[:, 2:5, :].rearrange("p a b -> p (a b)")
        tri, ones = mats[:, 2, :], mats[:, 3, :]
        strict3 = mats[:, 5:8, :].rearrange("p a b -> p (a b)")
        low, cmask = mats[:, 8, :], mats[:, 9, :]
        inv_freq, rank0 = crow[:, 0:16], crow[:, 16:48].rearrange("p (g e) -> p g e", e=4)

        at = [0]

        def take(n):
            at[0] += n
            assert at[0] <= ARENA, at[0]
            return arena[:, at[0] - n:at[0]]

        gates = take(T * 4 * D).rearrange("p (t n) -> p t n", t=T)
        hidT = gates.rearrange("p t n -> p (t n)").rearrange("p (k s) -> p k s", s=S)
        u_cqkv = take(T * 672)
        cq = u_cqkv[:, 0:T * QL].rearrange("p (t n) -> p t n", t=T)
        ckv = u_cqkv[:, T * QL:T * 672].rearrange("p (t n) -> p t n", t=T)
        y_ssd = u_cqkv[:, 0:T * MIX].rearrange("p (t n) -> p t n", t=T)
        u_up = take(T * MIX)
        up = u_up.rearrange("p (t n) -> p t n", t=T)
        lru_i = u_up.rearrange("p (c s) -> p c s", c=KM)
        z_silu = take(T * MIX).rearrange("p (t n) -> p t n", t=T)
        u_xb = take(KX * (S + 3))
        xbT = u_xb.rearrange("p (c s) -> p c s", c=KX)
        lru_a = u_xb[:, 0:KM * S].rearrange("p (c s) -> p c s", c=KM)
        u_xbS = take(KX * S)
        xbS = u_xbS.rearrange("p (c s) -> p c s", c=KX)
        xdt = u_xbS[:, 0:T * MIX].rearrange("p (t n) -> p t n", t=T)
        lru_g = take(KM * S).rearrange("p (c s) -> p c s", c=KM)
        u_lx = take(KM * (S + 3))
        lxT = u_lx.rearrange("p (c s) -> p c s", c=KM)
        lru_r = u_lx[:, 0:KM * S].rearrange("p (c s) -> p c s", c=KM)
        xcT = take(KM * S).rearrange("p (c s) -> p c s", c=KM)
        ycT = xcT
        u_cT = take(5 * S)
        cT = u_cT.rearrange("p (c s) -> p c s", c=5)
        cbm = u_cT[:, 0:2 * 384].rearrange("p (g s) -> p g s", g=2)
        lru_t = u_cT[:, 0:KM * S].rearrange("p (c s) -> p c s", c=KM)
        u_qk = take(2 * T * MH * QKD)
        q_tok = u_qk[:, 0:T * MH * QKD].rearrange("p (t h d) -> p t h d", t=T, h=MH)
        k_tok = u_qk[:, T * MH * QKD:].rearrange("p (t h d) -> p t h d", t=T, h=MH)
        dm = u_qk.rearrange("p (h s) -> p h s", h=MH)
        u_v = take(T * MIX)
        v_tok = u_v.rearrange("p (t h d) -> p t h d", t=T, h=MH)
        yaT = u_v.rearrange("p (c s) -> p c s", c=KM)
        probs = take(384)
        probsT = take(384)
        o_mla = take(T * MIX).rearrange("p (t n) -> p t n", t=T)
        u_dT = take(KM * S)
        dT = u_dT.rearrange("p (c s) -> p c s", c=KM)
        ybT = dT
        xs_tok = take(T * MIX).rearrange("p (t n) -> p t n", t=T)
        rope_cs = take(2 * T * 16).rearrange("p (a t f) -> p a t f", a=2, t=T)
        rope_tmp = take(4 * T * MH * 16).rearrange("p (a n) -> p a n", a=4)
        qT = x_norm[:, :, :].rearrange("p t n -> p (t n)").rearrange("p (h s) -> p h s", h=MH)
        kT = x_tok[:, :, :].rearrange("p t n -> p (t n)").rearrange("p (h s) -> p h s", h=MH)
        band = ln_gb[:, :, :].rearrange("p a n -> p (a n)")[:, 0:4 * 384].rearrange("p (g s) -> p g s", g=4)
        prow = probs
        dt_tok = stats[:, 0:16].rearrange("p (t h) -> p t h", t=T)
        a_tok = stats[:, 16:32].rearrange("p (t h) -> p t h", t=T)
        acs = stats[:, 32:48].rearrange("p (t h) -> p t h", t=T)
        ms, rstd, neghalf = stats[:, 48:52], stats[:, 52:56], stats[:, 56:60]
        mx = stats[:, 60:62]
        p_tok = o_mla.rearrange("p t n -> p (t n)")[:, 0:T * DE].rearrange("p (t n) -> p t n", t=T)
        pT = o_mla.rearrange("p t n -> p (t n)")[:, T * DE:2 * T * DE].rearrange("p (c s) -> p c s", c=2)
        pos_i = sb("pos_i", [P, T], I32)
        router_w = sb("router_w", [P, KD, NE])
        bn_part = sb("bn_part", [P, T, 2, 6])
        bn_mv = sb("bn_mv", [P, T, 2])
        mx4 = sb("mx4", [P, 4])
        ms_part = sb("ms_part", [P, 2, T])
        minus_mean = sb("minus_mean", [P, 1])
        pos_f = sb("pos_f", [P, T])
        zero16 = sb("zero16", [P, 640], BF16)
        den = sb("den", [P, 8])
        sp_v, sp_a, sp_e = (sb(f"softplus_{n}", [P, 20]) for n in "vae")
        decay8 = sb("decay8", [P, 4])
        a_head = sb("a_head", [P, MH])
        zc_mask = sb("zc_mask", [P, S])

        at[0] = 0
        u_q2 = take(3 * KD * S)
        q2T = u_q2.rearrange("p (g c s) -> p g c s", g=3, c=KD)
        k2T = take(3 * KD * S).rearrange("p (g c s) -> p g c s", g=3, c=KD)
        v2 = take(3 * T * D).rearrange("p (g t n) -> p g t n", g=3, t=T)
        bias_h = take(H2 * S).rearrange("p (h s) -> p h s", h=H2)
        relmask = take(3 * S).rearrange("p (g s) -> p g s", g=3)
        bm = take(2 * 3 * S).rearrange("p (b g s) -> p b g s", b=2, g=3)
        u_e = take(2 * 1152)
        e_dil = u_e.rearrange("p (b n) -> p b n", b=2)
        eT_dil = take(1152)
        eT_two = ((eT_dil[:, 0:384], eT_dil[:, 384:1152]),
                  (pool_w[:, :, :].rearrange("p g n -> p (g n)")[:, 0:384],
                   lru_w[:, :, :, :].rearrange("p i c n -> p (i c n)")[:, 0:768]))
        rel_row = u_e[0:H2, 1152:1536]
        rel_tab = eT_dil[0:32, 0:H2]
        rel_spread = v2.rearrange("p g t n -> p (g t n)")[:, 0:H2 * S].rearrange("p (h s) -> p h s", h=H2)
        onehot = eT_dil[0:32, 16:400]
        SBN = 4
        HIGH = 14400
        sb_sets = tuple(arena[:, HIGH + 3072 * i:HIGH + 3072 * (i + 1)] for i in range(SBN))
        sb_zt, sb_e, sb_l, sb_h = ([u[:, 768 * i:768 * i + 768].rearrange("p (h s) -> p h s", h=2) for u in sb_sets]
                                   for i in range(4))
        at[0] = 0
        half = lambda v: v.bitcast(F16)
        aT_hi, aT_lo = (half(take(KD * S // 2)).rearrange("p (k s) -> p k s", k=KD) for _ in range(2))
        e_silu = take(2 * T * DE).rearrange("p (b t n) -> p b t n", b=2, t=T)
        h_tok = take(2 * T * DE).rearrange("p (b t n) -> p b t n", b=2, t=T)
        hT_hi, hT_lo = (half(take(S * DE // P)).rearrange("p (b n) -> p b n", b=2) for _ in range(2))
        score = take(T * NE)
        r_v, r_rank, r_cmp, r_sel, r_gate = (take(T * NE) for _ in range(5))
        r_gs = take(8)
        r_gr = take(8)
        r_best = take(8)
        r_den = take(4)
        at[0] = HIGH
        w_hi, w_lo = (half(take(3 * SLOT // 2)).rearrange("p (b n) -> p b n", b=3) for _ in range(2))
        rel_dram = nc.dram_tensor("rel_rows_dram", [H2, 384], F32, kind="Internal").ap()
        block = ctx.enter_context(nc.Block())

        EVAC, _n = [], {"A": 0, "D": 0}
        for e in "ADAADDAD" + "A" * 8:
            _n[e] += 1
            EVAC.append((sig("out_by_act" if e == "A" else "out_by_dve"), _n[e]))

        w_in = a["w_in"].rearrange("o (k p) n -> (o p) k n", p=P)

        def landed(eng, n):
            eng.wait_ge(sig(f"w_landed{n % RING}"), 32 * (n // RING + 1))

        def moe_index(n):
            if MOE0 <= n < SBI0:
                return n - MOE0
            return n - MOE1 + 3 * NE // 2 if n >= MOE1 else None

        def staged(i, *stages):
            for stage, behind in stages:
                if 0 <= i - behind < H2 // 2:
                    stage(i - behind)

        def bcast(ap, n, offset=0):
            return bass.AP(tensor=ap.tensor, offset=offset, ap=[[0, P], [1, n]])

        @block.sync
        def _(sp):
            def slot_free(n):
                m = n - RING
                if m >= 0:
                    q = moe_index(m)
                    if q is None:
                        sp.wait_ge(sig("w_used"), m + 1)
                    else:
                        sp.wait_ge(sig("w_lo"), q + 1)

            def slot(n, pairs):
                slot_free(n)
                for o, k, c, src in pairs:
                    sp.dma_start(w_ring[:, n % RING, o:o + k * c].rearrange("p (k n) -> p k n", k=k), src)\
                        .then_inc(sig(f"w_landed{n % RING}"), 16)

            def halves(n, w, c0, c):
                h = KD // 2
                slot(n, [(0, h, c, w[:, 0:h, c0:c0 + c]), (h * c, h, c, w[:, h:KD, c0:c0 + c])])

            def rows4(n, w):
                slot(n, [(0, 2, D, w[:, 0:2, :]), (2 * D, 2, D, w[:, 2:4, :])])

            sp.dma_start(x_norm[:, :, :], a["x"].rearrange("o (t p) d -> (o p) t d", p=P)).then_inc(sig("ld_x"), 16)
            sp.dma_start(mats[:, :, :].rearrange("p a b -> p (a b)"), a["c_mats"]).then_inc(sig("ld_mats"), 16)
            halves(0, w_in, C_Q, 384)
            for name, n in PARAM_ROWS:
                v = a[name]
                flat = bass.AP(tensor=v.tensor, offset=0, ap=[[P, n], [1, P]])
                sp.dma_start(prow[PROW[name]:PROW[name] + n, 0:P], flat).then_inc(sig("ld_params"), 16)
            for i, (name, layer) in enumerate(LN_ROWS):
                flat = bass.AP(tensor=a[name].tensor, offset=layer * D, ap=[[P, 8], [1, P]])
                sp.dma_start(prow[8 * i:8 * i + 8, P:2 * P], flat).then_inc(sig("ld_params"), 16)
            sp.dma_start(crow[:, :], a["c_rows"]).then_inc(sig("ld_rows"), 16)
            for i, (name, n) in enumerate((("ssd_dt_bias", 8), ("ssd_a_log", 8), ("ssd_d", 8), ("router_b_2", NE))):
                sp.dma_start(brow[:, 8 * i:8 * i + n], bcast(a[name], n)).then_inc(sig("ld_rows"), 16)
            sp.dma_start(pos_i[:, :], a["positions"]).then_inc(sig("ld_rows"), 16)
            halves(1, w_in, C_KV, 288)
            halves(2, w_in, C_POOL, 512)
            sp.dma_start(band, a["c_band"].rearrange("p (g s) -> p g s", g=4)).then_inc(sig("ld_pool"), 16)
            sp.dma_start(pool_w[:, :, :], a["w_pool"].rearrange("o g c d -> (o c) g d")).then_inc(sig("ld_pool"), 16)
            sp.wait_ge(sig("lru_zeroed"), 1)
            for i, name in enumerate(("lru_w_a", "lru_w_i")):
                w = a[name].rearrange("o (c b) i j -> (o b) i c j", b=2)
                for b in range(2):
                    sp.dma_start(lru_w[64 * b:64 * b + 64, i, :, 64 * b:64 * b + 64], w[b])\
                        .then_inc(sig("ld_lru"), 16)
            halves(3, w_in, C_Z, 512)
            halves(4, w_in, C_XBC, 384)
            w = a["w_uq"].rearrange("o (k p) n -> (o p) k n", p=P)
            slot(5, [(0, 2, 768, w[:, 0:2, :]), (1536, 1, 768, w[:, 2:3, :])])
            halves(6, w_in, C_XBC + 384, 392)
            w = a["w_ukv"].rearrange("o (k p) n -> (o p) k n", p=P)
            slot(7, [(0, 1, D, w[:, 0:1, :]), (D, 1, D, w[:, 1:2, :])])
            halves(8, w_in, C_LG, 512)
            halves(9, w_in, C_LX, 512)
            for i in range(8):
                halves(10 + i, w_in, C_GATE + 512 * i, 512)
            for i, b in enumerate((1, 0, 3, 2)):
                rows4(18 + i, a["w_branch"][0, b].rearrange("(k p) n -> p k n", p=P))
            sp.wait_ge(sig("mla_scores"), MH)
            sp.dma_start(x_tok[:, :, :], a["x"].rearrange("o (t p) d -> (o p) t d", p=P)).then_inc(sig("ld_x"), 16)
            sp.wait_ge(sig("pool_d"), 1)
            sp.dma_start(ln_gb[:, 0, :], bcast(a["g_final"], D)).then_inc(sig("ld_gb"), 16)
            w = a["w_out"].rearrange("o (k p) n -> (o p) k n", p=P)
            halves(22, w, 0, 512)
            halves(23, w, 512, 512)
            sp.wait_ge(sig("mla_oT_pe"), KM)
            sp.dma_start(p_tok, a["p"].rearrange("l o (t p) d -> (l o p) t d", p=P)).then_inc(sig("ld_p"), 16)
            w = a["w_ff1"].rearrange("o (k p) n -> (o p) k n", p=P)
            for i in range(8):
                halves(24 + i, w, 512 * i, 512)
            sp.wait_ge(sig("branch"), 4)
            sp.dma_start(relmask, a["c_relmask"].rearrange("p (g s) -> p g s", g=3)).then_inc(sig("ld_rel"), 16)
            sp.dma_start(rel_tab, a["rel_table_2"]).then_inc(sig("ld_rel"), 16)
            sp.dma_start(onehot, a["c_onehot"]).then_inc(sig("ld_rel"), 16)
            sp.dma_start(router_w[:, :, :], a["router_w_2"].rearrange("(k p) e -> p k e", p=P)).then_inc(sig("ld_router"), 16)
            for i in range(8):
                rows4(32 + i, a["w_ff2"][0, 512 * i:512 * i + 512, :].rearrange("(k p) n -> p k n", p=P))
            sp.wait_ge(sig("rel_row"), 1)
            sp.dma_start(rel_dram, rel_row).then_inc(sig("st_rel"), 16)
            sp.wait_ge(sig("st_rel"), 16)
            spread = bass.AP(tensor=rel_dram.tensor, offset=0, ap=[[1, P], [384, H2], [1, S]])
            sp.dma_start(rel_spread, spread).then_inc(sig("ld_spread"), 16)

            w = a["w_ple"].rearrange("o (k p) n -> (o p) k n", p=P)
            slot(40, [(0, 1, D, w[:, 0:1, :]), (D, 1, D, w[:, 1:2, :])])
            w = a["w_ple_gate"].rearrange("o (k p) n -> (o p) k n", p=P)
            halves(41, w, 0, 512)
            halves(42, w, 512, 512)
            def slot_g(n, pairs):
                for dst, src in pairs:
                    sp.dma_start(dst, src).then_inc(sig(f"w_landed{n % RING}"), 16)

            w = a["dil_w_in_2"].rearrange("o (k p) n -> (o p) k n", p=P)
            with sp.Fori(0, 3) as g:
                for s in range(6):
                    dst = w_ring[:, (DIL0 + s) % RING, :].rearrange("p (k n) -> p k n", k=KD)
                    sp.wait_ge(sig("w_used"), DIL0 + s - RING + 1 + g * 6)
                    slot_g(DIL0 + s, [(dst[:, kk:kk + 4, :], w[:, kk:kk + 4, bass.ds(g * 3 * D + 512 * s, 512)])
                                      for kk in (0, 4)])

            def gb(m):
                layer, name = m // 2, ("ln1", "ln2")[m % 2]
                sp.wait_ge(sig("x_full"), m + 1)
                sp.dma_start(ln_gb[:, 0, :], bcast(a[name + "_g_2"], D, layer * D)).then_inc(sig("ld_gb"), 16)
                sp.dma_start(ln_gb[:, 1, :], bcast(a[name + "_b_2"], D, layer * D)).then_inc(sig("ld_gb"), 16)

            def experts(layer, n0):
                wg = a["exp_w_gate_2"][layer].rearrange("e (k p) n -> p e k n", p=P)
                wu = a["exp_w_up_2"][layer].rearrange("e (k p) n -> p e k n", p=P)
                wd = a["exp_w_down_2"][layer].rearrange("e (k p) n -> p e k n", p=P)

                def pair(j):
                    for b in range(3):
                        n = n0 + b
                        if isinstance(j, int):
                            slot_free(n)
                        else:
                            sp.wait_ge(sig("w_lo"), moe_index(n0) + b - 2 + j * 3)
                        if b < 2:
                            dst = w_ring[:, n % RING, :].rearrange("p (o k n) -> p o k n", o=1, k=KD)
                            slot_g(n, [(dst[:, :, :, 0:DE], wg[:, bass.ds(2 * j + b, 1), :, :]),
                                       (dst[:, :, :, DE:2 * DE], wu[:, bass.ds(2 * j + b, 1), :, :])])
                        else:
                            dst = w_ring[:, n % RING, :].rearrange("p (o k n) -> p o k n", o=2, k=2)
                            slot_g(n, [(dst[:, i:i + 1, :, :], wd[:, bass.ds(2 * j + i, 1), :, :]) for i in range(2)])

                pair(0)
                with sp.Fori(1, NE // 2) as j:
                    pair(j)

            gb(0)
            w = a["dil_w_out_2"].rearrange("o (k p) n -> (o p) k n", p=P)
            halves(DOUT0, w, 0, 512)
            halves(DOUT0 + 1, w, 512, 512)
            experts(0, MOE0)
            gb(1)
            w = a["sb_w_in_2"].rearrange("o (k p) n -> (o p) k n", p=P)
            for s in range(6):
                halves(SBI0 + s, w, 512 * s, 512)
            gb(2)
            w = a["sb_w_out_2"].rearrange("o (k p) n -> (o p) k n", p=P)
            halves(SBO0, w, 0, 512)
            halves(SBO0 + 1, w, 512, 512)
            experts(1, MOE1)
            gb(3)
            for t in range(T):
                sp.wait_ge(sig("out_ready"), t + 1)
                sp.dma_start(out[0, t * P:(t + 1) * P, :], x_tok[:, t, :]).then_inc(sig("stored"), 16)
            sp.wait_ge(sig("stored"), 16 * T)

        @block.gpsimd
        def _(pool):
            pool.memset(neghalf, -0.5)
            pool.memset(zero16[:, :], 0.0)
            pool.memset(lru_w[:, :, :, :], 0.0)
            pool.drain()
            pool.memset(xbT[:, :, 0:CONV - 1], 0.0)
            pool.memset(lxT[:, :, 0:CONV - 1], 0.0).then_inc(sig("lru_zeroed"), 1)

            def rsqrt(i, n):
                pool.wait_ge(sig("ms_ready"), i + 1)
                pool.tensor_tensor(rstd[:, 0:n], ms[:, 0:n], neghalf[:, 0:n], ALU.pow).then_inc(sig("rstd_ready"), 1)

            rsqrt(0, 2)
            rsqrt(1, 4)
            for i in range(2, 6):
                rsqrt(i, 2)

            def full(norm, bias):
                pool.wait_ge(sig("xn0_ready"), norm)
                pool.wait_ge(sig("xn1_ready"), norm)
                for t in range(T):
                    ins = pool.tensor_tensor(x_tok[:, t, :], x_norm[:, t, :], ln_gb[:, 0, :], ALU.mult)
                if bias:
                    pool.drain()
                    for t in range(T):
                        ins = pool.tensor_tensor(x_tok[:, t, :], x_tok[:, t, :], ln_gb[:, 1, :], ALU.add)
                ins.then_inc(sig("x_full"), 1)

            pool.wait_ge(sig("ld_gb"), 16)
            full(5, False)
            pool.wait_ge(sig("bias_h"), 2)
            pool.wait_ge(sig("ld_rel"), 16 * 3)
            for h in range(H2):
                if h >= 2:
                    pool.wait_ge(sig("dil_max"), h - 1)
                pool.tensor_tensor(bm[:, h % 2, :, :], relmask, bias_h[:, h:h + 1, :].broadcast_to([P, 3, S]), ALU.add)\
                    .then_inc(sig("bm"), 1)
            for m in range(4):
                rsqrt(6 + m, 2)
                if m < 3:
                    pool.wait_ge(sig("ld_gb"), 16 + 32 * (m + 1))
                    full((7, 8, 10)[m], True)

        def pcols(name, i):
            c = PROW[name] + i
            return pcol[:, c:c + 1]

        @block.tensor
        def _(pe):
            def w_slot(n, k):
                return w_ring[:, n % RING, :].rearrange("p (k n) -> p k n", k=k) if k else w_ring[:, n % RING, :]

            def transposes(i, src, chunks, sem_name, first_bank=4):
                for k in range(chunks):
                    for t in range(T):
                        o = (k % 2) * 256 + t * P
                        ins = pe.transpose(ps[:, first_bank + k // 2, o:o + P], src[:, t, k * P:(k + 1) * P], ident)
                    ins.then_inc(sig(sem_name), 1)

            def act_transposes(i):
                if i:
                    pe.wait_ge(sig("xp_act"), 4 * i)
                    pe.wait_ge(sig("xp_dve"), 4 * i)
                for t in range(T):
                    pe.wait_ge(sig(f"xn{t}_ready"), i + 1)
                    for k in range(KD):
                        o = (k % 2) * 256 + t * P
                        ins = pe.transpose(ps[:, 4 + k // 2, o:o + P], x_norm[:, t, k * P:(k + 1) * P], ident)
                        if t == T - 1:
                            ins.then_inc(sig("xp_pe"), 1)

            def act_ready(i):
                pe.wait_ge(sig("xp_act"), 4 * i + 4)
                pe.wait_ge(sig("xp_dve"), 4 * i + 4)

            def gemm_tok(n, bank, cols):
                landed(pe, n)
                w = w_ring[:, n % RING, 0:KD * cols].rearrange("p (k n) -> p k n", k=KD)
                for t in range(T):
                    for k in range(KD):
                        ins = pe.matmul(ps[:, bank + t, 0:cols], actT[:, k, t * P:(t + 1) * P], w[:, k, :],
                                        start=(k == 0), stop=(k == KD - 1))
                return ins

            def gemm_T(n, bank, cols, chunks):
                landed(pe, n)
                w = w_ring[:, n % RING, 0:KD * cols].rearrange("p (k n) -> p k n", k=KD)
                for c in range(chunks):
                    o = (c % 2) * S
                    for k in range(KD):
                        ins = pe.matmul(ps[:, bank + c // 2, o:o + S], w[:, k, c * P:(c + 1) * P], actT[:, k, :],
                                        start=(k == 0), stop=(k == KD - 1))
                return ins

            def evacuated(g):
                if g >= 2:
                    pe.wait_ge(*EVAC[g - 2])

            pe.wait_ge(sig("ld_mats"), 16)
            pe.wait_ge(sig("ld_params"), 16 * (len(PARAM_ROWS) + len(LN_ROWS)))
            pe.transpose(ps[:, 0, NPROW:NCOL], prow[0:NCOL - NPROW, P:2 * P], ident[0:NCOL - NPROW, 0:NCOL - NPROW])
            pe.transpose(ps[:, 0, 0:NPROW], prow[0:NPROW, 0:P], ident[0:NPROW, 0:NPROW]).then_inc(sig("params_T"), 1)
            act_transposes(0)
            act_ready(0)
            pe.wait_ge(sig("pcol"), 1)
            g = 0
            for n, cols in ((0, 384), (1, 288), (2, 512), (3, 512)):
                evacuated(g)
                gemm_tok(n, (g % 2) * 2, cols).then_inc(sig("w_used"), 1)
                g += 1
            pe.wait_ge(sig("ld_pool"), 32)
            pe.wait_ge(*EVAC[2])
            for c in range(KM):
                o = (c % 2) * S
                pe.matmul(ps[:, 4 + c // 2, o:o + S], up[:, 0, c * P:(c + 1) * P], band[:, c, 0:S],
                          start=True, stop=False, skip_group_check=True)
                ins = pe.matmul(ps[:, 4 + c // 2, o + P:o + S], up[:, 1, c * P:(c + 1) * P], band[:, c, S:384],
                                start=False, stop=True, skip_group_check=True)
            ins.then_inc(sig("pool_d"), 1)
            evacuated(g)
            gemm_T(4, (g % 2) * 2, 384, 3).then_inc(sig("w_used"), 1)
            g += 1
            pe.wait_ge(sig("dT"), 1)
            pe.wait_ge(sig("mla_normed"), 1)
            for k in range(5):
                src, kk = (cq, k) if k < 3 else (ckv, k - 3)
                for t in range(T):
                    o = (k % 2) * S + t * P
                    ins = pe.transpose(ps[:, 4 + k // 2, o:o + P], src[:, t, kk * P:(kk + 1) * P], ident)
            ins.then_inc(sig("cT_pe"), 1)
            landed(pe, 5)
            pe.wait_ge(sig("cT"), 1)
            w = w_ring[:, 5 % RING, 0:3 * 768].rearrange("p (k n) -> p k n", k=3)
            for t in range(T):
                for h in range(2):
                    for k in range(3):
                        ins = pe.matmul(ps[:, 4 + 2 * t + h, 0:384], cT[:, k, t * P:(t + 1) * P],
                                        w[:, k, h * 384:(h + 1) * 384], start=(k == 0), stop=(k == 2))
            ins.then_inc(sig("w_used"), 1)
            evacuated(g)
            gemm_T(6, (g % 2) * 2, 392, 3)
            w = w_ring[:, 6 % RING, 0:KD * 392].rearrange("p (k n) -> p k n", k=KD)
            for t in range(T):
                for k in range(KD):
                    ins = pe.matmul(ps[:, (g % 2) * 2 + 1, S + 8 * t:S + 8 * t + 8], actT[:, k, t * P:(t + 1) * P],
                                    w[:, k, 384:392], start=(k == 0), stop=(k == KD - 1))
            ins.then_inc(sig("w_used"), 1)
            g += 1
            landed(pe, 7)
            pe.wait_ge(sig("q_out"), 1)
            w = w_ring[:, 7 % RING, 0:2 * D].rearrange("p (k n) -> p k n", k=2)
            for t in range(T):
                for h in range(2):
                    for k in range(2):
                        ins = pe.matmul(ps[:, 4 + 2 * t + h, :], cT[:, 3 + k, t * P:(t + 1) * P],
                                        w[:, k, h * 512:(h + 1) * 512], start=(k == 0), stop=(k == 1))
            ins.then_inc(sig("w_used"), 1)
            evacuated(g)
            gemm_T(8, (g % 2) * 2, 512, 4).then_inc(sig("w_used"), 1)
            g += 1

            def head_turns(src, done):
                for h in range(MH):
                    for t in range(T):
                        o = (h % 2) * S + t * P
                        ins = pe.transpose(ps[0:QKD, 4 + h // 2, o:o + P], src[:, t, h, :], ident)
                ins.then_inc(sig(done), 1)

            pe.wait_ge(sig("q_roped"), 1)
            pe.wait_ge(sig("kv_out"), 1)
            head_turns(q_tok, "qT_pe")
            evacuated(g)
            gemm_T(9, (g % 2) * 2, 512, 4).then_inc(sig("w_used"), 1)
            g += 1
            pe.wait_ge(sig("k_roped"), 1)
            pe.wait_ge(sig("qT"), 1)
            head_turns(k_tok, "kT_pe")

            def mla_score(h):
                if h == 0:
                    pe.wait_ge(sig("kT"), 1)
                else:
                    pe.wait_ge(sig("mla_max"), h)
                pe.matmul(ps[:, 4, 0:P], qT[0:QKD, h, 0:P], kT[0:QKD, h, 0:P], start=True, stop=True)
                pe.matmul(ps[:, 4, P:384], qT[0:QKD, h, P:S], kT[0:QKD, h, :], start=True, stop=True)\
                    .then_inc(sig("mla_scores"), 1)

            def mla_out(h):
                pe.wait_ge(sig("mla_exp"), h + 1)
                if h == 0:
                    pe.wait_ge(sig("kT"), 1)
                else:
                    pe.wait_ge(sig("mla_o"), h)
                for j in range(3):
                    ins = pe.transpose(ps[:, 5, j * P:(j + 1) * P], probs[:, j * P:(j + 1) * P], ident)
                ins.then_inc(sig("mla_pT_pe"), 1)
                pe.wait_ge(sig("mla_pT"), h + 1)
                pe.matmul(ps[:, 5, 384:448], probsT[:, 0:P], v_tok[:, 0, h, :], start=True, stop=True)
                pe.matmul(ps[:, 5, 448:512], probsT[:, P:2 * P], v_tok[:, 0, h, :], start=True, stop=False)
                pe.matmul(ps[:, 5, 448:512], probsT[:, 2 * P:3 * P], v_tok[:, 1, h, :], start=False, stop=True)\
                    .then_inc(sig("mla_pv"), 1)

            def ssd_cb():
                pe.wait_ge(sig("xbS"), 1)
                pe.wait_ge(sig("kT"), 1)
                for gr in range(2):
                    r = slice(64 * gr, 64 * gr + 64)
                    pe.matmul(ps[:, 6 + gr, 0:S], xbS[r, 4, 0:P], xbS[r, 5, :], start=True, stop=True)
                    ins = pe.matmul(ps[:, 6 + gr, S:384], xbS[r, 4, P:S], xbS[r, 5, P:S], start=True, stop=True)
                ins.then_inc(sig("cb_pe"), 1)

            def ssd_xs():
                pe.wait_ge(sig("cbm"), 1)
                for t in range(T):
                    for c in range(KM):
                        ins = pe.transpose(ps[:, 6 + t, c * P:(c + 1) * P], xbS[:, c, t * P:(t + 1) * P], ident)
                ins.then_inc(sig("xs_pe"), 1)

            def ssd_cumsum(half):
                if half == 0:
                    pe.wait_ge(sig("acs"), 1)
                else:
                    pe.wait_ge(sig("dm"), 1)
                for j in range(4):
                    h = 4 * half + j
                    o = (j % 2) * S
                    b = 6 + j // 2
                    pe.matmul(ps[:, b, o:o + S], a_tok[:, 0, h:h + 1].broadcast_to([P, P]), tri3[:, 0:S],
                              start=True, stop=False, skip_group_check=True)
                    ins = pe.matmul(ps[:, b, o + P:o + S], a_tok[:, 1, h:h + 1].broadcast_to([P, P]), tri,
                                    start=False, stop=True, skip_group_check=True)
                ins.then_inc(sig("cum_pe"), 1)

            def ssd_cumcol():
                pe.wait_ge(sig("a_tok"), 1)
                pe.wait_ge(sig("xs_tok"), 1)
                pe.matmul(ps[:, 6, 0:8], tri, a_tok[:, 0, :], start=True, stop=True)
                pe.matmul(ps[:, 6, 8:16], ones, a_tok[:, 0, :], start=True, stop=False)
                pe.matmul(ps[:, 6, 8:16], tri, a_tok[:, 1, :], start=False, stop=True).then_inc(sig("acs_pe"), 1)

            def lru_gate(i):
                pe.wait_ge(sig("ld_lru"), 64)
                pe.wait_ge(sig("xcT"), 1)
                if i == 0:
                    pe.wait_ge(sig("dm"), 2)
                else:
                    pe.wait_ge(sig("lru_r"), 1)
                for c in range(KM):
                    o = (c % 2) * S
                    ins = pe.matmul(ps[:, 6 + c // 2, o:o + S], lru_w[:, i, c, :], xcT[:, c, :], start=True, stop=True)
                ins.then_inc(sig("lru_pe"), 1)

            def ssd_y():
                pe.wait_ge(sig("lru_i"), 1)
                pe.wait_ge(sig("dm_cb"), 1)
                pe.wait_ge(sig("xdt"), 1)
                for h in range(MH):
                    c = slice(64 * h, 64 * h + 64)
                    pe.matmul(ps[:, 6, c], dm[:, h, 0:P], xdt[:, 0, c], start=True, stop=True)
                    pe.matmul(ps[:, 7, c], dm[:, h, P:S], xdt[:, 0, c], start=True, stop=False)
                    ins = pe.matmul(ps[:, 7, c], dm[:, h, S:384], xdt[:, 1, c], start=False, stop=True)
                ins.then_inc(sig("ssd_y_pe"), 1)

            def pool_y():
                pe.wait_ge(sig("ssd_y"), 1)
                for c in range(KM):
                    o = (c % 2) * S
                    ins = pe.matmul(ps[:, 6 + c // 2, o:o + S], pool_w[:, c, :], dT[:, c, :], start=True, stop=True)
                ins.then_inc(sig("pool_y"), 1)

            def ssd_turn():
                pe.wait_ge(sig("ybT"), 1)
                pe.wait_ge(sig("ssd_normed"), 1)
                transposes(0, y_ssd, KM, "ycT_pe", 6)

            extra = {0: [ssd_cb], 1: [ssd_xs, ssd_cumcol], 2: [lambda: ssd_cumsum(0)], 3: [lambda: ssd_cumsum(1)],
                     4: [lambda: lru_gate(0)], 5: [lambda: lru_gate(1), ssd_y], 6: [pool_y], 7: [ssd_turn]}
            for i in range(8):
                evacuated(g)
                gemm_tok(10 + i, (g % 2) * 2, 512).then_inc(sig("w_used"), 1)
                g += 1
                mla_score(i)
                if i:
                    mla_out(i - 1)
                for f in extra[i]:
                    f()
            mla_out(MH - 1)
            pe.wait_ge(sig("mla_o"), MH)
            transposes(0, o_mla, KM, "mla_oT_pe", 4)
            for i, (b, yT) in enumerate(((1, ybT), (0, yaT), (3, lru_g), (2, ycT))):
                n = 18 + i
                landed(pe, n)
                pe.wait_ge(sig(("ybT", "yaT", "ydT", "ycT")[i]), 1)
                if i == 0:
                    pe.wait_ge(*EVAC[15])
                    pe.wait_ge(*EVAC[14])
                elif i == 1:
                    pe.wait_ge(sig("ycT"), 1)
                else:
                    pe.wait_ge(sig("branch"), i - 1)
                w = w_ring[:, n % RING, :].rearrange("p (k n) -> p k n", k=KM)
                for t in range(T):
                    for h in range(2):
                        for k in range(KM):
                            ins = pe.matmul(ps[:, 4 * (i % 2) + 2 * t + h, :], yT[:, k, t * P:(t + 1) * P],
                                            w[:, k, h * 512:(h + 1) * 512], start=(k == 0), stop=(k == KM - 1))
                ins.then_inc(sig("w_used"), 1)
            pe.wait_ge(sig("branch"), 4)
            act_transposes(1)
            act_ready(1)
            gemm_tok(22, 0, 512).then_inc(sig("w_used"), 1)
            gemm_tok(23, 2, 512).then_inc(sig("w_used"), 1)
            act_transposes(2)
            act_ready(2)
            for i in range(8):
                if i >= 2:
                    pe.wait_ge(sig("ff1_relu"), i - 1)
                elif i == 0:
                    pe.wait_ge(sig("x_res"), 1)
                gemm_T(24 + i, (i % 2) * 2, 512, 4).then_inc(sig("w_used"), 1)
            pe.wait_ge(sig("ld_rel"), 48)
            pe.matmul(ps[0:H2, 5, 0:384], rel_tab, onehot, start=True, stop=True).then_inc(sig("rel_pe"), 1)
            pe.wait_ge(sig("ld_p"), 16)
            transposes(0, p_tok, 2, "pT_pe", 4)
            pe.wait_ge(sig("ff1_square"), 8)
            for i in range(8):
                landed(pe, 32 + i)
                w = w_ring[:, (32 + i) % RING, :].rearrange("p (k n) -> p k n", k=KM)
                for t in range(T):
                    for h in range(2):
                        for k in range(KM):
                            kk = KM * i + k
                            ins = pe.matmul(ps[:, 2 * t + h, :], hidT[:, kk, t * P:(t + 1) * P],
                                            w[:, k, h * 512:(h + 1) * 512], start=(kk == 0), stop=(kk == 31),
                                            skip_group_check=True)
                    if i == 7 and t == 0:
                        ins.then_inc(sig("ff2_first"), 1)
                ins.then_inc(sig("w_used"), 1)
            pe.wait_ge(sig("ld_spread"), 16)
            pe.wait_ge(sig("pT"), 1)
            pe.wait_ge(sig("rel_row"), 1)
            for i in range(8):
                if i == 4:
                    pe.wait_ge(sig("bias_h"), 1)
                ins = pe.matmul(ps[:, 4 + i % 4, :], flip, rel_spread[:, 2 * i:2 * i + 2, :], start=True, stop=True)
                if i % 4 == 3:
                    ins.then_inc(sig("flip_pe"), 1)
            pe.wait_ge(sig("x_res"), 2)
            pe.wait_ge(sig("pT"), 1)
            landed(pe, 40)
            w = w_ring[:, 40 % RING, 0:2 * D].rearrange("p (k n) -> p k n", k=2)
            for t in range(T):
                for h in range(2):
                    for k in range(2):
                        ins = pe.matmul(ps[:, 2 * t + h, :], pT[:, k, t * P:(t + 1) * P],
                                        w[:, k, h * 512:(h + 1) * 512], start=(k == 0), stop=(k == 1))
            ins.then_inc(sig("w_used"), 1)
            pe.wait_ge(sig("bias_h"), 2)
            act_transposes(3)
            act_ready(3)
            for i in range(2):
                gemm_tok(41 + i, 4 + 2 * i, 512).then_inc(sig("w_used"), 1)

            def qkv(n0, g, base):
                for s in range(6):
                    n = n0 + s
                    pe.wait_ge(sig(f"w_landed{n % RING}"), 32 * (n // RING + 1) + g * 64)
                    if s >= 2:
                        pe.wait_ge(sig("qkv_act" if s % 2 == 0 else "qkv_dve"), base + s // 2 + g * 3)
                    w = w_ring[:, n % RING, :].rearrange("p (k n) -> p k n", k=KD)
                    for c in range(4 if s < 4 else T):
                        for k in range(KD):
                            if s < 4:
                                o = (c % 2) * S
                                ins = pe.matmul(ps[:, (s % 2) * 2 + c // 2, o:o + S], w[:, k, c * P:(c + 1) * P],
                                                actT[:, k, :], start=(k == 0), stop=(k == KD - 1))
                            else:
                                ins = pe.matmul(ps[:, (s % 2) * 2 + c, :], actT[:, k, c * P:(c + 1) * P], w[:, k, :],
                                                start=(k == 0), stop=(k == KD - 1))
                    ins.then_inc(sig("w_used"), 1)
                pe.wait_ge(sig("qkv_act"), base + 3 + g * 3)
                pe.wait_ge(sig("qkv_dve"), base + 3 + g * 3)

            act_transposes(4)
            act_ready(4)
            with pe.Fori(0, 3) as g:
                qkv(DIL0, g, 0)

            def dil_scores(h):
                if h:
                    pe.wait_ge(sig("dil_max"), h)
                c, r = h // 2, slice(64 * (h % 2), 64 * (h % 2) + 64)
                for g in range(3):
                    pe.matmul(ps[:, 0, g * P:(g + 1) * P], q2T[r, g, c, 0:P], k2T[r, g, c, 0:P], start=True, stop=True)
                for g in range(3):
                    o = (g % 2) * S
                    ins = pe.matmul(ps[:, 1 + g // 2, o:o + S], q2T[r, g, c, P:S], k2T[r, g, c, :], start=True, stop=True)
                ins.then_inc(sig("dil_scores"), 1)

            def dil_turn(h):
                pe.wait_ge(sig("dil_exp"), h + 1)
                if h == 0:
                    pe.wait_ge(sig("xp_act"), 20)
                else:
                    pe.wait_ge(sig("dil_pT_act"), h)
                    pe.wait_ge(sig("dil_pT_dve"), h)
                for j in range(9):
                    b, o = (3, j * P) if j < 3 else (4 + (j - 3) // 4, ((j - 3) % 4) * P)
                    ins = pe.transpose(ps[:, b, o:o + P], e_dil[:, h % 2, j * P:(j + 1) * P], ident)
                ins.then_inc(sig("dil_pT_pe"), 1)

            def dil_out(h):
                eT0, eT1 = eT_two[h % 2]
                pe.wait_ge(sig("dil_pT_act"), h + 1)
                pe.wait_ge(sig("dil_pT_dve"), h + 1)
                if h >= 2:
                    pe.wait_ge(sig("dil_o"), h - 1)
                cols = slice(64 * h, 64 * h + 64)
                for g in range(3):
                    pe.matmul(ps[:, 6 + h % 2, 0:64], eT0[:, g * P:(g + 1) * P], v2[:, g, 0, cols],
                              start=(g == 0), stop=(g == 2))
                for g in range(3):
                    for kt in range(2):
                        o = g * S + kt * P
                        ins = pe.matmul(ps[:, 6 + h % 2, 64:128], eT1[:, o:o + P], v2[:, g, kt, cols],
                                        start=(g + kt == 0), stop=(g + kt == 3))
                ins.then_inc(sig("dil_pv"), 1)

            dil_scores(0)
            for h in range(H2):
                if h + 1 < H2:
                    dil_scores(h + 1)
                dil_turn(h)
                if h:
                    dil_out(h - 1)
            dil_out(H2 - 1)
            act_transposes(5)
            act_ready(5)
            gemm_tok(DOUT0, 0, 512).then_inc(sig("w_used"), 1)
            gemm_tok(DOUT0 + 1, 2, 512).then_inc(sig("w_used"), 1)

            def experts(layer, n0, turn):
                q0 = moe_index(n0)
                act_transposes(turn)
                act_ready(turn)
                pe.wait_ge(sig("ld_router"), 16)
                for t in range(T):
                    for k in range(KD):
                        ins = pe.matmul(ps[:, 0, t * NE:(t + 1) * NE], actT[:, k, t * P:(t + 1) * P], router_w[:, k, :],
                                        start=(k == 0), stop=(k == KD - 1))
                ins.then_inc(sig("logits"), 1)

                def gate_up(b, t):
                    w_h, w_l = (v[:, (n0 + b) % 3, :].rearrange("p (k n) -> p k n", k=KD) for v in (w_hi, w_lo))
                    for k in range(KD):
                        c = slice(t * P, (t + 1) * P)
                        for i, (u, v) in enumerate(((aT_hi, w_h), (aT_hi, w_l), (aT_lo, w_h))):
                            ins = pe.matmul(ps[:, 4 + 2 * b + t, :], u[:, k, c], v[:, k, :],
                                            start=(k + i == 0), stop=(k == KD - 1 and i == 2))
                    return ins

                def turn_h(b, j):
                    pe.wait_ge(sig("moe_h"), NE * layer + 1 + b + j * 2)
                    for f in range(2):
                        for t in range(T):
                            o = f * S + t * P
                            ins = pe.transpose(ps[:, 4 + 2 * b, o:o + P], h_tok[:, b, t, f * P:(f + 1) * P], ident)
                    ins.then_inc(sig("moe_hT_pe"), 1)

                def down(b, j, last=False):
                    pe.wait_ge(sig("moe_hT"), NE * layer + 1 + b + j * 2)
                    o = b * 2048
                    w_h, w_l = (v[:, (n0 + 2) % 3, o:o + 2048].rearrange("p (k n) -> p k n", k=2) for v in (w_hi, w_lo))
                    for t in range(T):
                        for f in range(2):
                            c = slice(f * S + t * P, f * S + (t + 1) * P)
                            for u, v in ((hT_hi, w_h), (hT_hi, w_l), (hT_lo, w_h)):
                                for h in range(2):
                                    ins = pe.matmul(ps[:, 2 * t + h, :], u[:, b, c], v[:, f, h * 512:(h + 1) * 512],
                                                    start=False, stop=(last and f == 1 and u is hT_lo),
                                                    skip_group_check=True)
                        if last and t == 0:
                            ins.then_inc(sig("moe_first"), 1)
                    return ins

                def pair(j, last):
                    gate_up(0, 1).then_inc(sig("w_used"), 1)
                    pe.wait_ge(sig("w_lo"), q0 + 2 + j * 3)
                    gate_up(1, 0)
                    turn_h(0, j)
                    gate_up(1, 1).then_inc(sig("w_used"), 1)
                    pe.wait_ge(sig("w_lo"), q0 + 3 + j * 3)
                    down(0, j)
                    turn_h(1, j)
                    if not last:
                        pe.wait_ge(sig("w_lo"), q0 + 4 + j * 3)
                        gate_up(0, 0)
                    down(1, j, last).then_inc(sig("w_used"), 1)

                pe.wait_ge(sig("w_lo"), q0 + 1)
                pe.wait_ge(sig("aT_lo"), 2 * layer + 1)
                gate_up(0, 0)
                pe.wait_ge(sig("router_exp"), layer + 1)
                for b in range(4):
                    pe.matmul(ps[:, b, :], zero16[:, 0:P], zero16[:, P:640], start=True, stop=False,
                              skip_group_check=True)
                pe.wait_ge(sig("aT_lo"), 2 * layer + 2)
                with pe.Fori(0, NE // 2 - 1) as j:
                    pair(j, False)
                pair(NE // 2 - 1, True)

            experts(0, MOE0, 6)
            act_transposes(7)
            act_ready(7)
            qkv(SBI0, 0, 9)

            def sb_z(m):
                if m >= 2:
                    pe.wait_ge(sig("sb_zc"), m - 1)
                for j in range(2):
                    r, b = slice(64 * j, 64 * j + 64), 2 * (m % 2) + j
                    pe.matmul(ps[:, b, 0:S], k2T[r, 0, m, 0:P], q2T[r, 0, m, :], start=True, stop=True)
                    ins = pe.matmul(ps[:, b, S:384], k2T[r, 0, m, P:S], q2T[r, 0, m, P:S], start=True, stop=True)
                ins.then_inc(sig("sb_z"), 1)

            def sb_r(m):
                pe.wait_ge(sig("sb_sp"), m + 1)
                if m:
                    pe.wait_ge(sig("sb_d"), m)
                for j in range(2):
                    pe.matmul(ps[:, 4 + j, 0:384], low, sb_l[m % SBN][:, j, :], start=True, stop=False,
                              skip_group_check=True)
                    ins = pe.matmul(ps[:, 4 + j, P:S], ones, sb_l[m % SBN][:, j, S:384], start=False, stop=True,
                                    skip_group_check=True)
                ins.then_inc(sig("sb_r"), 1)

            def sb_pv(m):
                pe.wait_ge(sig("sb_att"), m + 1)
                if m >= 2:
                    pe.wait_ge(sig("sb_o"), m - 1)
                for j in range(2):
                    att, cols = sb_e[m % SBN][:, j, :], slice(64 * (2 * m + j), 64 * (2 * m + j) + 64)
                    pe.matmul(ps[:, 6 + m % 2, j * 64:j * 64 + 64], att[:, 0:P], v2[:, 0, 0, cols], start=True, stop=True)
                    o = 128 + j * 64
                    pe.matmul(ps[:, 6 + m % 2, o:o + 64], att[:, P:S], v2[:, 0, 0, cols], start=True, stop=False)
                    ins = pe.matmul(ps[:, 6 + m % 2, o:o + 64], att[:, S:384], v2[:, 0, 1, cols], start=False, stop=True)
                ins.then_inc(sig("sb_pv"), 1)

            sb_z(0)
            for i in range(H2 // 2 + 3):
                staged(i, (sb_z, -1), (sb_r, 1), (sb_pv, 3))
            act_transposes(8)
            act_ready(8)
            gemm_tok(SBO0, 0, 512).then_inc(sig("w_used"), 1)
            gemm_tok(SBO0 + 1, 2, 512).then_inc(sig("w_used"), 1)
            experts(1, MOE1, 9)

        def turned(eng, copy, i, gains, done, first, norm=None):
            for b in range(first, KD // 2, 2):
                eng.wait_ge(sig("xp_pe"), KD * i + 2 * b + 2)
                for k in (2 * b, 2 * b + 1):
                    dst, src = actT[:, k, :], ps[:, 4 + b, (k % 2) * S:(k % 2) * S + S]
                    if norm is None:
                        ins = copy(dst, src, pcols(gains, k) if gains else 1.0)
                    else:
                        c = NPROW + 16 * norm + k
                        ins = copy(dst, src, pcol[:, c:c + 1], pcol[:, c + 8:c + 9])
                    ins.then_inc(sig(done), 1)

        @block.scalar
        def _(act):
            def copy(dst, src, scale=1.0, bias=None):
                if bias is not None:
                    return act.activation(dst, src, ACT.Identity, scale=scale, bias=bias)
                return act.activation(dst, src, ACT.Copy, scale=scale)

            def second_tile(n, src=x_tok):
                act.wait_ge(sig("rstd_ready"), n + 1)
                copy(x_norm[:, 1, :], src[:, 1, :], rstd[:, 1:2]).then_inc(sig("xn1_ready"), 1)

            def second_tile_ln(m):
                act.wait_ge(sig("minus_mean"), m + 1)
                copy(x_norm[:, 1, :], x_tok[:, 1, :], rstd[:, 1:2], minus_mean[:, :]).then_inc(sig("xn1_ready"), 1)

            def bank_pair(g, cols):
                return ps[:, (g % 2) * 2:(g % 2) * 2 + 2, 0:cols]

            second_tile(0, x_norm)
            act.wait_ge(sig("angle"), 1)
            act.activation(rope_cs[:, 1, :, :], rope_tmp[:, 0, 0:32].rearrange("p (t f) -> p t f", t=T), ACT.Sin)
            act.activation(rope_cs[:, 0, :, :], rope_tmp[:, 0, 0:32].rearrange("p (t f) -> p t f", t=T), ACT.Sin,
                           scale=0.5).then_inc(sig("sines"), 1)
            act.wait_ge(sig("pcol"), 1)
            turned(act, copy, 0, "g_mix", "xp_act", 0)
            act.wait_ge(sig("w_used"), 1)
            copy(cq, bank_pair(0, 384)).then_inc(sig("out_by_act"), 1)
            act.wait_ge(sig("w_used"), 3)
            copy(up, bank_pair(2, 512)).then_inc(sig("out_by_act"), 1)
            act.wait_ge(sig("w_used"), 4)
            act.activation(z_silu, bank_pair(3, 512), ACT.Silu).then_inc(sig("out_by_act"), 1)
            act.wait_ge(sig("w_used"), 6)
            for t in range(T):
                ins = copy(q_tok[:, t, :, :].rearrange("p (b h) d -> p b (h d)", b=2), ps[:, 4 + 2 * t:6 + 2 * t, 0:384])
            ins.then_inc(sig("q_out"), 1)
            act.wait_ge(sig("w_used"), 8)
            for t in range(T):
                src = ps[:, 4 + 2 * t:6 + 2 * t, :].rearrange("p b (h d) -> p (b h) d", h=4)
                copy(k_tok[:, t, :, 0:NOPE], src[:, :, 0:NOPE])
                ins = copy(v_tok[:, t, :, :], src[:, :, NOPE:])
            ins.then_inc(sig("kv_out"), 1)
            act.wait_ge(sig("w_used"), 9)
            act.activation(lru_g, ps[:, 0:2, :].rearrange("p b (c s) -> p (b c) s", c=2), ACT.Gelu_apprx_tanh)\
                .then_inc(sig("out_by_act"), 1)
            act.wait_ge(sig("qT_pe"), 1)
            copy(qT[0:QKD, :, :], ps[0:QKD, 4:8, :].rearrange("p b (h s) -> p (b h) s", h=2)).then_inc(sig("qT"), 1)
            act.wait_ge(sig("x_conv"), 1)
            act.activation(xbS, xbS, ACT.Silu).then_inc(sig("xbS"), 1)
            act.wait_ge(sig("sp_abs"), 1)
            act.activation(sp_e[:, :], sp_a[:, :], ACT.Exp, scale=-1.0)
            act.activation(a_head[:, :], brow[:, 8:16], ACT.Exp)
            act.drain()
            act.activation(sp_e[:, :], sp_e[:, :], ACT.Ln, bias=1.0).then_inc(sig("sp_ln"), 1)
            act.wait_ge(sig("kT_pe"), 1)
            copy(kT[0:QKD, :, :], ps[0:QKD, 4:8, :].rearrange("p b (h s) -> p (b h) s", h=2)).then_inc(sig("kT"), 1)

            def gate(i):
                g = 8 + i
                act.wait_ge(sig("w_used"), 11 + i)
                act.activation(gates[:, :, 512 * i:512 * i + 512], bank_pair(g, 512), ACT.Sigmoid)\
                    .then_inc(sig("out_by_act"), 1)

            def mla_exp(h):
                act.wait_ge(sig("mla_max"), h + 1)
                d = 2 * (h % 2)
                act.activation(probs[:, 0:P], probs[:, 0:P], ACT.Exp, bias=mx[:, 0:1], accum_out=den[:, d:d + 1])
                act.activation(probs[:, P:384], probs[:, P:384], ACT.Exp, bias=mx[:, 1:2],
                               accum_out=den[:, d + 1:d + 2]).then_inc(sig("mla_exp"), 1)

            def xs_out():
                act.wait_ge(sig("xs_pe"), 1)
                copy(xs_tok, ps[:, 6:8, :]).then_inc(sig("xs_tok"), 1)

            def dm_exp(half):
                act.wait_ge(sig("dm"), half + 1)
                v = dm[:, 4 * half:4 * half + 4, :]
                act.activation(v, v, ACT.Exp).then_inc(sig("dm_exp"), 1)

            def lru_sigmoid(i):
                act.wait_ge(sig("lru_pe"), i + 1)
                dst, bias = ((lru_r, "lru_b_a"), (lru_i, "lru_b_i"))[i]
                for c in range(KM):
                    ins = act.activation(dst[:, c, :], ps[:, 6 + c // 2, (c % 2) * S:(c % 2) * S + S], ACT.Sigmoid,
                                         bias=pcols(bias, c))
                ins.then_inc(sig(("lru_r", "lru_i")[i]), 1)

            def lru_decay():
                act.wait_ge(sig("lru_nl"), 1)
                act.activation(lru_a, lru_r, ACT.Exp, scale=-1.0)
                act.activation(lru_t, lru_r, ACT.Tanh).then_inc(sig("lru_at"), 1)

            def lru_root():
                act.wait_ge(sig("lru_sq"), 1)
                act.activation(lru_t, lru_t, ACT.Sqrt).then_inc(sig("lru_root"), 1)

            extra = {1: [xs_out], 2: [lambda: dm_exp(0)], 3: [lambda: dm_exp(1)], 4: [lambda: lru_sigmoid(0)],
                     5: [lambda: lru_sigmoid(1), lru_decay], 6: [lru_root]}
            for i in range(8):
                gate(i)
                mla_exp(i)
                for f in extra.get(i, []):
                    f()
            act.wait_ge(sig("mla_oT_pe"), KM)
            copy(yaT, ps[:, 4:6, :].rearrange("p b (c s) -> p (b c) s", c=2)).then_inc(sig("yaT"), 1)
            turned(act, copy, 1, None, "xp_act", 0)
            second_tile(3)
            turned(act, copy, 2, "g_mlp", "xp_act", 0)
            for i in range(8):
                act.wait_ge(sig("w_used"), 25 + i)
                act.activation(hidT[:, 4 * i:4 * i + 4, :],
                               ps[:, (i % 2) * 2:(i % 2) * 2 + 2, :].rearrange("p b (c s) -> p (b c) s", c=2),
                               ACT.Relu).then_inc(sig("ff1_relu"), 1)
            act.wait_ge(sig("pT_pe"), 2)
            copy(pT, ps[:, 4, :].rearrange("p (c s) -> p c s", c=2)).then_inc(sig("pT"), 1)
            for i in range(2):
                act.wait_ge(sig("flip_pe"), i + 1)
                copy(bias_h[:, 8 * i:8 * i + 8, :], ps[:, 4:8, :].rearrange("p b (h s) -> p (b h) s", h=2))\
                    .then_inc(sig("bias_h"), 1)
            second_tile(4)
            turned(act, copy, 3, "g_ple", "xp_act", 0)
            for h in range(2):
                act.wait_ge(sig("w_used"), 42 + h)
                act.activation(x_norm[:, :, 512 * h:512 * h + 512], ps[:, 4 + 2 * h:6 + 2 * h, :], ACT.Sigmoid)\
                    .then_inc(sig("ple_gate"), 1)
            second_tile(5)
            turned(act, copy, 4, "g_final", "xp_act", 0)

            def qkv(n0, g, step):
                for i, (dst, scale) in enumerate(((q2T, 0.125), (k2T, 1.0), (v2, 1.0))):
                    act.wait_ge(sig("w_used"), n0 + 2 * i + 1 + g * step)
                    d = dst[:, bass.ds(g, 1), 0:4, :] if i < 2 else dst[:, bass.ds(g, 1), :, 0:512]
                    src = ps[:, 0:2, :].rearrange("p b (c s) -> p (b c) s", c=2) if i < 2 else ps[:, 0:2, :]
                    copy(d.rearrange("p o c s -> p (o c) s"), src, scale).then_inc(sig("qkv_act"), 1)

            with act.Fori(0, 3) as g:
                qkv(DIL0, g, 6)

            def dil_exp(h):
                act.wait_ge(sig("dil_max"), h + 1)
                d = 2 * (h % 2)
                e, m = e_dil[:, h % 2, :], mx4[:, d:d + 2]
                act.activation(e[:, 0:384], e[:, 0:384], ACT.Exp, bias=m[:, 0:1], accum_out=den[:, d:d + 1])
                act.activation(e[:, 384:], e[:, 384:], ACT.Exp, bias=m[:, 1:2], accum_out=den[:, d + 1:d + 2])\
                    .then_inc(sig("dil_exp"), 1)

            dil_exp(0)
            for h in range(H2):
                if h + 1 < H2:
                    dil_exp(h + 1)
                act.wait_ge(sig("dil_pT_pe"), h + 1)
                copy(eT_two[h % 2][0], ps[:, 3, 0:384]).then_inc(sig("dil_pT_act"), 1)
            turned(act, copy, 5, None, "xp_act", 0)

            def w_split(n0, b, j):
                n = n0 + b
                act.wait_ge(sig(f"w_landed{n % RING}"), 32 * (n // RING + 1) + j * 32)
                act.wait_ge(sig("w_used"), n - 2 + j * 3)
                copy(w_hi[:, n % 3, :], w_ring[:, n % RING, :], W_POW).then_inc(sig("w_hi"), 1)

            def experts(layer, n0, turn):
                for b in range(2):
                    w_split(n0, b, 0)
                second_tile_ln(2 * layer)
                turned(act, copy, turn, None, "xp_act", 0, 2 * layer)
                act.wait_ge(sig("xp_dve"), 4 * turn + 4)
                act.drain()
                for t in range(T):
                    copy(aT_hi[:, :, t * P:(t + 1) * P], actT[:, :, t * P:(t + 1) * P], A_POW).then_inc(sig("aT_hi"), 1)
                act.wait_ge(sig("logits"), layer + 1)
                act.activation(score, ps[:, 0, 0:T * NE], ACT.Exp, scale=-1.0).then_inc(sig("router_exp"), 1)

                def silu(b, j):
                    act.wait_ge(sig("w_used"), n0 + b + 1 + j * 3)
                    act.activation(e_silu[:, b, :, :], ps[:, 4 + 2 * b:6 + 2 * b, 0:DE], ACT.Silu, scale=1.0 / SUM_POW)\
                        .then_inc(sig("moe_silu"), 1)

                def h_high(b, j):
                    act.wait_ge(sig("moe_hT_pe"), NE * layer + 1 + b + j * 2)
                    copy(hT_hi[:, b, :], ps[:, 4 + 2 * b, :]).then_inc(sig("moe_hT_hi"), 1)

                def pair(j, last):
                    silu(0, j)
                    w_split(n0, 2, j)
                    if not last:
                        w_split(n0 + 3, 0, j)
                    h_high(0, j)
                    silu(1, j)
                    if not last:
                        w_split(n0 + 3, 1, j)
                    h_high(1, j)

                with act.Fori(0, NE // 2 - 1) as j:
                    pair(j, False)
                pair(NE // 2 - 1, True)

            act.wait_ge(sig("dil_pv"), H2)
            experts(0, MOE0, 6)
            second_tile_ln(1)
            turned(act, copy, 7, None, "xp_act", 0, 1)
            for i, (dst, scale) in enumerate(((q2T, 0.125), (k2T, 1.0), (v2, 1.0))):
                act.wait_ge(sig("w_used"), SBI0 + 2 * i + 1)
                d = dst[:, 0, 0:4, :] if i < 2 else dst[:, 0, :, 0:512]
                src = ps[:, 0:2, :].rearrange("p b (c s) -> p (b c) s", c=2) if i < 2 else ps[:, 0:2, :]
                copy(d, src, scale).then_inc(sig("qkv_act"), 1)

            def sb_softplus(m):
                act.wait_ge(sig("sb_zc"), m + 1)
                act.activation(sb_l[m % SBN], sb_e[m % SBN], ACT.Exp)
                act.drain()
                act.activation(sb_l[m % SBN], sb_l[m % SBN], ACT.Ln, bias=1.0).then_inc(sig("sb_ln"), 1)

            def sb_exp(m):
                act.wait_ge(sig("sb_d"), m + 1)
                act.activation(sb_e[m % SBN], sb_e[m % SBN], ACT.Exp).then_inc(sig("sb_exp"), 1)

            for i in range(H2 // 2 + 2):
                staged(i, (sb_softplus, 0), (sb_exp, 2))
            turned(act, copy, 8, None, "xp_act", 0)
            act.wait_ge(sig("sb_pv"), H2 // 2)
            experts(1, MOE1, 9)
            second_tile_ln(3)

        @block.vector
        def _(dve):
            def scaled(dst, src, scale, bias=None):
                if bias is not None:
                    return dve.tensor_scalar(dst, src, scale, bias, ALU.mult, ALU.add)
                return dve.tensor_scalar(dst, src, scale, None, ALU.mult)

            def both_tiles():
                dve.drain()
                for t in range(T):
                    dve.engine_nop().then_inc(sig(f"xn{t}_ready"), 1)

            def bank_pair(g, cols, o=0):
                return ps[:, (g % 2) * 2:(g % 2) * 2 + 2, o:o + cols]

            def mean_square(src, cols, i, junk):
                for t in range(T):
                    dve.tensor_tensor_reduce(junk[:, t, 0:cols], src[:, t, :], src[:, t, :], 1.0, 0.0, ALU.mult, ALU.add,
                                             ms[:, i + t:i + t + 1])
                dve.drain()
                return dve.tensor_scalar(ms[:, i:i + T], ms[:, i:i + T], 1.0 / cols, EPS, ALU.mult, ALU.add)

            def squares(t, c, part):
                dve.tensor_tensor_reduce(x_norm[:, t, c], x_tok[:, t, c], x_tok[:, t, c], 1.0, 0.0, ALU.mult, ALU.add, part)

            def first_tile(n):
                dve.drain()
                dve.tensor_scalar(ms[:, 0:T], ms[:, 0:T], 1.0 / D, EPS, ALU.mult, ALU.add).then_inc(sig("ms_ready"), 1)
                dve.wait_ge(sig("rstd_ready"), n + 1)
                scaled(x_norm[:, 0, :], x_tok[:, 0, :], rstd[:, 0:1]).then_inc(sig("xn0_ready"), 1)

            def halves_sum():
                dve.drain()
                dve.tensor_tensor(ms[:, 0:T], ms_part[:, 0, :], ms_part[:, 1, :], ALU.add)

            junk = gates[:, :, 0:D]
            dve.wait_ge(sig("ld_x"), 16)
            mean_square(x_norm, D, 0, junk).then_inc(sig("ms_ready"), 1)
            dve.wait_ge(sig("rstd_ready"), 1)
            scaled(x_norm[:, 0, :], x_norm[:, 0, :], rstd[:, 0:1]).then_inc(sig("xn0_ready"), 1)
            dve.wait_ge(sig("ld_rows"), 16 * 6)
            dve.tensor_copy(pos_f[:, :], pos_i[:, :])
            dve.drain()
            ang, turns, tmp = (rope_tmp[:, 0, 32 * i:32 * i + 32] for i in range(3))
            for t in range(T):
                dve.tensor_scalar(ang[:, 16 * t:16 * t + 16], inv_freq, pos_f[:, t:t + 1], None, ALU.mult)
            dve.drain()
            dve.tensor_scalar(turns, ang, float(1 / (2 * np.pi)), None, ALU.mult)
            dve.drain()
            dve.tensor_scalar(turns, turns, 12582912.0, None, ALU.add)
            dve.drain()
            dve.tensor_scalar(turns, turns, -12582912.0, None, ALU.add)
            dve.drain()
            c1 = 6.28125
            c2 = round((2 * np.pi - c1) * 2 ** 19) / 2 ** 19
            c3 = 2 * np.pi - c1 - c2
            for c in (c1, c2, c3):
                dve.scalar_tensor_tensor(out=ang, in0=turns, scalar=-c, in1=ang, op0=ALU.mult, op1=ALU.add)
                dve.drain()
            dve.tensor_scalar(ang, ang, 3.1415925, -3.1415925, ALU.min, ALU.max).then_inc(sig("angle"), 1)
            dve.wait_ge(sig("params_T"), 1)
            dve.tensor_copy(pcol[:, :], ps[:, 0, 0:NCOL]).then_inc(sig("pcol"), 1)
            dve.drain()
            turned(dve, scaled, 0, "g_mix", "xp_dve", 1)
            dve.wait_ge(sig("sines"), 1)
            cos, sin = rope_cs[:, 0, :, :], rope_cs[:, 1, :, :]
            dve.tensor_tensor(cos, cos, cos, ALU.mult)
            dve.drain()
            dve.tensor_scalar(cos, cos, -2.0, 1.0, ALU.mult, ALU.add)
            dve.wait_ge(sig("w_used"), 2)
            for t in range(T):
                ins = dve.tensor_copy(u_cqkv[:, T * QL + 288 * t:T * QL + 288 * t + 288], ps[:, 2 + t, 0:288])
            ins.then_inc(sig("out_by_dve"), 1)
            dve.drain()
            dve.wait_ge(sig("out_by_act"), 1)
            mean_square(cq, QL, 0, junk)
            mean_square(ckv[:, :, 0:KVL], KVL, 2, junk).then_inc(sig("ms_ready"), 1)
            dve.wait_ge(sig("rstd_ready"), 2)
            for t in range(T):
                scaled(cq[:, t, :], cq[:, t, :], rstd[:, t:t + 1])
                ins = scaled(ckv[:, t, 0:KVL], ckv[:, t, 0:KVL], rstd[:, 2 + t:3 + t])
            ins.then_inc(sig("mla_normed"), 1)
            dve.wait_ge(sig("pool_d"), 1)
            dve.tensor_copy(u_dT, ps[:, 4:6, :].rearrange("p b s -> p (b s)")).then_inc(sig("dT"), 1)
            dve.wait_ge(sig("w_used"), 5)
            xb_in = xbT[:, :, CONV - 1:]
            dve.tensor_copy(xb_in[:, 0:2, :], ps[:, 0, :].rearrange("p (c s) -> p c s", c=2))
            dve.tensor_copy(xb_in[:, 2, :], ps[:, 1, 0:S]).then_inc(sig("out_by_dve"), 1)
            dve.wait_ge(sig("cT_pe"), 1)
            for k in range(5):
                gain = pcols("q_norm", k) if k < 3 else pcols("kv_norm", k - 3)
                ins = scaled(cT[:, k, :], ps[:, 4 + k // 2, (k % 2) * S:(k % 2) * S + S], gain)
            ins.then_inc(sig("cT"), 1)

            def rope(x, heads, t4):
                def cs(c):
                    return c.unsqueeze(2).broadcast_to([P, T, heads, 16]) if heads > 1 else c
                lo, hi = (x[:, :, :, 0:16], x[:, :, :, 16:32]) if heads > 1 else (x[:, :, 0:16], x[:, :, 16:32])
                dve.tensor_tensor(t4[0], lo, cs(cos), ALU.mult)
                dve.tensor_tensor(t4[1], hi, cs(sin), ALU.mult)
                dve.tensor_tensor(t4[2], hi, cs(cos), ALU.mult)
                dve.tensor_tensor(t4[3], lo, cs(sin), ALU.mult)
                dve.drain()
                dve.tensor_tensor(lo, t4[0], t4[1], ALU.subtract)
                return dve.tensor_tensor(hi, t4[2], t4[3], ALU.add)

            dve.wait_ge(sig("q_out"), 1)
            rope(q_tok[:, :, :, NOPE:], MH, [rope_tmp[:, i, :].rearrange("p (t h f) -> p t h f", t=T, h=MH)
                                             for i in range(4)]).then_inc(sig("q_roped"), 1)
            dve.wait_ge(sig("w_used"), 7)
            dve.tensor_copy(xb_in[:, 3:5, :], ps[:, 2, :].rearrange("p (c s) -> p c s", c=2))
            dve.tensor_copy(xb_in[:, 5, :], ps[:, 3, 0:S])
            dve.tensor_tensor(sp_v[:, 0:16].rearrange("p (t h) -> p t h", t=T),
                              ps[:, 3, S:S + 16].rearrange("p (t h) -> p t h", t=T),
                              brow[:, 0:8].unsqueeze(1).broadcast_to([P, T, MH]), ALU.add)\
                .then_inc(sig("out_by_dve"), 1)
            dve.tensor_scalar(sp_v[:, 16:20], pcol[:, PROW["lru_lambda"]:PROW["lru_lambda"] + 4], -1.0, None, ALU.mult)
            dve.drain()
            dve.scalar_tensor_tensor(out=sp_a[:, :], in0=sp_v[:, :], scalar=-1.0, in1=sp_v[:, :], op0=ALU.mult, op1=ALU.max)\
                .then_inc(sig("sp_abs"), 1)
            rope(ckv[:, :, KVL:288], 1, [rope_tmp[:, i, 0:32].rearrange("p (t f) -> p t f", t=T) for i in range(4)])
            dve.drain()
            dve.wait_ge(sig("kv_out"), 1)
            for t in range(T):
                ins = dve.tensor_copy(k_tok[:, t, :, NOPE:], ckv[:, t:t + 1, KVL:288].broadcast_to([P, MH, ROPE]))
            ins.then_inc(sig("k_roped"), 1)

            def conv(dst, src, chunks, w, b):
                for j in range(CONV):
                    for c in range(chunks):
                        win = src[:, c, j:j + S]
                        if j == 0:
                            ins = dve.tensor_scalar(dst[:, c, :], win, pcols(w, c), pcols(b, c), ALU.mult, ALU.add)
                        else:
                            ins = dve.scalar_tensor_tensor(out=dst[:, c, :], in0=win, scalar=pcols(w, j * chunks + c),
                                                           in1=dst[:, c, :], op0=ALU.mult, op1=ALU.add)
                    if j < CONV - 1:
                        dve.drain()
                return ins

            dve.wait_ge(sig("lru_zeroed"), 1)
            conv(xbS, xbT, KX, "ssd_conv_w", "ssd_conv_b").then_inc(sig("x_conv"), 1)
            dve.wait_ge(sig("w_used"), 10)
            dve.tensor_copy(lxT[:, :, CONV - 1:], ps[:, 2:4, :].rearrange("p b (c s) -> p (b c) s", c=2))\
                .then_inc(sig("out_by_dve"), 1)
            dve.wait_ge(sig("sp_ln"), 1)
            dve.scalar_tensor_tensor(out=sp_v[:, :], in0=sp_v[:, :], scalar=0.0, in1=sp_e[:, :], op0=ALU.max, op1=ALU.add)
            dve.drain()
            dve.tensor_copy(stats[:, 0:16], sp_v[:, 0:16])
            dve.tensor_scalar(decay8[:, :], sp_v[:, 16:20], 8.0, None, ALU.mult)
            dve.drain()
            dve.scalar_tensor_tensor(out=a_tok, in0=dt_tok, scalar=-1.0,
                                     in1=a_head[:, :].unsqueeze(1).broadcast_to([P, T, MH]),
                                     op0=ALU.mult, op1=ALU.mult).then_inc(sig("a_tok"), 1)
            conv(xcT, lxT, KM, "lru_conv_w", "lru_conv_b").then_inc(sig("xcT"), 1)

            def mla_max(h):
                dve.wait_ge(sig("mla_scores"), h + 1)
                if h:
                    dve.wait_ge(sig("mla_pT_pe"), h)
                dve.tensor_tensor_reduce(probs[:, 0:P], ps[:, 4, 0:P], cmask, MLA_SCALE, -3e38, ALU.add, ALU.max,
                                         mx[:, 0:1])
                dve.tensor_tensor_reduce(probs[:, P:384], ps[:, 4, P:384], zc_mask[:, :], MLA_SCALE, -3e38,
                                         ALU.add, ALU.max, mx[:, 1:2])
                dve.drain()
                dve.tensor_scalar(mx, mx, -1.0, None, ALU.mult).then_inc(sig("mla_max"), 1)

            def mla_o(h):
                dve.wait_ge(sig("mla_pT_pe"), h + 1)
                dve.tensor_copy(probsT, ps[:, 5, 0:384]).then_inc(sig("mla_pT"), 1)
                d = 2 * (h % 2)
                dve.reciprocal(den[:, 4 + d:6 + d], den[:, d:d + 2])
                dve.drain()
                dve.wait_ge(sig("mla_pv"), h + 1)
                for t in range(T):
                    ins = scaled(o_mla[:, t, 64 * h:64 * h + 64], ps[:, 5, 384 + 64 * t:448 + 64 * t],
                                 den[:, 4 + d + t:5 + d + t])
                ins.then_inc(sig("mla_o"), 1)

            def cb_mask():
                dve.wait_ge(sig("cb_pe"), 1)
                for gr in range(2):
                    ins = dve.tensor_tensor(cbm[:, gr, :], ps[:, 6 + gr, 0:384], tri3, ALU.mult)
                ins.then_inc(sig("cbm"), 1)

            def ssd_xdt():
                dve.wait_ge(sig("acs_pe"), 1)
                dve.tensor_copy(stats[:, 32:48], ps[:, 6, 0:16]).then_inc(sig("acs"), 1)
                dve.wait_ge(sig("xs_tok"), 1)
                dve.tensor_tensor(xdt.rearrange("p t (h d) -> p (t h) d", d=64),
                                  xs_tok.rearrange("p t (h d) -> p (t h) d", d=64),
                                  stats[:, 0:16].unsqueeze(2).broadcast_to([P, 16, 64]), ALU.mult).then_inc(sig("xdt"), 1)

            def decay(half):
                dve.wait_ge(sig("cum_pe"), half + 1)
                dve.drain()
                for j in range(4):
                    h = 4 * half + j
                    src = ps[:, 6 + j // 2, (j % 2) * S:(j % 2) * S + S]
                    dve.tensor_scalar(dm[:, h, 0:S], src, acs[:, 0, h:h + 1], 0.0, ALU.subtract, ALU.min)
                    ins = dve.tensor_scalar(dm[:, h, S:384], src[:, P:S], acs[:, 1, h:h + 1], 0.0, ALU.subtract, ALU.min)
                ins.then_inc(sig("dm"), 1)

            def decay_cb():
                for half in range(2):
                    dve.wait_ge(sig("dm_exp"), half + 1)
                    for j in range(4):
                        ins = dve.tensor_tensor(dm[:, 4 * half + j, :], dm[:, 4 * half + j, :], cbm[:, half, :], ALU.mult)
                ins.then_inc(sig("dm_cb"), 1)

            def lru_log():
                dve.wait_ge(sig("lru_r"), 1)
                for c in range(KM):
                    ins = scaled(lru_r[:, c, :], lru_r[:, c, :], decay8[:, c:c + 1])
                ins.then_inc(sig("lru_nl"), 1)

            def ssd_out():
                dv = y_ssd.rearrange("p t (h d) -> p t h d", h=MH)
                for t in range(T):
                    dve.tensor_tensor(dv[:, t, :, :], xs_tok[:, t, :].rearrange("p (h d) -> p h d", h=MH),
                                      brow[:, 16:24].unsqueeze(2).broadcast_to([P, MH, 64]), ALU.mult)
                dve.drain()
                dve.wait_ge(sig("ssd_y_pe"), 1)
                dve.tensor_tensor(y_ssd, y_ssd, ps[:, 6:8, :], ALU.add).then_inc(sig("ssd_y"), 1)
                dve.drain()
                dve.tensor_tensor(y_ssd, y_ssd, z_silu, ALU.mult)
                dve.drain()
                mean_square(y_ssd, MIX, 0, xs_tok).then_inc(sig("ms_ready"), 1)
                dve.wait_ge(sig("rstd_ready"), 3)
                for t in range(T):
                    ins = scaled(y_ssd[:, t, :], y_ssd[:, t, :], rstd[:, t:t + 1])
                ins.then_inc(sig("ssd_normed"), 1)

            def lru_input():
                dve.wait_ge(sig("lru_at"), 1)
                sq = xs_tok.rearrange("p t n -> p (t n)").rearrange("p (c s) -> p c s", c=KM)
                dve.drain()
                dve.tensor_tensor(sq, lru_a, lru_a, ALU.mult)
                dve.drain()
                dve.scalar_tensor_tensor(out=lru_t, in0=sq, scalar=1.0, in1=lru_t, op0=ALU.add, op1=ALU.mult)\
                    .then_inc(sig("lru_sq"), 1)
                dve.wait_ge(sig("lru_i"), 1)
                dve.tensor_tensor(lru_i, lru_i, xcT, ALU.mult)

            def pool_out():
                dve.wait_ge(sig("pool_y"), 1)
                for c in range(KM):
                    ins = scaled(ybT[:, c, :], ps[:, 6 + c // 2, (c % 2) * S:(c % 2) * S + S], pcols("pool_scale", c))
                ins.then_inc(sig("ybT"), 1)

            def lru_scan():
                dve.wait_ge(sig("lru_root"), 1)
                dve.drain()
                dve.tensor_tensor(lru_i, lru_i, lru_t, ALU.mult)
                dve.drain()
                for c in range(KM):
                    dve.tensor_tensor_scan(lru_r[:, c, :], lru_a[:, c, :], lru_i[:, c, :], 0.0, ALU.mult, ALU.add)
                dve.drain()
                dve.tensor_tensor(lru_g, lru_g, lru_r, ALU.mult).then_inc(sig("ydT"), 1)

            def ssd_turned():
                dve.wait_ge(sig("ycT_pe"), KM)
                for c in range(KM):
                    ins = scaled(ycT[:, c, :], ps[:, 6 + c // 2, (c % 2) * S:(c % 2) * S + S], pcols("ssd_norm", c))
                ins.then_inc(sig("ycT"), 1)

            extra = {0: [cb_mask], 1: [ssd_xdt], 2: [lambda: decay(0)], 3: [lambda: decay(1), decay_cb],
                     4: [lru_log], 5: [ssd_out], 6: [lru_input, pool_out], 7: [lru_scan, ssd_turned]}
            dve.memset(zc_mask[:, 0:P], 0.0)
            dve.tensor_copy(zc_mask[:, P:S], cmask)
            dve.drain()
            for i in range(8):
                mla_max(i)
                if i:
                    mla_o(i - 1)
                for f in extra[i]:
                    f()
            mla_o(MH - 1)
            for i, b in enumerate((1, 0, 3, 2)):
                dve.wait_ge(sig("w_used"), 19 + i)
                if i == 0:
                    dve.wait_ge(sig("out_by_act"), 12)
                for t in range(T):
                    y = ps[:, 4 * (i % 2) + 2 * t:4 * (i % 2) + 2 * t + 2, :].rearrange("p b n -> p (b n)")
                    gt = gates[:, t, D * b:D * b + D]
                    if i == 0:
                        ins = dve.tensor_tensor(x_norm[:, t, :], y, gt, ALU.mult)
                    else:
                        ins = dve.tensor_tensor(gt, y, gt, ALU.mult)
                ins.then_inc(sig("branch"), 1)
                if i:
                    dve.drain()
                    for t in range(T):
                        ins = dve.tensor_tensor(x_norm[:, t, :], x_norm[:, t, :], gates[:, t, D * b:D * b + D], ALU.add)
                if i < 3:
                    dve.drain()
            both_tiles()
            turned(dve, scaled, 1, None, "xp_dve", 1)
            dve.wait_ge(sig("ld_x"), 32)
            for h in range(2):
                dve.wait_ge(sig("w_used"), 23 + h)
                ins = dve.tensor_tensor(x_tok[:, :, 512 * h:512 * h + 512], x_tok[:, :, 512 * h:512 * h + 512],
                                        ps[:, 2 * h:2 * h + 2, :], ALU.add)
                if h:
                    ins.then_inc(sig("x_res"), 1)
                dve.drain()
                for t in range(T):
                    squares(t, slice(512 * h, 512 * h + 512), ms_part[:, h, t:t + 1])
            halves_sum()
            first_tile(3)
            turned(dve, scaled, 2, "g_mlp", "xp_dve", 1)
            for i in range(8):
                dve.wait_ge(sig("ff1_relu"), i + 1)
                h4 = hidT[:, 4 * i:4 * i + 4, :]
                dve.tensor_tensor(h4, h4, h4, ALU.mult).then_inc(sig("ff1_square"), 1)
            dve.wait_ge(sig("rel_pe"), 1)
            dve.tensor_copy(rel_row, ps[0:H2, 5, 0:384]).then_inc(sig("rel_row"), 1)
            for t in range(T):
                if t == 0:
                    dve.wait_ge(sig("ff2_first"), 1)
                else:
                    dve.wait_ge(sig("w_used"), 40)
                ins = dve.tensor_tensor(x_tok[:, t, :], x_tok[:, t, :],
                                        ps[:, 2 * t:2 * t + 2, :].rearrange("p b n -> p (b n)"), ALU.add)
                if t:
                    ins.then_inc(sig("x_res"), 1)
                dve.drain()
                squares(t, slice(0, D), ms[:, t:t + 1])
            first_tile(4)
            turned(dve, scaled, 3, "g_ple", "xp_dve", 1)
            for h in range(2):
                dve.wait_ge(sig("ple_gate"), h + 1)
                xn, xt = (v[:, :, 512 * h:512 * h + 512] for v in (x_norm, x_tok))
                y = ps[:, 0:4, :].rearrange("p (t h) n -> p t h n", h=2)[:, :, h, :]
                ins = dve.tensor_tensor(xn, xn, y, ALU.mult)
                if h:
                    ins.then_inc(sig("x_res"), 1)
                dve.drain()
                dve.tensor_tensor(xt, xt, xn, ALU.add)
                dve.drain()
                for t in range(T):
                    squares(t, slice(512 * h, 512 * h + 512), ms_part[:, h, t:t + 1])
            halves_sum()
            first_tile(5)
            turned(dve, scaled, 4, "g_final", "xp_dve", 1)

            def qkv(n0, g, step):
                for i, (dst, scale) in enumerate(((q2T, 0.125), (k2T, 1.0), (v2, 1.0))):
                    dve.wait_ge(sig("w_used"), n0 + 2 * i + 2 + g * step)
                    d = dst[:, bass.ds(g, 1), 4:8, :] if i < 2 else dst[:, bass.ds(g, 1), :, 512:]
                    src = ps[:, 2:4, :].rearrange("p b (c s) -> p (b c) s", c=2) if i < 2 else ps[:, 2:4, :]
                    scaled(d.rearrange("p o c s -> p (o c) s"), src, scale).then_inc(sig("qkv_dve"), 1)

            with dve.Fori(0, 3) as g:
                qkv(DIL0, g, 6)

            def dil_max(h):
                dve.wait_ge(sig("dil_scores"), h + 1)
                dve.wait_ge(sig("bm"), h + 1)
                if h >= 2:
                    dve.wait_ge(sig("dil_pT_pe"), h - 1)
                e, m = e_dil[:, h % 2, :], mx4[:, 2 * (h % 2):2 * (h % 2) + 2]
                dve.tensor_tensor_reduce(e[:, 0:384].rearrange("p (g s) -> p g s", g=3),
                                         ps[:, 0, 0:384].rearrange("p (g s) -> p g s", g=3), bm[:, h % 2, :, P:S],
                                         1.0, -3e38, ALU.add, ALU.max, m[:, 0:1])
                dve.tensor_tensor_reduce(e[:, 384:], ps[:, 1:3, :].rearrange("p b n -> p (b n)")[:, 0:768],
                                         bm[:, h % 2, :, :].rearrange("p g s -> p (g s)"),
                                         1.0, -3e38, ALU.add, ALU.max, m[:, 1:2])
                dve.drain()
                dve.tensor_scalar(m, m, -1.0, None, ALU.mult).then_inc(sig("dil_max"), 1)

            def dil_o(h):
                d = 2 * (h % 2)
                dve.wait_ge(sig("dil_pv"), h + 1)
                for t in range(T):
                    ins = scaled(x_norm[:, t, 64 * h:64 * h + 64], ps[:, 6 + h % 2, 64 * t:64 * t + 64],
                                 den[:, 4 + d + t:5 + d + t])
                ins.then_inc(sig("dil_o"), 1)

            dve.wait_ge(sig("x_full"), 1)
            dil_max(0)
            for h in range(H2):
                if h + 1 < H2:
                    dil_max(h + 1)
                dve.wait_ge(sig("dil_pT_pe"), h + 1)
                dve.tensor_copy(eT_two[h % 2][1], ps[:, 4:6, :].rearrange("p b n -> p (b n)")[:, 0:768])\
                    .then_inc(sig("dil_pT_dve"), 1)
                d = 2 * (h % 2)
                dve.drain()
                dve.reciprocal(den[:, 4 + d:6 + d], den[:, d:d + 2])
                if h:
                    dil_o(h - 1)
            dve.drain()
            dil_o(H2 - 1)
            both_tiles()
            turned(dve, scaled, 5, None, "xp_dve", 1)

            def w_split(n0, b, j):
                n = n0 + b
                dve.wait_ge(sig("w_hi"), moe_index(n0) + b + 1 + j * 3)
                dve.scalar_tensor_tensor(out=w_lo[:, n % 3, :], in0=w_ring[:, n % RING, :], scalar=W_POW,
                                         in1=w_hi[:, n % 3, :], op0=ALU.mult, op1=ALU.subtract).then_inc(sig("w_lo"), 1)

            def layer_norm(m):
                after_experts = m % 2
                pow2 = SUM_POW if after_experts else 1.0
                dve.wait_ge(sig("x_full"), m + 1)
                for i in range(2):
                    if after_experts:
                        if i == 0:
                            dve.wait_ge(sig("moe_first"), m // 2 + 1)
                        else:
                            dve.wait_ge(sig("w_used"), (MOE0, MOE1)[m // 2] + 3 * NE // 2)
                        dst, src = x_tok[:, i, :], ps[:, 2 * i:2 * i + 2, :].rearrange("p b n -> p (b n)")
                    else:
                        dve.wait_ge(sig("w_used"), (DOUT0, SBO0)[m // 2] + 1 + i)
                        dst, src = x_tok[:, :, 512 * i:512 * i + 512], ps[:, 2 * i:2 * i + 2, :]
                    dve.scalar_tensor_tensor(out=dst, in0=dst, scalar=ALPHA * pow2, in1=src, op0=ALU.mult, op1=ALU.add)
                    dve.drain()
                    for j in range(2):
                        t, h = (i, j) if after_experts else (j, i)
                        dve.bn_stats(bn_part[:, t, h, :], x_tok[:, t, 512 * h:512 * h + 512])
                dve.drain()
                for t in range(T):
                    dve.bn_aggr(bn_mv[:, t, :], bn_part[:, t, :, :])
                dve.drain()
                dve.tensor_scalar(ms[:, 0:T], bn_mv[:, :, 1], LN_EPS * pow2 * pow2, None, ALU.add)\
                    .then_inc(sig("ms_ready"), 1)
                dve.wait_ge(sig("rstd_ready"), 7 + m)
                dve.scalar_tensor_tensor(out=minus_mean[:, :], in0=bn_mv[:, 1, 0:1], scalar=-1.0, in1=rstd[:, 1:2],
                                         op0=ALU.mult, op1=ALU.mult).then_inc(sig("minus_mean"), 1)
                dve.tensor_scalar(x_norm[:, 0, :], x_tok[:, 0, :], bn_mv[:, 0, 0:1], rstd[:, 0:1],
                                  ALU.subtract, ALU.mult).then_inc(sig("xn0_ready"), 1)

            def rank_of_four(v, rank, tmp, init):
                dve.tensor_copy(rank, init)
                dve.drain()
                for s in (1, 2, 3):
                    c = tmp[:, :, 0:4 - s]
                    dve.tensor_tensor(c, v[:, :, 0:4 - s], v[:, :, s:4], ALU.is_ge)
                    dve.drain()
                    dve.tensor_tensor(rank[:, :, s:4], rank[:, :, s:4], c, ALU.add)
                    dve.drain()
                    dve.tensor_tensor(rank[:, :, 0:4 - s], rank[:, :, 0:4 - s], c, ALU.subtract)
                    dve.drain()

            def experts(layer, n0, turn):
                turned(dve, scaled, turn, None, "xp_dve", 1, 2 * layer)
                dve.wait_ge(sig("xp_act"), 4 * turn + 4)
                dve.drain()
                for t in range(T):
                    c = slice(t * P, (t + 1) * P)
                    dve.wait_ge(sig("aT_hi"), 2 * layer + t + 1)
                    dve.scalar_tensor_tensor(out=aT_lo[:, :, c], in0=actT[:, :, c], scalar=A_POW, in1=aT_hi[:, :, c],
                                             op0=ALU.mult, op1=ALU.subtract).then_inc(sig("aT_lo"), 1)
                w_split(n0, 1, 0)
                g4 = lambda v: v.rearrange("p (g e) -> p g e", e=4)
                tg = lambda v: v.rearrange("p (t e) -> p t e", t=T)
                dve.wait_ge(sig("router_exp"), layer + 1)
                dve.tensor_scalar(score, score, 1.0, None, ALU.add)
                dve.drain()
                dve.reciprocal(score, score)
                dve.drain()
                dve.tensor_tensor(tg(r_v), tg(score), brow[:, 24:40].unsqueeze(1).broadcast_to([P, T, NE]), ALU.add)
                dve.drain()
                rank_of_four(g4(r_v), g4(r_rank), g4(r_cmp), rank0)
                dve.tensor_scalar(r_sel, r_rank, 2.0, None, ALU.is_lt)
                dve.drain()
                dve.tensor_tensor(r_cmp, r_sel, r_v, ALU.mult)
                dve.drain()
                dve.tensor_reduce(r_gs, g4(r_cmp), AX.X, ALU.add)
                dve.drain()
                rank_of_four(g4(r_gs), g4(r_gr), g4(r_best), rank0[:, 0:T, :])
                dve.tensor_scalar(r_best, r_gr, 1.0, None, ALU.is_lt)
                dve.drain()
                dve.tensor_tensor(g4(r_sel), g4(r_sel), r_best.unsqueeze(2).broadcast_to([P, 8, 4]), ALU.mult)
                dve.drain()
                dve.tensor_tensor(r_sel, r_sel, score, ALU.mult)
                dve.drain()
                dve.tensor_reduce(r_den[:, 0:T], tg(r_sel), AX.X, ALU.add)
                dve.drain()
                dve.reciprocal(r_den[:, 2:2 + T], r_den[:, 0:T])
                dve.drain()
                dve.scalar_tensor_tensor(out=tg(r_gate), in0=tg(r_sel), scalar=A_POW / SUM_POW,
                                         in1=r_den[:, 2:2 + T].unsqueeze(2).broadcast_to([P, T, NE]),
                                         op0=ALU.mult, op1=ALU.mult)
                dve.drain()

                def weigh(b, j):
                    dve.wait_ge(sig("moe_silu"), NE * layer + b + 1 + j * 2)
                    for t in range(T):
                        ins = dve.scalar_tensor_tensor(out=h_tok[:, b, t, :], in0=ps[:, 4 + 2 * b + t, DE:2 * DE],
                                                       scalar=r_gate[:, bass.ds(2 * j + b + t * NE, 1)],
                                                       in1=e_silu[:, b, t, :], op0=ALU.mult, op1=ALU.mult)
                    ins.then_inc(sig("moe_h"), 1)

                def h_low(b, j):
                    dve.wait_ge(sig("moe_hT_hi"), NE * layer + 1 + b + j * 2)
                    dve.tensor_tensor(hT_lo[:, b, :], ps[:, 4 + 2 * b, :], hT_hi[:, b, :], ALU.subtract)\
                        .then_inc(sig("moe_hT"), 1)

                def pair(j, last):
                    weigh(0, j)
                    w_split(n0, 2, j)
                    h_low(0, j)
                    if not last:
                        w_split(n0 + 3, 0, j)
                    weigh(1, j)
                    if not last:
                        w_split(n0 + 3, 1, j)
                    h_low(1, j)

                with dve.Fori(0, NE // 2 - 1) as j:
                    pair(j, False)
                pair(NE // 2 - 1, True)

            w_split(MOE0, 0, 0)
            layer_norm(0)
            experts(0, MOE0, 6)
            layer_norm(1)
            turned(dve, scaled, 7, None, "xp_dve", 1, 1)
            for i, (dst, scale) in enumerate(((q2T, 0.125), (k2T, 1.0), (v2, 1.0))):
                dve.wait_ge(sig("w_used"), SBI0 + 2 * i + 2)
                d = dst[:, 0, 4:8, :] if i < 2 else dst[:, 0, :, 512:]
                src = ps[:, 2:4, :].rearrange("p b (c s) -> p (b c) s", c=2) if i < 2 else ps[:, 2:4, :]
                scaled(d, src, scale).then_inc(sig("qkv_dve"), 1)

            mask2 = strict3.unsqueeze(1).broadcast_to([P, 2, 384])

            def sb_clip(m):
                dve.wait_ge(sig("sb_z"), m + 1)
                if m >= SBN:
                    dve.wait_ge(sig("sb_pv"), m - SBN + 1)
                z, b = sb_zt[m % SBN], 2 * (m % 2)
                dve.tensor_scalar(z, ps[:, b:b + 2, 0:384], SB_CLIP, -SB_CLIP, ALU.min, ALU.max)
                dve.drain()
                dve.tensor_scalar(sb_e[m % SBN], z, LN_TOP, None, ALU.min).then_inc(sig("sb_zc"), 1)
                dve.tensor_scalar(sb_h[m % SBN], z, -LN_TOP, 0.0, ALU.add, ALU.max)

            def sb_sp(m):
                dve.wait_ge(sig("sb_ln"), m + 1)
                v = sb_l[m % SBN]
                dve.drain()
                dve.tensor_tensor(v, v, sb_h[m % SBN], ALU.add)
                dve.drain()
                dve.tensor_tensor(v, v, mask2, ALU.mult).then_inc(sig("sb_sp"), 1)

            def sb_att(m):
                dve.wait_ge(sig("sb_r"), m + 1)
                v = sb_e[m % SBN]
                dve.tensor_tensor(v, sb_zt[m % SBN], ps[:, 4:6, 0:384], ALU.subtract).then_inc(sig("sb_d"), 1)

            def sb_mask(m):
                dve.wait_ge(sig("sb_exp"), m + 1)
                v = sb_e[m % SBN]
                dve.tensor_tensor(v, v, mask2, ALU.mult).then_inc(sig("sb_att"), 1)

            def sb_o(m):
                dve.wait_ge(sig("sb_pv"), m + 1)
                dve.tensor_copy(x_norm[:, :, P * m:P * m + P], ps[:, 6 + m % 2, 0:S].rearrange("p (t n) -> p t n", t=T))\
                    .then_inc(sig("sb_o"), 1)

            dve.wait_ge(sig("x_full"), 3)
            for i in range(H2 // 2 + 4):
                staged(i, (sb_att, 2), (sb_sp, 1), (sb_clip, 0), (sb_mask, 3), (sb_o, 4))
            both_tiles()
            turned(dve, scaled, 8, None, "xp_dve", 1)
            w_split(MOE1, 0, 0)
            layer_norm(2)
            experts(1, MOE1, 9)
            layer_norm(3)
            dve.wait_ge(sig("ld_gb"), 16 + 32 * 4)
            for t in range(T):
                if t:
                    dve.wait_ge(sig("xn1_ready"), 11)
                dve.drain()
                dve.tensor_tensor(x_norm[:, t, :], x_norm[:, t, :], ln_gb[:, 0, :], ALU.mult)
                dve.drain()
                dve.tensor_tensor(x_tok[:, t, :], x_norm[:, t, :], ln_gb[:, 1, :], ALU.add)\
                    .then_inc(sig("out_ready"), 1)

_SHAPES_IN = ("x", "p", "positions", "w_in", "w_uq", "w_ukv", "w_pool", "ssd_dt_bias", "ssd_a_log", "ssd_d",
              "lru_w_a", "lru_w_i", "w_branch", "w_out", "w_ff1", "w_ff2", "w_ple_gate", "w_ple",
              "rel_table_2", "router_w_2", "router_b_2", "ln1_g_2", "ln1_b_2", "ln2_g_2", "ln2_b_2",
              "exp_w_gate_2", "exp_w_up_2", "exp_w_down_2", "dil_w_in_2", "dil_w_out_2", "sb_w_in_2",
              "sb_w_out_2") + tuple(n for n, _ in PARAM_ROWS)


def kernel(**inputs):
    import concourse.bacc as bacc
    from concourse.bass_utils import run_bass_kernel_spmd

    nc = bacc.Bacc("TRN2", target_bir_lowering=False, num_devices=1)
    arrays, aps = {}, {}
    named = [(n, inputs[n]) for n in _SHAPES_IN] + list(constants().items())
    for name, value in named:
        if name == "positions":
            value = np.asarray(value).reshape(T, P).T
        v = np.ascontiguousarray(value)
        arrays["in_" + name] = v
        aps[name] = nc.dram_tensor("in_" + name, v.shape, mybir.dt.from_np(v.dtype), kind="ExternalInput").ap()
    out = nc.dram_tensor("out_0", (1, S, D), F32, kind="ExternalOutput").ap()
    build(nc, aps, out)
    r = run_bass_kernel_spmd(nc, [arrays], core_ids=[0])
    return r.results[0]["out_0"]
```

```python
from contextlib import ExitStack

import numpy as np
import concourse.bass as bass
from concourse import mybir

F32 = mybir.dt.float32
BF16 = mybir.dt.bfloat16
F16 = mybir.dt.float16
I32 = mybir.dt.int32
ALU = mybir.AluOpType
ACT = mybir.ActivationFunctionType
AX = mybir.AxisListType

P = 128
S = 256
T = S // P
D = 1024
KD = D // P
MIX = 512
KM = MIX // P
EPS = 1e-6
LN_EPS = 1e-5
QL, KVL, ROPE, NOPE = 384, 256, 32, 64
MH = 8
QKD = NOPE + ROPE
MLA_SCALE = float(QKD) ** -0.5
XBC = 768
KX = XBC // P
CONV = 4
NE = 16
DE = 256
H2 = 16
HD = 64
ALPHA = 4.0 ** 0.25
SB_CLIP = 60.0
LN_TOP = 40.0
NEG = -1e30
W_POW, A_POW = 2.0 ** 8, 2.0 ** 3
SUM_POW = W_POW * A_POW
H_POW = 4.0
RING = 3
SLOT = 4096

FF0, DIL0, DOUT0, MOE0, SBI0, SBO0, MOE1 = 24, 43, 61, 63, 87, 93, 95
SPLIT = ((FF0, FF0 + 16), (DIL0, DOUT0), (MOE0, SBI0), (SBI0, SBO0), (MOE1, MOE1 + 24))

C_Q, C_KV, C_POOL, C_Z, C_XBC, C_DT, C_LG, C_LX, C_GATE = 0, 384, 672, 1184, 1696, 2464, 2472, 2984, 3496

PARAM_ROWS = (("g_mix", 8), ("q_norm", 3), ("kv_norm", 2), ("pool_scale", 4), ("ssd_conv_w", 24),
              ("ssd_conv_b", 6), ("ssd_norm", 4), ("lru_conv_w", 16), ("lru_conv_b", 4),
              ("lru_b_a", 4), ("lru_b_i", 4), ("lru_lambda", 4), ("g_mlp", 8), ("g_ple", 8), ("g_final", 8))
LN_ROWS = (("ln1_g_2", 0), ("ln1_b_2", 0), ("ln2_g_2", 0), ("ln2_b_2", 0), ("ln1_g_2", 1), ("ln1_b_2", 1))
PROW = {}
_at = 0
for _name, _n in PARAM_ROWS:
    PROW[_name] = _at
    _at += _n
NPROW = _at
NCOL = NPROW + 8 * len(LN_ROWS)


def constants():
    i = np.arange(P)
    f = np.float32
    eye = np.eye(P, dtype=f)
    flip = eye[::-1].copy()
    tri = (i[:, None] <= i[None, :]).astype(f)
    ones = np.ones((P, P), f)
    strict = (i[:, None] < i[None, :]).astype(f)
    low = (i[:, None] >= i[None, :]).astype(f)
    cmask = np.where(i[None, :] <= i[:, None], f(0), f(NEG)).astype(f)
    mats = np.concatenate([eye, flip, tri, ones, tri, strict, ones, strict, low, cmask], axis=1)
    t = np.arange(S)
    band = []
    for w in (2, 4, 8, 16):
        cnt = np.minimum(t + 1, w)
        m = ((t[:, None] <= t[None, :]) & (t[:, None] > t[None, :] - w)) / cnt[None, :] - np.eye(S)
        band.append(np.concatenate([m[:P, :], m[P:, P:]], axis=1).astype(f))
    band = np.concatenate(band, axis=1)
    dist = 255 - np.arange(384)
    n = np.maximum(dist, 0)
    logf = (np.log(np.maximum(n, 1).astype(f) / f(16)) / f(np.log(2048 / 16))).astype(f)
    large = np.minimum(16 + (logf * f(16)).astype(np.int32), 31)
    bucket = np.where(n < 16, n, large)
    onehot = (np.arange(32)[:, None] == bucket[None, :]).astype(f)
    d = 128 + i[:, None] - np.arange(S)[None, :]
    rel = np.stack([(d >= 0) & (d <= 128), (d >= 0) & (d % 4 == 0), (d >= 0) & (d % 16 == 0)], 1)
    relmask = np.where(rel, f(0), f(NEG)).astype(f)
    inv = (f(1) / (f(10000.0) ** (np.arange(0, ROPE, 2).astype(f) / f(ROPE)))).astype(f)
    rank0 = np.tile(np.array([3, 2, 1, 0], f), 8)
    rows = np.concatenate([inv, rank0]).reshape(1, 48).repeat(P, 0).astype(f)
    return {"c_mats": mats, "c_band": band.astype(f), "c_onehot": onehot,
            "c_relmask": relmask.reshape(P, 3 * S), "c_rows": rows}


def build(nc, a, out):
    ctx = ExitStack()
    with ctx:
        sems = {}

        def sig(name):
            if name not in sems:
                sems[name] = ctx.enter_context(nc.semaphore(name))
            return sems[name]

        def sb(name, shape, dt=F32):
            return ctx.enter_context(nc.sbuf_tensor(name, shape, dt))

        w_ring = sb("w_ring", [P, RING, SLOT])
        x_tok = sb("x_tok", [P, T, D])
        x_norm = sb("x_norm", [P, T, D])
        actT = sb("actT", [P, KD, S])
        ln_gb = sb("ln_gb", [P, 2, D])
        mats = sb("mats", [P, 10, P])
        crow = sb("crow", [P, 48])
        brow = sb("brow", [P, 24 + NE])
        pcol = sb("pcol", [P, NCOL])
        stats = sb("stats", [P, 64])
        lru_w = sb("lru_w", [P, 2, KM, P])
        pool_w = sb("pool_w", [P, KM, P])
        ARENA = 28350
        arena = sb("arena", [P, ARENA])
        ps = ctx.enter_context(nc.psum_tensor("ps", [P, 8, 512], F32))

        ident, flip = mats[:, 0, :], mats[:, 1, :]
        tri3 = mats[:, 2:5, :].rearrange("p a b -> p (a b)")
        tri, ones = mats[:, 2, :], mats[:, 3, :]
        strict3 = mats[:, 5:8, :].rearrange("p a b -> p (a b)")
        low, cmask = mats[:, 8, :], mats[:, 9, :]
        inv_freq, rank0 = crow[:, 0:16], crow[:, 16:48].rearrange("p (g e) -> p g e", e=4)

        at = [0]

        def take(n):
            at[0] += n
            assert at[0] <= ARENA, at[0]
            return arena[:, at[0] - n:at[0]]

        gates = take(T * 4 * D).rearrange("p (t n) -> p t n", t=T)
        u_cqkv = take(T * 672)
        cq = u_cqkv[:, 0:T * QL].rearrange("p (t n) -> p t n", t=T)
        ckv = u_cqkv[:, T * QL:T * 672].rearrange("p (t n) -> p t n", t=T)
        y_ssd = u_cqkv[:, 0:T * MIX].rearrange("p (t n) -> p t n", t=T)
        u_up = take(T * MIX)
        up = u_up.rearrange("p (t n) -> p t n", t=T)
        lru_i = u_up.rearrange("p (c s) -> p c s", c=KM)
        z_silu = take(T * MIX).rearrange("p (t n) -> p t n", t=T)
        u_xb = take(KX * (S + 3))
        xbT = u_xb.rearrange("p (c s) -> p c s", c=KX)
        lru_a = u_xb[:, 0:KM * S].rearrange("p (c s) -> p c s", c=KM)
        u_xbS = take(KX * S)
        xbS = u_xbS.rearrange("p (c s) -> p c s", c=KX)
        xdt = u_xbS[:, 0:T * MIX].rearrange("p (t n) -> p t n", t=T)
        lru_g = take(KM * S).rearrange("p (c s) -> p c s", c=KM)
        u_lx = take(KM * (S + 3))
        lxT = u_lx.rearrange("p (c s) -> p c s", c=KM)
        lru_r = u_lx[:, 0:KM * S].rearrange("p (c s) -> p c s", c=KM)
        xcT = take(KM * S).rearrange("p (c s) -> p c s", c=KM)
        ycT = xcT
        u_cT = take(5 * S)
        cT = u_cT.rearrange("p (c s) -> p c s", c=5)
        cbm = u_cT[:, 0:2 * 384].rearrange("p (g s) -> p g s", g=2)
        lru_t = u_cT[:, 0:KM * S].rearrange("p (c s) -> p c s", c=KM)
        u_qk = take(2 * T * MH * QKD)
        q_tok = u_qk[:, 0:T * MH * QKD].rearrange("p (t h d) -> p t h d", t=T, h=MH)
        k_tok = u_qk[:, T * MH * QKD:].rearrange("p (t h d) -> p t h d", t=T, h=MH)
        dm = u_qk.rearrange("p (h s) -> p h s", h=MH)
        u_v = take(T * MIX)
        v_tok = u_v.rearrange("p (t h d) -> p t h d", t=T, h=MH)
        yaT = u_v.rearrange("p (c s) -> p c s", c=KM)
        probs = take(384)
        probsT = take(384)
        o_mla = take(T * MIX).rearrange("p (t n) -> p t n", t=T)
        u_dT = take(KM * S)
        dT = u_dT.rearrange("p (c s) -> p c s", c=KM)
        ybT = dT
        xs_tok = take(T * MIX).rearrange("p (t n) -> p t n", t=T)
        rope_cs = take(2 * T * 16).rearrange("p (a t f) -> p a t f", a=2, t=T)
        rope_tmp = take(4 * T * MH * 16).rearrange("p (a n) -> p a n", a=4)
        qT = x_norm[:, :, :].rearrange("p t n -> p (t n)").rearrange("p (h s) -> p h s", h=MH)
        kT = x_tok[:, :, :].rearrange("p t n -> p (t n)").rearrange("p (h s) -> p h s", h=MH)
        band = ln_gb[:, :, :].rearrange("p a n -> p (a n)")[:, 0:4 * 384].rearrange("p (g s) -> p g s", g=4)
        prow = probs
        dt_tok = stats[:, 0:16].rearrange("p (t h) -> p t h", t=T)
        a_tok = stats[:, 16:32].rearrange("p (t h) -> p t h", t=T)
        acs = stats[:, 32:48].rearrange("p (t h) -> p t h", t=T)
        ms, rstd, neghalf = stats[:, 48:52], stats[:, 52:56], stats[:, 56:60]
        mx = stats[:, 60:62]
        p_tok = o_mla.rearrange("p t n -> p (t n)")[:, 0:T * DE].rearrange("p (t n) -> p t n", t=T)
        pT = o_mla.rearrange("p t n -> p (t n)")[:, T * DE:2 * T * DE].rearrange("p (c s) -> p c s", c=2)
        pos_i = sb("pos_i", [P, T], I32)
        router_w = sb("router_w", [P, KD, NE])
        bn_part = sb("bn_part", [P, T, 2, 6])
        bn_mv = sb("bn_mv", [P, T, 2])
        mx4 = sb("mx4", [P, 4])
        ms_part = sb("ms_part", [P, 2, T])
        pos_f = sb("pos_f", [P, T])
        zero16 = sb("zero16", [P, 640], BF16)
        den = sb("den", [P, 8])
        sp_v, sp_a, sp_e = (sb(f"softplus_{n}", [P, 20]) for n in "vae")
        decay8 = sb("decay8", [P, 4])
        a_head = sb("a_head", [P, MH])
        zc_mask = sb("zc_mask", [P, S])

        half = lambda v: v.bitcast(F16)

        def operands(bufs, act_parts):
            parts = [half(v).rearrange("p (k n) -> p k n", n=2 * S) for v in act_parts]
            return [(half(h), half(l)) for h, l in bufs], parts, [v[:, k, :] for v in parts for k in range(v.shape[1])]

        hid_hi, hid_lo = (half(u).rearrange("p (k s) -> p k s", s=S) for u in (arena[:, 0:4096], arena[:, 4096:8192]))
        hid_tmp = [arena[:, o:o + 1024] for o in (12288, 13312)]
        ff_w, ff_parts, ff_a = operands([(arena[:, 8192 + o:10240 + o], arena[:, 18432 + o:20480 + o]) for o in (0, 2048)],
                                        [arena[:, 16384:18432]])
        DQ = 23296
        dil_w, dil_parts, dil_a = operands(
            [(arena[:, DQ:DQ + 2048], arena[:, DQ + 2048:DQ + 4096]),
             (x_norm[:, :, :].rearrange("p t n -> p (t n)"), ln_gb[:, :, :].rearrange("p t n -> p (t n)"))],
            [lru_w[:, :, :, :].rearrange("p i c n -> p (i c n)"), pool_w[:, :, :].rearrange("p g n -> p (g n)"),
             arena[:, DQ + 4096:DQ + 4608]])
        sbq_w, sbq_parts, sbq_a = operands([(arena[:, 8192:10240], arena[:, 10240:12288]),
                                            (arena[:, 14400:16448], arena[:, 16448:18496]),
                                            (arena[:, 6144:8192], arena[:, 12288:14336])], [arena[:, 2048:4096]])
        sbq_w = [sbq_w[i] for i in (0, 2, 0, 1, 0, 1)]
        dil_w = 3 * dil_w

        at[0] = 0
        u_q2 = take(3 * KD * S)
        q2T = u_q2.rearrange("p (g c s) -> p g c s", g=3, c=KD)
        k2T = take(3 * KD * S).rearrange("p (g c s) -> p g c s", g=3, c=KD)
        v2 = take(3 * T * D).rearrange("p (g t n) -> p g t n", g=3, t=T)
        bias_h = take(H2 * S).rearrange("p (h s) -> p h s", h=H2)
        relmask = take(3 * S).rearrange("p (g s) -> p g s", g=3)
        bm = take(2 * 3 * S).rearrange("p (b g s) -> p b g s", b=2, g=3)
        u_e = take(2 * 1152)
        e_dil = u_e.rearrange("p (b n) -> p b n", b=2)
        eT_dil = take(1152)
        eT_two = ((eT_dil[:, 0:384], eT_dil[:, 384:1152]),
                  (pool_w[:, :, :].rearrange("p g n -> p (g n)")[:, 0:384],
                   lru_w[:, :, :, :].rearrange("p i c n -> p (i c n)")[:, 0:768]))
        rel_row = u_e[0:H2, 1152:1536]
        rel_tab = eT_dil[0:32, 0:H2]
        rel_spread = v2.rearrange("p g t n -> p (g t n)")[:, 0:H2 * S].rearrange("p (h s) -> p h s", h=H2)
        onehot = eT_dil[0:32, 16:400]
        SBN = 4
        HIGH = 14400
        sb_sets = tuple(arena[:, HIGH + 3072 * i:HIGH + 3072 * (i + 1)] for i in range(SBN))
        sb_zt, sb_e, sb_l, sb_h = ([u[:, 768 * i:768 * i + 768].rearrange("p (h s) -> p h s", h=2) for u in sb_sets]
                                   for i in range(4))
        at[0] = 0
        aT_hi, aT_lo = (half(take(KD * S // 2)).rearrange("p (k s) -> p k s", k=KD) for _ in range(2))
        e_silu = take(2 * T * DE).rearrange("p (b t n) -> p b t n", b=2, t=T)
        h_tok = take(2 * T * DE).rearrange("p (b t n) -> p b t n", b=2, t=T)
        hT_hi, hT_lo = (half(take(S * DE // P)).rearrange("p (b n) -> p b n", b=2) for _ in range(2))
        score = take(T * NE)
        r_v, r_rank, r_cmp, r_sel, r_gate = (take(T * NE) for _ in range(5))
        r_gs = take(8)
        r_gr = take(8)
        r_best = take(8)
        r_den = take(4)
        at[0] = HIGH
        w_hi, w_lo = (half(take(3 * SLOT // 2)).rearrange("p (b n) -> p b n", b=3) for _ in range(2))
        rel_dram = nc.dram_tensor("rel_rows_dram", [H2, 384], F32, kind="Internal").ap()
        block = ctx.enter_context(nc.Block())

        EVAC, _n = [], {"A": 0, "D": 0}
        for e in "ADAADDAD" + "A" * 8:
            _n[e] += 1
            EVAC.append((sig("out_by_act" if e == "A" else "out_by_dve"), _n[e]))

        w_in = a["w_in"].rearrange("o (k p) n -> (o p) k n", p=P)

        def landed(eng, n):
            eng.wait_ge(sig(f"w_landed{n % RING}"), 32 * (n // RING + 1))

        def norm_count(n, t):
            return 3 + T * (n - 3) + t + 1

        def split_index(n):
            if not any(a <= n < b for a, b in SPLIT):
                return None
            return sum(min(n, b) - a for a, b in SPLIT if a < n)

        def staged(i, *stages):
            for stage, behind in stages:
                if 0 <= i - behind < H2 // 2:
                    stage(i - behind)

        def bcast(ap, n, offset=0):
            return bass.AP(tensor=ap.tensor, offset=offset, ap=[[0, P], [1, n]])

        @block.sync
        def _(sp):
            def slot_free(n):
                m = n - RING
                if m >= 0:
                    q = split_index(m)
                    if q is None:
                        sp.wait_ge(sig("w_used"), m + 1)
                    else:
                        sp.wait_ge(sig("w_lo"), q + 1)

            def slot(n, pairs):
                slot_free(n)
                for o, k, c, src in pairs:
                    sp.dma_start(w_ring[:, n % RING, o:o + k * c].rearrange("p (k n) -> p k n", k=k), src)\
                        .then_inc(sig(f"w_landed{n % RING}"), 16)

            def halves(n, w, c0, c):
                h = KD // 2
                slot(n, [(0, h, c, w[:, 0:h, c0:c0 + c]), (h * c, h, c, w[:, h:KD, c0:c0 + c])])

            def rows4(n, w):
                slot(n, [(0, 2, D, w[:, 0:2, :]), (2 * D, 2, D, w[:, 2:4, :])])

            sp.dma_start(x_norm[:, :, :], a["x"].rearrange("o (t p) d -> (o p) t d", p=P)).then_inc(sig("ld_x"), 16)
            sp.dma_start(mats[:, :, :].rearrange("p a b -> p (a b)"), a["c_mats"]).then_inc(sig("ld_mats"), 16)
            sp.dma_start(prow[0:NPROW, 0:P], a["p_rows"][0:NPROW, :]).then_inc(sig("ld_params"), 16)
            sp.dma_start(prow[0:NCOL - NPROW, P:2 * P], a["p_rows"][NPROW:NCOL, :]).then_inc(sig("ld_params"), 16)
            halves(0, w_in, C_Q, 384)
            sp.dma_start(crow[:, :], a["c_rows"]).then_inc(sig("ld_rows"), 16)
            sp.dma_start(brow[:, :], bcast(a["p_brow"], 24 + NE)).then_inc(sig("ld_rows"), 16)
            sp.dma_start(pos_i[:, :], a["positions"]).then_inc(sig("ld_rows"), 16)
            halves(1, w_in, C_KV, 288)
            halves(2, w_in, C_POOL, 512)
            sp.dma_start(band, a["c_band"].rearrange("p (g s) -> p g s", g=4)).then_inc(sig("ld_pool"), 16)
            sp.dma_start(pool_w[:, :, :], a["w_pool"].rearrange("o g c d -> (o c) g d")).then_inc(sig("ld_pool"), 16)
            sp.wait_ge(sig("lru_zeroed"), 1)
            for i, name in enumerate(("lru_w_a", "lru_w_i")):
                w = a[name].rearrange("o (c b) i j -> (o b) i c j", b=2)
                for b in range(2):
                    sp.dma_start(lru_w[64 * b:64 * b + 64, i, :, 64 * b:64 * b + 64], w[b])\
                        .then_inc(sig("ld_lru"), 16)
            halves(3, w_in, C_Z, 512)
            halves(4, w_in, C_XBC, 384)
            w = a["w_uq"].rearrange("o (k p) n -> (o p) k n", p=P)
            slot(5, [(0, 2, 768, w[:, 0:2, :]), (1536, 1, 768, w[:, 2:3, :])])
            halves(6, w_in, C_XBC + 384, 392)
            w = a["w_ukv"].rearrange("o (k p) n -> (o p) k n", p=P)
            slot(7, [(0, 1, D, w[:, 0:1, :]), (D, 1, D, w[:, 1:2, :])])
            halves(8, w_in, C_LG, 512)
            halves(9, w_in, C_LX, 512)
            for i in range(8):
                halves(10 + i, w_in, C_GATE + 512 * i, 512)
            for i, b in enumerate((1, 0, 3, 2)):
                rows4(18 + i, a["w_branch"][0, b].rearrange("(k p) n -> p k n", p=P))
            sp.wait_ge(sig("mla_scores"), MH)
            sp.dma_start(x_tok[:, :, :], a["x"].rearrange("o (t p) d -> (o p) t d", p=P)).then_inc(sig("ld_x"), 16)
            sp.wait_ge(sig("pool_d"), 1)
            sp.dma_start(ln_gb[:, 0, :], bcast(a["g_final"], D)).then_inc(sig("ld_gb"), 16)
            w = a["w_out"].rearrange("o (k p) n -> (o p) k n", p=P)
            halves(22, w, 0, 512)
            halves(23, w, 512, 512)
            sp.wait_ge(sig("mla_oT_pe"), KM)
            sp.dma_start(p_tok, a["p"].rearrange("l o (t p) d -> (l o p) t d", p=P)).then_inc(sig("ld_p"), 16)
            w = a["w_ff1"].rearrange("o (k p) n -> (o p) k n", p=P)
            for i in range(8):
                halves(24 + i, w, 512 * i, 512)
            sp.wait_ge(sig("branch"), 4)
            sp.dma_start(relmask, a["c_relmask"].rearrange("p (g s) -> p g s", g=3)).then_inc(sig("ld_rel"), 16)
            sp.dma_start(rel_tab, a["rel_table_2"]).then_inc(sig("ld_rel"), 16)
            sp.dma_start(onehot, a["c_onehot"]).then_inc(sig("ld_rel"), 16)
            sp.dma_start(router_w[:, :, :], a["router_w_2"].rearrange("(k p) e -> p k e", p=P)).then_inc(sig("ld_router"), 16)
            for i in range(8):
                rows4(32 + i, a["w_ff2"][0, 512 * i:512 * i + 512, :].rearrange("(k p) n -> p k n", p=P))
            sp.wait_ge(sig("rel_row"), 1)
            sp.dma_start(rel_dram, rel_row).then_inc(sig("st_rel"), 16)
            sp.wait_ge(sig("st_rel"), 16)
            spread = bass.AP(tensor=rel_dram.tensor, offset=0, ap=[[1, P], [384, H2], [1, S]])
            sp.dma_start(rel_spread, spread).then_inc(sig("ld_spread"), 16)

            w = a["w_ple"].rearrange("o (k p) n -> (o p) k n", p=P)
            slot(40, [(0, 1, D, w[:, 0:1, :]), (D, 1, D, w[:, 1:2, :])])
            w = a["w_ple_gate"].rearrange("o (k p) n -> (o p) k n", p=P)
            halves(41, w, 0, 512)
            halves(42, w, 512, 512)
            def slot_g(n, pairs):
                for dst, src in pairs:
                    sp.dma_start(dst, src).then_inc(sig(f"w_landed{n % RING}"), 16)

            w = a["dil_w_in_2"].rearrange("o (k p) n -> (o p) k n", p=P)
            def dil_group(g):
                for s in range(6):
                    n = DIL0 + s
                    if isinstance(g, int):
                        slot_free(n)
                    else:
                        sp.wait_ge(sig("w_lo"), split_index(DIL0) + s - 2 + g * 6)
                    dst = w_ring[:, n % RING, :].rearrange("p (k n) -> p k n", k=KD)
                    slot_g(n, [(dst[:, kk:kk + 4, :], w[:, kk:kk + 4, bass.ds(g * 3 * D + 512 * s, 512)])
                               for kk in (0, 4)])

            dil_group(0)
            with sp.Fori(1, 3) as g:
                dil_group(g)

            def gb(m):
                layer, name = m // 2, ("ln1", "ln2")[m % 2]
                sp.wait_ge(sig("x_full"), m + 1)
                sp.dma_start(ln_gb[:, 0, :], bcast(a[name + "_g_2"], D, layer * D)).then_inc(sig("ld_gb"), 16)
                sp.dma_start(ln_gb[:, 1, :], bcast(a[name + "_b_2"], D, layer * D)).then_inc(sig("ld_gb"), 16)

            def experts(layer, n0):
                wg = a["exp_w_gate_2"][layer].rearrange("e (k p) n -> p e k n", p=P)
                wu = a["exp_w_up_2"][layer].rearrange("e (k p) n -> p e k n", p=P)
                wd = a["exp_w_down_2"][layer].rearrange("e (k p) n -> p e k n", p=P)

                def pair(j):
                    for b in range(3):
                        n = n0 + b
                        if isinstance(j, int):
                            slot_free(n)
                        else:
                            sp.wait_ge(sig("w_lo"), split_index(n0) + b - 2 + j * 3)
                        if b < 2:
                            dst = w_ring[:, n % RING, :].rearrange("p (o k n) -> p o k n", o=1, k=KD)
                            slot_g(n, [(dst[:, :, :, 0:DE], wg[:, bass.ds(2 * j + b, 1), :, :]),
                                       (dst[:, :, :, DE:2 * DE], wu[:, bass.ds(2 * j + b, 1), :, :])])
                        else:
                            dst = w_ring[:, n % RING, :].rearrange("p (o k n) -> p o k n", o=2, k=2)
                            slot_g(n, [(dst[:, i:i + 1, :, :], wd[:, bass.ds(2 * j + i, 1), :, :]) for i in range(2)])

                pair(0)
                with sp.Fori(1, NE // 2) as j:
                    pair(j)

            w = a["dil_w_out_2"].rearrange("o (k p) n -> (o p) k n", p=P)
            halves(DOUT0, w, 0, 512)
            halves(DOUT0 + 1, w, 512, 512)
            sp.wait_ge(sig("w_used"), DOUT0)
            gb(0)
            experts(0, MOE0)
            gb(1)
            w = a["sb_w_in_2"].rearrange("o (k p) n -> (o p) k n", p=P)
            for s in range(6):
                halves(SBI0 + s, w, 512 * s, 512)
            gb(2)
            w = a["sb_w_out_2"].rearrange("o (k p) n -> (o p) k n", p=P)
            halves(SBO0, w, 0, 512)
            halves(SBO0 + 1, w, 512, 512)
            experts(1, MOE1)
            gb(3)
            for i in range(2 * T):
                t, c = i // 2, slice(512 * (i % 2), 512 * (i % 2) + 512)
                sp.wait_ge(sig("out_ready"), i + 1)
                sp.dma_start(out[0, t * P:(t + 1) * P, c], x_tok[:, t, c]).then_inc(sig("stored"), 16)
            sp.wait_ge(sig("stored"), 16 * 2 * T)

        @block.gpsimd
        def _(pool):
            pool.memset(neghalf, -0.5)
            pool.memset(zero16[:, :], 0.0)
            pool.memset(lru_w[:, :, :, :], 0.0)
            pool.drain()
            pool.memset(xbT[:, :, 0:CONV - 1], 0.0)
            pool.memset(lxT[:, :, 0:CONV - 1], 0.0).then_inc(sig("lru_zeroed"), 1)

            def rsqrt(i, n):
                pool.wait_ge(sig("ms_ready"), i + 1)
                pool.tensor_tensor(rstd[:, 0:n], ms[:, 0:n], neghalf[:, 0:n], ALU.pow).then_inc(sig("rstd_ready"), 1)

            def rsqrt_tiles(n):
                for t in range(T):
                    pool.wait_ge(sig("ms_ready"), norm_count(n, t))
                    pool.tensor_tensor(rstd[:, t:t + 1], ms[:, t:t + 1], neghalf[:, t:t + 1], ALU.pow)\
                        .then_inc(sig("rstd_ready"), 1)

            rsqrt(0, 2)
            rsqrt(1, 4)
            rsqrt(2, 2)
            for n in range(3, 6):
                rsqrt_tiles(n)

            def full(norm, bias):
                pool.wait_ge(sig("xn0_ready"), norm)
                pool.wait_ge(sig("xn1_ready"), norm)
                for t in range(T):
                    ins = pool.tensor_tensor(x_tok[:, t, :], x_norm[:, t, :], ln_gb[:, 0, :], ALU.mult)
                if bias:
                    pool.drain()
                    for t in range(T):
                        ins = pool.tensor_tensor(x_tok[:, t, :], x_tok[:, t, :], ln_gb[:, 1, :], ALU.add)
                ins.then_inc(sig("x_full"), 1)

            pool.wait_ge(sig("ld_gb"), 16)
            full(5, False)
            pool.wait_ge(sig("bias_h"), 2)
            pool.wait_ge(sig("ld_rel"), 16 * 3)
            pool.wait_ge(sig("w_used"), DOUT0)
            for h in range(H2):
                if h >= 2:
                    pool.wait_ge(sig("dil_max"), h - 1)
                pool.tensor_tensor(bm[:, h % 2, :, :], relmask, bias_h[:, h:h + 1, :].broadcast_to([P, 3, S]), ALU.add)\
                    .then_inc(sig("bm"), 1)
            for m in range(4):
                rsqrt_tiles(6 + m)
                if m < 3:
                    pool.wait_ge(sig("ld_gb"), 16 + 32 * (m + 1))
                    full((7, 8, 10)[m], True)

        def pcols(name, i):
            c = PROW[name] + i
            return pcol[:, c:c + 1]

        @block.tensor
        def _(pe):
            def w_slot(n, k):
                return w_ring[:, n % RING, :].rearrange("p (k n) -> p k n", k=k) if k else w_ring[:, n % RING, :]

            def transposes(i, src, chunks, sem_name, first_bank=4):
                for k in range(chunks):
                    for t in range(T):
                        o = (k % 2) * 256 + t * P
                        ins = pe.transpose(ps[:, first_bank + k // 2, o:o + P], src[:, t, k * P:(k + 1) * P], ident)
                    ins.then_inc(sig(sem_name), 1)

            def act_transposes(i):
                if i:
                    pe.wait_ge(sig("xp_act"), 4 * i)
                    pe.wait_ge(sig("xp_dve"), 4 * i)
                for t in range(T):
                    pe.wait_ge(sig(f"xn{t}_ready"), i + 1)
                    for k in range(KD):
                        o = (k % 2) * 256 + t * P
                        ins = pe.transpose(ps[:, 4 + k // 2, o:o + P], x_norm[:, t, k * P:(k + 1) * P], ident)
                        if t == T - 1:
                            ins.then_inc(sig("xp_pe"), 1)

            def act_ready(i):
                pe.wait_ge(sig("xp_act"), 4 * i + 4)
                pe.wait_ge(sig("xp_dve"), 4 * i + 4)

            def gemm_tok(n, bank, cols, first=False):
                landed(pe, n)
                w = w_ring[:, n % RING, 0:KD * cols].rearrange("p (k n) -> p k n", k=KD)
                for t in range(T):
                    for k in range(KD):
                        ins = pe.matmul(ps[:, bank + t, 0:cols], actT[:, k, t * P:(t + 1) * P], w[:, k, :],
                                        start=(k == 0), stop=(k == KD - 1))
                    if first and t == 0:
                        ins.then_inc(sig("first_tile"), 1)
                return ins

            def gemm_T(n, bank, cols, chunks):
                landed(pe, n)
                w = w_ring[:, n % RING, 0:KD * cols].rearrange("p (k n) -> p k n", k=KD)
                for c in range(chunks):
                    o = (c % 2) * S
                    for k in range(KD):
                        ins = pe.matmul(ps[:, bank + c // 2, o:o + S], w[:, k, c * P:(c + 1) * P], actT[:, k, :],
                                        start=(k == 0), stop=(k == KD - 1))
                return ins

            def evacuated(g):
                if g >= 2:
                    pe.wait_ge(*EVAC[g - 2])

            pe.wait_ge(sig("ld_mats"), 16)
            pe.wait_ge(sig("ld_params"), 32)
            pe.transpose(ps[:, 0, NPROW:NCOL], prow[0:NCOL - NPROW, P:2 * P], ident[0:NCOL - NPROW, 0:NCOL - NPROW])
            pe.transpose(ps[:, 0, 0:NPROW], prow[0:NPROW, 0:P], ident[0:NPROW, 0:NPROW]).then_inc(sig("params_T"), 1)
            act_transposes(0)
            act_ready(0)
            pe.wait_ge(sig("pcol"), 1)
            g = 0
            for n, cols in ((0, 384), (1, 288), (2, 512), (3, 512)):
                evacuated(g)
                gemm_tok(n, (g % 2) * 2, cols).then_inc(sig("w_used"), 1)
                g += 1
            pe.wait_ge(sig("ld_pool"), 32)
            pe.wait_ge(*EVAC[2])
            for c in range(KM):
                o = (c % 2) * S
                pe.matmul(ps[:, 4 + c // 2, o:o + S], up[:, 0, c * P:(c + 1) * P], band[:, c, 0:S],
                          start=True, stop=False, skip_group_check=True)
                ins = pe.matmul(ps[:, 4 + c // 2, o + P:o + S], up[:, 1, c * P:(c + 1) * P], band[:, c, S:384],
                                start=False, stop=True, skip_group_check=True)
            ins.then_inc(sig("pool_d"), 1)
            evacuated(g)
            gemm_T(4, (g % 2) * 2, 384, 3).then_inc(sig("w_used"), 1)
            g += 1
            pe.wait_ge(sig("dT"), 1)
            pe.wait_ge(sig("mla_normed"), 1)
            for k in range(5):
                src, kk = (cq, k) if k < 3 else (ckv, k - 3)
                for t in range(T):
                    o = (k % 2) * S + t * P
                    ins = pe.transpose(ps[:, 4 + k // 2, o:o + P], src[:, t, kk * P:(kk + 1) * P], ident)
            ins.then_inc(sig("cT_pe"), 1)
            landed(pe, 5)
            pe.wait_ge(sig("cT"), 1)
            w = w_ring[:, 5 % RING, 0:3 * 768].rearrange("p (k n) -> p k n", k=3)
            for t in range(T):
                for h in range(2):
                    for k in range(3):
                        ins = pe.matmul(ps[:, 4 + 2 * t + h, 0:384], cT[:, k, t * P:(t + 1) * P],
                                        w[:, k, h * 384:(h + 1) * 384], start=(k == 0), stop=(k == 2))
            ins.then_inc(sig("w_used"), 1)
            evacuated(g)
            gemm_T(6, (g % 2) * 2, 392, 3)
            w = w_ring[:, 6 % RING, 0:KD * 392].rearrange("p (k n) -> p k n", k=KD)
            for t in range(T):
                for k in range(KD):
                    ins = pe.matmul(ps[:, (g % 2) * 2 + 1, S + 8 * t:S + 8 * t + 8], actT[:, k, t * P:(t + 1) * P],
                                    w[:, k, 384:392], start=(k == 0), stop=(k == KD - 1))
            ins.then_inc(sig("w_used"), 1)
            g += 1
            landed(pe, 7)
            pe.wait_ge(sig("q_out"), 1)
            w = w_ring[:, 7 % RING, 0:2 * D].rearrange("p (k n) -> p k n", k=2)
            for t in range(T):
                for h in range(2):
                    for k in range(2):
                        ins = pe.matmul(ps[:, 4 + 2 * t + h, :], cT[:, 3 + k, t * P:(t + 1) * P],
                                        w[:, k, h * 512:(h + 1) * 512], start=(k == 0), stop=(k == 1))
            ins.then_inc(sig("w_used"), 1)
            evacuated(g)
            gemm_T(8, (g % 2) * 2, 512, 4).then_inc(sig("w_used"), 1)
            g += 1

            def head_turns(src, done):
                for h in range(MH):
                    for t in range(T):
                        o = (h % 2) * S + t * P
                        ins = pe.transpose(ps[0:QKD, 4 + h // 2, o:o + P], src[:, t, h, :], ident)
                ins.then_inc(sig(done), 1)

            pe.wait_ge(sig("q_roped"), 1)
            pe.wait_ge(sig("kv_out"), 1)
            head_turns(q_tok, "qT_pe")
            evacuated(g)
            gemm_T(9, (g % 2) * 2, 512, 4).then_inc(sig("w_used"), 1)
            g += 1
            pe.wait_ge(sig("k_roped"), 1)
            pe.wait_ge(sig("qT"), 1)
            head_turns(k_tok, "kT_pe")

            def mla_score(h):
                if h == 0:
                    pe.wait_ge(sig("kT"), 1)
                else:
                    pe.wait_ge(sig("mla_max"), h)
                pe.matmul(ps[:, 4, 0:P], qT[0:QKD, h, 0:P], kT[0:QKD, h, 0:P], start=True, stop=True)
                pe.matmul(ps[:, 4, P:384], qT[0:QKD, h, P:S], kT[0:QKD, h, :], start=True, stop=True)\
                    .then_inc(sig("mla_scores"), 1)

            def mla_turn(h):
                pe.wait_ge(sig("mla_exp"), h + 1)
                if h:
                    pe.wait_ge(sig("mla_o"), h)
                for j in range(3):
                    ins = pe.transpose(ps[:, 5, j * P:(j + 1) * P], probs[:, j * P:(j + 1) * P], ident)
                ins.then_inc(sig("mla_pT_pe"), 1)

            def mla_out(h):
                pe.wait_ge(sig("mla_pT"), h + 1)
                pe.matmul(ps[:, 5, 384:448], probsT[:, 0:P], v_tok[:, 0, h, :], start=True, stop=True)
                pe.matmul(ps[:, 5, 448:512], probsT[:, P:2 * P], v_tok[:, 0, h, :], start=True, stop=False)
                pe.matmul(ps[:, 5, 448:512], probsT[:, 2 * P:3 * P], v_tok[:, 1, h, :], start=False, stop=True)\
                    .then_inc(sig("mla_pv"), 1)

            def ssd_cb():
                pe.wait_ge(sig("xbS"), 1)
                pe.wait_ge(sig("kT"), 1)
                for gr in range(2):
                    r = slice(64 * gr, 64 * gr + 64)
                    pe.matmul(ps[:, 6 + gr, 0:S], xbS[r, 4, 0:P], xbS[r, 5, :], start=True, stop=True)
                    ins = pe.matmul(ps[:, 6 + gr, S:384], xbS[r, 4, P:S], xbS[r, 5, P:S], start=True, stop=True)
                ins.then_inc(sig("cb_pe"), 1)

            def ssd_xs():
                pe.wait_ge(sig("cbm"), 1)
                for t in range(T):
                    for c in range(KM):
                        ins = pe.transpose(ps[:, 6 + t, c * P:(c + 1) * P], xbS[:, c, t * P:(t + 1) * P], ident)
                ins.then_inc(sig("xs_pe"), 1)

            def ssd_cumsum(half):
                if half == 0:
                    pe.wait_ge(sig("acs"), 1)
                else:
                    pe.wait_ge(sig("dm"), 1)
                for j in range(4):
                    h = 4 * half + j
                    o = (j % 2) * S
                    b = 6 + j // 2
                    pe.matmul(ps[:, b, o:o + S], a_tok[:, 0, h:h + 1].broadcast_to([P, P]), tri3[:, 0:S],
                              start=True, stop=False, skip_group_check=True)
                    ins = pe.matmul(ps[:, b, o + P:o + S], a_tok[:, 1, h:h + 1].broadcast_to([P, P]), tri,
                                    start=False, stop=True, skip_group_check=True)
                ins.then_inc(sig("cum_pe"), 1)

            def ssd_cumcol():
                pe.wait_ge(sig("a_tok"), 1)
                pe.wait_ge(sig("xs_tok"), 1)
                pe.matmul(ps[:, 6, 0:8], tri, a_tok[:, 0, :], start=True, stop=True)
                pe.matmul(ps[:, 6, 8:16], ones, a_tok[:, 0, :], start=True, stop=False)
                pe.matmul(ps[:, 6, 8:16], tri, a_tok[:, 1, :], start=False, stop=True).then_inc(sig("acs_pe"), 1)

            def lru_gate(i):
                pe.wait_ge(sig("ld_lru"), 64)
                pe.wait_ge(sig("xcT"), 1)
                if i == 0:
                    pe.wait_ge(sig("dm"), 2)
                else:
                    pe.wait_ge(sig("lru_r"), 1)
                for c in range(KM):
                    o = (c % 2) * S
                    ins = pe.matmul(ps[:, 6 + c // 2, o:o + S], lru_w[:, i, c, :], xcT[:, c, :], start=True, stop=True)
                ins.then_inc(sig("lru_pe"), 1)

            def ssd_y():
                pe.wait_ge(sig("lru_i"), 1)
                pe.wait_ge(sig("dm_cb"), 1)
                pe.wait_ge(sig("xdt"), 1)
                for h in range(MH):
                    c = slice(64 * h, 64 * h + 64)
                    pe.matmul(ps[:, 6, c], dm[:, h, 0:P], xdt[:, 0, c], start=True, stop=True)
                    pe.matmul(ps[:, 7, c], dm[:, h, P:S], xdt[:, 0, c], start=True, stop=False)
                    ins = pe.matmul(ps[:, 7, c], dm[:, h, S:384], xdt[:, 1, c], start=False, stop=True)
                ins.then_inc(sig("ssd_y_pe"), 1)

            def pool_y():
                pe.wait_ge(sig("ssd_y"), 1)
                for c in range(KM):
                    o = (c % 2) * S
                    ins = pe.matmul(ps[:, 6 + c // 2, o:o + S], pool_w[:, c, :], dT[:, c, :], start=True, stop=True)
                ins.then_inc(sig("pool_y"), 1)

            def ssd_turn():
                pe.wait_ge(sig("ybT"), 1)
                pe.wait_ge(sig("ssd_normed"), 1)
                transposes(0, y_ssd, KM, "ycT_pe", 6)

            extra = {0: [ssd_cb], 1: [ssd_xs, ssd_cumcol], 2: [lambda: ssd_cumsum(0)], 3: [lambda: ssd_cumsum(1)],
                     4: [lambda: lru_gate(0)], 5: [lambda: lru_gate(1), ssd_y], 6: [pool_y], 7: [ssd_turn]}
            for i in range(8):
                evacuated(g)
                gemm_tok(10 + i, (g % 2) * 2, 512).then_inc(sig("w_used"), 1)
                g += 1
                if i >= 2:
                    mla_out(i - 2)
                mla_score(i)
                if i:
                    mla_turn(i - 1)
                for f in extra[i]:
                    f()
            mla_out(MH - 2)

            def branch(i, yT, t):
                w = w_ring[:, (18 + i) % RING, :].rearrange("p (k n) -> p k n", k=KM)
                for h in range(2):
                    for k in range(KM):
                        ins = pe.matmul(ps[:, 4 * (i % 2) + 2 * t + h, :], yT[:, k, t * P:(t + 1) * P],
                                        w[:, k, h * 512:(h + 1) * 512], start=(k == 0), stop=(k == KM - 1))
                return ins

            for i, yT in enumerate((ybT, yaT, lru_g, ycT)):
                landed(pe, 18 + i)
                pe.wait_ge(sig(("ybT", "yaT", "ydT", "ycT")[i]), 1)
                if i == 0:
                    pe.wait_ge(*EVAC[15])
                    pe.wait_ge(*EVAC[14])
                elif i == 1:
                    pe.wait_ge(sig("ycT"), 1)
                else:
                    pe.wait_ge(sig("branch"), i - 1)
                ins = branch(i, yT, 0)
                if i == 0:
                    mla_turn(MH - 1)
                elif i == 3:
                    ins.then_inc(sig("branch_first"), 1)
                branch(i, yT, 1).then_inc(sig("w_used"), 1)
                if i == 0:
                    mla_out(MH - 1)
                    pe.wait_ge(sig("mla_o"), MH)
                    transposes(0, o_mla, KM, "mla_oT_pe", 4)
            pe.wait_ge(sig("branch"), 4)
            act_transposes(1)
            act_ready(1)
            gemm_tok(22, 0, 512).then_inc(sig("w_used"), 1)
            gemm_tok(23, 2, 512, True).then_inc(sig("w_used"), 1)

            def split_T(w, aT, bank):
                w_h, w_l = (v.rearrange("p (k n) -> p k n", k=KD) for v in w)
                for c in range(4):
                    for k in range(KD):
                        cols = slice(c * P, (c + 1) * P)
                        pe.matmul(ps[:, bank + c, :], w_h[:, k, cols], aT[k], start=(k == 0), stop=False,
                                  skip_group_check=True)
                        ins = pe.matmul(ps[:, bank + c, 0:S], w_l[:, k, cols], aT[k][:, 0:S], start=False,
                                        stop=(k == KD - 1), skip_group_check=True)
                return ins

            def split_tok(w, aT, bank):
                w_h, w_l = (v.rearrange("p (k n) -> p k n", k=KD) for v in w)
                for t in range(T):
                    hi, lo = slice(t * P, (t + 1) * P), slice(S + t * P, S + (t + 1) * P)
                    for k in range(KD):
                        for i, (u, v) in enumerate(((hi, w_h), (hi, w_l), (lo, w_h))):
                            ins = pe.matmul(ps[:, bank + t, :], aT[k][:, u], v[:, k, :],
                                            start=(k + i == 0), stop=(k == KD - 1 and i == 2))
                return ins

            act_transposes(2)
            act_ready(2)
            for i in range(8):
                pe.wait_ge(sig("w_lo"), i + 1)
                if i >= 2:
                    pe.wait_ge(sig("ff1_out"), i - 1)
                elif i == 0:
                    pe.wait_ge(sig("x_res"), 1)
                split_T(ff_w[i % 2], ff_a, (i % 2) * 4).then_inc(sig("w_used"), 1)
            pe.wait_ge(sig("ff1_out"), 7)
            for i in range(8):
                pe.wait_ge(sig("w_lo"), 8 + i + 1)
                pe.wait_ge(sig("hid_lo"), i + 1)
                w_h, w_l = (v.rearrange("p (k n) -> p k n", k=KM) for v in ff_w[i % 2])
                for t in range(T):
                    for k in range(KM):
                        kk = KM * i + k
                        c = slice(t * P, (t + 1) * P)
                        for u, v in ((hid_hi, w_h), (hid_hi, w_l), (hid_lo, w_h)):
                            for h in range(2):
                                ins = pe.matmul(ps[:, 2 * t + h, :], u[:, kk, c], v[:, k, h * 512:(h + 1) * 512],
                                                start=(kk == 0 and u is hid_hi and v is w_h),
                                                stop=(kk == 31 and u is hid_lo), skip_group_check=True)
                    if i == 7 and t == 0:
                        ins.then_inc(sig("first_tile"), 1)
                ins.then_inc(sig("w_used"), 1)
                if i == 0:
                    pe.wait_ge(sig("ff1_out"), 8)
                    pe.wait_ge(sig("ld_rel"), 48)
                    pe.matmul(ps[0:H2, 5, 0:384], rel_tab, onehot, start=True, stop=True).then_inc(sig("rel_pe"), 1)
                    pe.wait_ge(sig("ld_p"), 16)
                    transposes(0, p_tok, 2, "pT_pe", 4)
            pe.wait_ge(sig("ld_spread"), 16)
            pe.wait_ge(sig("pT"), 1)
            pe.wait_ge(sig("rel_row"), 1)
            for i in range(8):
                if i == 4:
                    pe.wait_ge(sig("bias_h"), 1)
                ins = pe.matmul(ps[:, 4 + i % 4, :], flip, rel_spread[:, 2 * i:2 * i + 2, :], start=True, stop=True)
                if i % 4 == 3:
                    ins.then_inc(sig("flip_pe"), 1)
            pe.wait_ge(sig("x_res"), 2)
            pe.wait_ge(sig("pT"), 1)
            landed(pe, 40)
            w = w_ring[:, 40 % RING, 0:2 * D].rearrange("p (k n) -> p k n", k=2)
            for t in range(T):
                for h in range(2):
                    for k in range(2):
                        ins = pe.matmul(ps[:, 2 * t + h, :], pT[:, k, t * P:(t + 1) * P],
                                        w[:, k, h * 512:(h + 1) * 512], start=(k == 0), stop=(k == 1))
            ins.then_inc(sig("w_used"), 1)
            pe.wait_ge(sig("bias_h"), 2)
            act_transposes(3)
            act_ready(3)
            for i in range(2):
                gemm_tok(41 + i, 4 + 2 * i, 512, i == 1).then_inc(sig("w_used"), 1)

            def qkv(n0, g, base, bufs, aT):
                for s in range(6):
                    pe.wait_ge(sig("w_lo"), split_index(n0) + s + 1 + g * 6)
                    pe.wait_ge(sig("qkv_out"), base + 1 + s + g * 6)
                    f = split_T if s < 4 else split_tok
                    f(bufs[s], aT, (s % 2) * 4).then_inc(sig("w_used"), 1)

            pe.wait_ge(sig("ple_gate"), 3)
            act_transposes(4)
            act_ready(4)
            with pe.Fori(0, 3) as g:
                qkv(DIL0, g, 0, dil_w, dil_a)
            pe.wait_ge(sig("qkv_out"), 20)

            def dil_scores(h):
                if h:
                    pe.wait_ge(sig("dil_max"), h)
                c, r = h // 2, slice(64 * (h % 2), 64 * (h % 2) + 64)
                for g in range(3):
                    pe.matmul(ps[:, 0, g * P:(g + 1) * P], q2T[r, g, c, 0:P], k2T[r, g, c, 0:P], start=True, stop=True)
                for g in range(3):
                    o = (g % 2) * S
                    ins = pe.matmul(ps[:, 1 + g // 2, o:o + S], q2T[r, g, c, P:S], k2T[r, g, c, :], start=True, stop=True)
                ins.then_inc(sig("dil_scores"), 1)

            def dil_turn(h):
                pe.wait_ge(sig("dil_exp"), h + 1)
                if h == 0:
                    pe.wait_ge(sig("xp_act"), 20)
                else:
                    pe.wait_ge(sig("dil_pT_act"), h)
                    pe.wait_ge(sig("dil_pT_dve"), h)
                for j in range(9):
                    b, o = (3, j * P) if j < 3 else (4 + (j - 3) // 4, ((j - 3) % 4) * P)
                    ins = pe.transpose(ps[:, b, o:o + P], e_dil[:, h % 2, j * P:(j + 1) * P], ident)
                ins.then_inc(sig("dil_pT_pe"), 1)

            def dil_out(h):
                eT0, eT1 = eT_two[h % 2]
                pe.wait_ge(sig("dil_pT_act"), h + 1)
                pe.wait_ge(sig("dil_pT_dve"), h + 1)
                if h >= 2:
                    pe.wait_ge(sig("dil_o"), h - 1)
                cols = slice(64 * h, 64 * h + 64)
                for g in range(3):
                    pe.matmul(ps[:, 6 + h % 2, 0:64], eT0[:, g * P:(g + 1) * P], v2[:, g, 0, cols],
                              start=(g == 0), stop=(g == 2))
                for g in range(3):
                    for kt in range(2):
                        o = g * S + kt * P
                        ins = pe.matmul(ps[:, 6 + h % 2, 64:128], eT1[:, o:o + P], v2[:, g, kt, cols],
                                        start=(g + kt == 0), stop=(g + kt == 3))
                ins.then_inc(sig("dil_pv"), 1)

            dil_scores(0)
            for h in range(H2):
                if h + 1 < H2:
                    dil_scores(h + 1)
                dil_turn(h)
                if h:
                    dil_out(h - 1)
            dil_out(H2 - 1)
            act_transposes(5)
            act_ready(5)
            gemm_tok(DOUT0, 0, 512).then_inc(sig("w_used"), 1)
            gemm_tok(DOUT0 + 1, 2, 512, True).then_inc(sig("w_used"), 1)

            def experts(layer, n0, turn):
                q0 = split_index(n0)
                act_transposes(turn)
                act_ready(turn)
                pe.wait_ge(sig("ld_router"), 16)
                for t in range(T):
                    for k in range(KD):
                        ins = pe.matmul(ps[:, 0, t * NE:(t + 1) * NE], actT[:, k, t * P:(t + 1) * P], router_w[:, k, :],
                                        start=(k == 0), stop=(k == KD - 1))
                ins.then_inc(sig("logits"), 1)

                def gate_up(b, t):
                    w_h, w_l = (v[:, (n0 + b) % 3, :].rearrange("p (k n) -> p k n", k=KD) for v in (w_hi, w_lo))
                    for k in range(KD):
                        c = slice(t * P, (t + 1) * P)
                        for i, (u, v) in enumerate(((aT_hi, w_h), (aT_hi, w_l), (aT_lo, w_h))):
                            ins = pe.matmul(ps[:, 4 + 2 * b + t, :], u[:, k, c], v[:, k, :],
                                            start=(k + i == 0), stop=(k == KD - 1 and i == 2))
                    return ins

                def turn_h(b, j):
                    pe.wait_ge(sig("moe_h"), NE * layer + 1 + b + j * 2)
                    for f in range(2):
                        for t in range(T):
                            o = f * S + t * P
                            ins = pe.transpose(ps[:, 4 + 2 * b, o:o + P], h_tok[:, b, t, f * P:(f + 1) * P], ident)
                    ins.then_inc(sig("moe_hT_pe"), 1)

                def down(b, j, last=False):
                    pe.wait_ge(sig("moe_hT"), NE * layer + 1 + b + j * 2)
                    o = b * 2048
                    w_h, w_l = (v[:, (n0 + 2) % 3, o:o + 2048].rearrange("p (k n) -> p k n", k=2) for v in (w_hi, w_lo))
                    for t in range(T):
                        for f in range(2):
                            c = slice(f * S + t * P, f * S + (t + 1) * P)
                            for u, v in ((hT_hi, w_h), (hT_hi, w_l), (hT_lo, w_h)):
                                for h in range(2):
                                    ins = pe.matmul(ps[:, 2 * t + h, :], u[:, b, c], v[:, f, h * 512:(h + 1) * 512],
                                                    start=False, stop=(last and f == 1 and u is hT_lo),
                                                    skip_group_check=True)
                        if last and t == 0:
                            ins.then_inc(sig("first_tile"), 1)
                    return ins

                def pair(j, last):
                    gate_up(0, 1).then_inc(sig("w_used"), 1)
                    pe.wait_ge(sig("w_lo"), q0 + 2 + j * 3)
                    gate_up(1, 0)
                    turn_h(0, j)
                    gate_up(1, 1).then_inc(sig("w_used"), 1)
                    pe.wait_ge(sig("w_lo"), q0 + 3 + j * 3)
                    down(0, j)
                    turn_h(1, j)
                    if not last:
                        pe.wait_ge(sig("w_lo"), q0 + 4 + j * 3)
                        gate_up(0, 0)
                    down(1, j, last).then_inc(sig("w_used"), 1)

                pe.wait_ge(sig("w_lo"), q0 + 1)
                pe.wait_ge(sig("aT_lo"), 4 * layer + 1)
                gate_up(0, 0)
                pe.wait_ge(sig("router_exp"), layer + 1)
                for b in range(4):
                    pe.matmul(ps[:, b, :], zero16[:, 0:P], zero16[:, P:640], start=True, stop=False,
                              skip_group_check=True)
                pe.wait_ge(sig("aT_lo"), 4 * layer + 2)
                with pe.Fori(0, NE // 2 - 1) as j:
                    pair(j, False)
                pair(NE // 2 - 1, True)

            experts(0, MOE0, 6)
            act_transposes(7)
            act_ready(7)
            pe.wait_ge(sig("aT_lo"), 4)
            qkv(SBI0, 0, 18, sbq_w, sbq_a)
            pe.wait_ge(sig("qkv_out"), 26)

            def sb_z(m):
                if m >= 2:
                    pe.wait_ge(sig("sb_zc"), m - 1)
                for j in range(2):
                    r, b = slice(64 * j, 64 * j + 64), 2 * (m % 2) + j
                    pe.matmul(ps[:, b, 0:S], k2T[r, 0, m, 0:P], q2T[r, 0, m, :], start=True, stop=True)
                    ins = pe.matmul(ps[:, b, S:384], k2T[r, 0, m, P:S], q2T[r, 0, m, P:S], start=True, stop=True)
                ins.then_inc(sig("sb_z"), 1)

            def sb_r(m):
                pe.wait_ge(sig("sb_sp"), m + 1)
                if m:
                    pe.wait_ge(sig("sb_d"), m)
                for j in range(2):
                    pe.matmul(ps[:, 4 + j, 0:384], low, sb_l[m % SBN][:, j, :], start=True, stop=False,
                              skip_group_check=True)
                    ins = pe.matmul(ps[:, 4 + j, P:S], ones, sb_l[m % SBN][:, j, S:384], start=False, stop=True,
                                    skip_group_check=True)
                ins.then_inc(sig("sb_r"), 1)

            def sb_pv(m):
                pe.wait_ge(sig("sb_att"), m + 1)
                if m >= 2:
                    pe.wait_ge(sig("sb_o"), m - 1)
                for j in range(2):
                    att, cols = sb_e[m % SBN][:, j, :], slice(64 * (2 * m + j), 64 * (2 * m + j) + 64)
                    pe.matmul(ps[:, 6 + m % 2, j * 64:j * 64 + 64], att[:, 0:P], v2[:, 0, 0, cols], start=True, stop=True)
                    o = 128 + j * 64
                    pe.matmul(ps[:, 6 + m % 2, o:o + 64], att[:, P:S], v2[:, 0, 0, cols], start=True, stop=False)
                    ins = pe.matmul(ps[:, 6 + m % 2, o:o + 64], att[:, S:384], v2[:, 0, 1, cols], start=False, stop=True)
                ins.then_inc(sig("sb_pv"), 1)

            sb_z(0)
            for i in range(H2 // 2 + 3):
                staged(i, (sb_z, -1), (sb_r, 1), (sb_pv, 3))
            act_transposes(8)
            act_ready(8)
            gemm_tok(SBO0, 0, 512).then_inc(sig("w_used"), 1)
            gemm_tok(SBO0 + 1, 2, 512, True).then_inc(sig("w_used"), 1)
            experts(1, MOE1, 9)

        def turned(eng, copy, i, gains, done, first, norm=None):
            for b in range(first, KD // 2, 2):
                eng.wait_ge(sig("xp_pe"), KD * i + 2 * b + 2)
                for k in (2 * b, 2 * b + 1):
                    dst, src = actT[:, k, :], ps[:, 4 + b, (k % 2) * S:(k % 2) * S + S]
                    if norm is None:
                        ins = copy(dst, src, pcols(gains, k) if gains else 1.0)
                    else:
                        c = NPROW + 16 * norm + k
                        ins = copy(dst, src, pcol[:, c:c + 1], pcol[:, c + 8:c + 9])
                    ins.then_inc(sig(done), 1)

        def split_chunk(parts, k):
            for v in parts:
                if k < v.shape[1]:
                    return v[:, k, 0:S], v[:, k, S:2 * S]
                k -= v.shape[1]

        @block.scalar
        def _(act):
            def copy(dst, src, scale=1.0, bias=None):
                if bias is not None:
                    return act.activation(dst, src, ACT.Identity, scale=scale, bias=bias)
                return act.activation(dst, src, ACT.Copy, scale=scale)

            def w_high(n0, b, dst, used, j=0, step=6):
                n = n0 + b
                act.wait_ge(sig(f"w_landed{n % RING}"), 32 * (n // RING + 1) + j * (step // RING * 32))
                act.wait_ge(sig("w_used"), used + j * step)
                copy(dst[0], w_ring[:, n % RING, :], W_POW).then_inc(sig("w_hi"), 1)

            def turned_high(i, gains, parts):
                for k in range(KD):
                    if k % 2 == 0:
                        act.wait_ge(sig("xp_pe"), KD * i + k + 2)
                    ins = copy(split_chunk(parts, k)[0], ps[:, 4 + k // 2, (k % 2) * S:(k % 2) * S + S], pcols(gains, k))
                    if k % 2:
                        ins.then_inc(sig("xp_act"), 1)

            def bank_pair(g, cols):
                return ps[:, (g % 2) * 2:(g % 2) * 2 + 2, 0:cols]

            act.wait_ge(sig("rstd_ready"), 1)
            copy(x_norm[:, 1, :], x_norm[:, 1, :], rstd[:, 1:2]).then_inc(sig("xn1_ready"), 1)
            act.wait_ge(sig("angle"), 1)
            act.activation(rope_cs[:, 1, :, :], rope_tmp[:, 0, 0:32].rearrange("p (t f) -> p t f", t=T), ACT.Sin)
            act.activation(rope_cs[:, 0, :, :], rope_tmp[:, 0, 0:32].rearrange("p (t f) -> p t f", t=T), ACT.Sin,
                           scale=0.5).then_inc(sig("sines"), 1)
            act.wait_ge(sig("pcol"), 1)
            turned(act, copy, 0, "g_mix", "xp_act", 0)
            act.wait_ge(sig("w_used"), 1)
            copy(cq, bank_pair(0, 384)).then_inc(sig("out_by_act"), 1)
            act.wait_ge(sig("w_used"), 3)
            copy(up, bank_pair(2, 512)).then_inc(sig("out_by_act"), 1)
            act.wait_ge(sig("w_used"), 4)
            act.activation(z_silu, bank_pair(3, 512), ACT.Silu).then_inc(sig("out_by_act"), 1)
            act.wait_ge(sig("w_used"), 6)
            for t in range(T):
                ins = copy(q_tok[:, t, :, :].rearrange("p (b h) d -> p b (h d)", b=2), ps[:, 4 + 2 * t:6 + 2 * t, 0:384])
            ins.then_inc(sig("q_out"), 1)
            act.wait_ge(sig("w_used"), 8)
            for t in range(T):
                src = ps[:, 4 + 2 * t:6 + 2 * t, :].rearrange("p b (h d) -> p (b h) d", h=4)
                copy(k_tok[:, t, :, 0:NOPE], src[:, :, 0:NOPE])
                ins = copy(v_tok[:, t, :, :], src[:, :, NOPE:])
            ins.then_inc(sig("kv_out"), 1)
            act.wait_ge(sig("w_used"), 9)
            act.activation(lru_g, ps[:, 0:2, :].rearrange("p b (c s) -> p (b c) s", c=2), ACT.Gelu_apprx_tanh)\
                .then_inc(sig("out_by_act"), 1)
            act.wait_ge(sig("qT_pe"), 1)
            copy(qT[0:QKD, :, :], ps[0:QKD, 4:8, :].rearrange("p b (h s) -> p (b h) s", h=2)).then_inc(sig("qT"), 1)
            act.wait_ge(sig("x_conv"), 1)
            act.activation(xbS, xbS, ACT.Silu).then_inc(sig("xbS"), 1)
            act.wait_ge(sig("sp_abs"), 1)
            act.activation(sp_e[:, :], sp_a[:, :], ACT.Exp, scale=-1.0)
            act.activation(a_head[:, :], brow[:, 8:16], ACT.Exp)
            act.drain()
            act.activation(sp_e[:, :], sp_e[:, :], ACT.Ln, bias=1.0).then_inc(sig("sp_ln"), 1)
            act.wait_ge(sig("kT_pe"), 1)
            copy(kT[0:QKD, :, :], ps[0:QKD, 4:8, :].rearrange("p b (h s) -> p (b h) s", h=2)).then_inc(sig("kT"), 1)

            def gate(i):
                g = 8 + i
                act.wait_ge(sig("w_used"), 11 + i)
                act.activation(gates[:, :, 512 * i:512 * i + 512], bank_pair(g, 512), ACT.Sigmoid)\
                    .then_inc(sig("out_by_act"), 1)

            def mla_exp(h):
                act.wait_ge(sig("mla_max"), h + 1)
                d = 2 * (h % 2)
                act.activation(probs[:, 0:P], probs[:, 0:P], ACT.Exp, bias=mx[:, 0:1], accum_out=den[:, d:d + 1])
                act.activation(probs[:, P:384], probs[:, P:384], ACT.Exp, bias=mx[:, 1:2],
                               accum_out=den[:, d + 1:d + 2]).then_inc(sig("mla_exp"), 1)

            def xs_out():
                act.wait_ge(sig("xs_pe"), 1)
                copy(xs_tok, ps[:, 6:8, :]).then_inc(sig("xs_tok"), 1)

            def dm_exp(half):
                act.wait_ge(sig("dm"), half + 1)
                v = dm[:, 4 * half:4 * half + 4, :]
                act.activation(v, v, ACT.Exp).then_inc(sig("dm_exp"), 1)

            def lru_sigmoid(i):
                act.wait_ge(sig("lru_pe"), i + 1)
                dst, bias = ((lru_r, "lru_b_a"), (lru_i, "lru_b_i"))[i]
                for c in range(KM):
                    ins = act.activation(dst[:, c, :], ps[:, 6 + c // 2, (c % 2) * S:(c % 2) * S + S], ACT.Sigmoid,
                                         bias=pcols(bias, c))
                ins.then_inc(sig(("lru_r", "lru_i")[i]), 1)

            def lru_decay():
                act.wait_ge(sig("lru_nl"), 1)
                act.activation(lru_a, lru_r, ACT.Exp, scale=-1.0)
                act.activation(lru_t, lru_r, ACT.Tanh).then_inc(sig("lru_at"), 1)

            def lru_root():
                act.wait_ge(sig("lru_sq"), 1)
                act.activation(lru_t, lru_t, ACT.Sqrt).then_inc(sig("lru_root"), 1)

            extra = {1: [xs_out], 2: [lambda: dm_exp(0)], 3: [lambda: dm_exp(1)], 4: [lambda: lru_sigmoid(0)],
                     5: [lambda: lru_sigmoid(1), lru_decay], 6: [lru_root]}
            for i in range(8):
                gate(i)
                mla_exp(i)
                for f in extra.get(i, []):
                    f()
            act.wait_ge(sig("mla_oT_pe"), KM)
            copy(yaT, ps[:, 4:6, :].rearrange("p b (c s) -> p (b c) s", c=2)).then_inc(sig("yaT"), 1)
            turned(act, copy, 1, None, "xp_act", 0)
            act.wait_ge(sig("xn1_ready"), 2)
            w_high(FF0, 0, ff_w[0], 22)
            w_high(FF0, 1, ff_w[1], 23)
            turned_high(2, "g_mlp", ff_parts)
            def banks(s):
                v = ps[:, 4 * (s % 2):4 * (s % 2) + 4, :]
                return v[:, :, 0:S], v[:, :, S:2 * S]

            for i in range(16):
                if i < 8:
                    act.wait_ge(sig("w_used"), 25 + i)
                    if i >= 2:
                        act.wait_ge(sig("hid_lo"), i - 1)
                    copy(hid_tmp[i % 2].rearrange("p (c s) -> p c s", c=4), banks(i)[1], H_POW ** 0.5 / SUM_POW)\
                        .then_inc(sig("ff1_low"), 1)
                if i == 9:
                    act.wait_ge(sig("pT_pe"), 2)
                    copy(pT, ps[:, 4, :].rearrange("p (c s) -> p c s", c=2)).then_inc(sig("pT"), 1)
                if i < 14:
                    w_high(FF0, i + 2, ff_w[i % 2], FF0 + i + 1)
                if i < 8:
                    act.wait_ge(sig("ff1_square"), i + 1)
                    copy(hid_hi[:, 4 * i:4 * i + 4, :].rearrange("p c s -> p (c s)"), hid_tmp[i % 2])\
                        .then_inc(sig("hid_hi"), 1)
            for i in range(2):
                act.wait_ge(sig("flip_pe"), i + 1)
                copy(bias_h[:, 8 * i:8 * i + 8, :], ps[:, 4:8, :].rearrange("p b (h s) -> p (b h) s", h=2))\
                    .then_inc(sig("bias_h"), 1)
            turned(act, copy, 3, "g_ple", "xp_act", 0)
            w_high(DIL0, 0, dil_w[0], 41)
            act.wait_ge(sig("w_used"), 42)
            act.activation(x_norm[:, :, 0:512], ps[:, 4:6, :], ACT.Sigmoid).then_inc(sig("ple_gate"), 1)
            for t in range(T):
                if t == 0:
                    act.wait_ge(sig("first_tile"), 3)
                else:
                    act.wait_ge(sig("w_used"), 43)
                act.activation(x_norm[:, t, 512:], ps[:, 6 + t, :], ACT.Sigmoid).then_inc(sig("ple_gate"), 1)
            turned_high(4, "g_final", dil_parts)
            act.wait_ge(sig("x_full"), 1)
            w_high(DIL0, 1, dil_w[1], 42)

            def qkv(n0, g, bufs, last):
                for s in range(6):
                    act.wait_ge(sig("w_used"), n0 + s + 1 + g * 6)
                    if s < 4:
                        d = (q2T, k2T)[s // 2][:, bass.ds(g, 1), 4 * (s % 2):4 * (s % 2) + 4, :]
                        copy(d.rearrange("p o c s -> p (o c) s"), banks(s)[1], (0.125 if s < 2 else 1.0) / SUM_POW)\
                            .then_inc(sig("qkv_low"), 1)
                    if s < 4 or not last:
                        w_high(n0, s + 2, bufs[(s + 2) % 6], n0 + s + 1, g)

            with act.Fori(0, 2) as g:
                qkv(DIL0, g, dil_w, False)
            qkv(DIL0, 2, dil_w, True)

            def dil_exp(h):
                act.wait_ge(sig("dil_max"), h + 1)
                d = 2 * (h % 2)
                e, m = e_dil[:, h % 2, :], mx4[:, d:d + 2]
                act.activation(e[:, 0:384], e[:, 0:384], ACT.Exp, bias=m[:, 0:1], accum_out=den[:, d:d + 1])
                act.activation(e[:, 384:], e[:, 384:], ACT.Exp, bias=m[:, 1:2], accum_out=den[:, d + 1:d + 2])\
                    .then_inc(sig("dil_exp"), 1)

            dil_exp(0)
            for h in range(H2):
                if h + 1 < H2:
                    dil_exp(h + 1)
                act.wait_ge(sig("dil_pT_pe"), h + 1)
                copy(eT_two[h % 2][0], ps[:, 3, 0:384]).then_inc(sig("dil_pT_act"), 1)
            turned(act, copy, 5, None, "xp_act", 0)

            def w_split(n0, b, j):
                n = n0 + b
                act.wait_ge(sig(f"w_landed{n % RING}"), 32 * (n // RING + 1) + j * 32)
                act.wait_ge(sig("w_used"), n - 2 + j * 3)
                copy(w_hi[:, n % 3, :], w_ring[:, n % RING, :], W_POW).then_inc(sig("w_hi"), 1)

            def experts(layer, n0, turn):
                def next_split(b, j, last):
                    if not last:
                        w_split(n0 + 3, b, j)
                    elif layer == 0:
                        w_high(SBI0, b, sbq_w[b], MOE0)

                for b in range(2):
                    w_split(n0, b, 0)
                turned(act, copy, turn, None, "xp_act", 0, 2 * layer)
                act.wait_ge(sig("xp_dve"), 4 * turn + 4)
                act.drain()
                for t in range(T):
                    copy(aT_hi[:, :, t * P:(t + 1) * P], actT[:, :, t * P:(t + 1) * P], A_POW).then_inc(sig("aT_hi"), 1)
                act.wait_ge(sig("logits"), layer + 1)
                act.activation(score, ps[:, 0, 0:T * NE], ACT.Exp, scale=-1.0).then_inc(sig("router_exp"), 1)

                def silu(b, j):
                    act.wait_ge(sig("w_used"), n0 + b + 1 + j * 3)
                    act.activation(e_silu[:, b, :, :], ps[:, 4 + 2 * b:6 + 2 * b, 0:DE], ACT.Silu, scale=1.0 / SUM_POW)\
                        .then_inc(sig("moe_silu"), 1)

                def h_high(b, j):
                    act.wait_ge(sig("moe_hT_pe"), NE * layer + 1 + b + j * 2)
                    copy(hT_hi[:, b, :], ps[:, 4 + 2 * b, :]).then_inc(sig("moe_hT_hi"), 1)

                def pair(j, last):
                    silu(0, j)
                    w_split(n0, 2, j)
                    next_split(0, j, last)
                    h_high(0, j)
                    silu(1, j)
                    if not last:
                        next_split(1, j, last)
                    h_high(1, j)
                    if last:
                        next_split(1, j, last)

                with act.Fori(0, NE // 2 - 1) as j:
                    pair(j, False)
                pair(NE // 2 - 1, True)

            act.wait_ge(sig("dil_pv"), H2)
            experts(0, MOE0, 6)
            turned(act, copy, 7, None, "xp_act", 0, 1)
            act.wait_ge(sig("xp_dve"), 4 * 7 + 4)
            act.drain()
            for k in (0, KD // 2):
                copy(sbq_parts[0][:, k:k + 4, 0:S], actT[:, k:k + 4, :], A_POW).then_inc(sig("aT_hi"), 1)
            qkv(SBI0, 0, sbq_w, True)

            def sb_softplus(m):
                act.wait_ge(sig("sb_zc"), m + 1)
                act.activation(sb_l[m % SBN], sb_e[m % SBN], ACT.Exp)
                act.drain()
                act.activation(sb_l[m % SBN], sb_l[m % SBN], ACT.Ln, bias=1.0).then_inc(sig("sb_ln"), 1)

            def sb_exp(m):
                act.wait_ge(sig("sb_d"), m + 1)
                act.activation(sb_e[m % SBN], sb_e[m % SBN], ACT.Exp).then_inc(sig("sb_exp"), 1)

            for i in range(H2 // 2 + 2):
                staged(i, (sb_softplus, 0), (sb_exp, 2))
            turned(act, copy, 8, None, "xp_act", 0)
            act.wait_ge(sig("sb_pv"), H2 // 2)
            experts(1, MOE1, 9)

        @block.vector
        def _(dve):
            def scaled(dst, src, scale, bias=None):
                if bias is not None:
                    return dve.tensor_scalar(dst, src, scale, bias, ALU.mult, ALU.add)
                return dve.tensor_scalar(dst, src, scale, None, ALU.mult)

            def w_low(n0, b, dst, j=0, step=6):
                dve.wait_ge(sig("w_hi"), split_index(n0) + b + 1 + j * step)
                dve.scalar_tensor_tensor(out=dst[1], in0=w_ring[:, (n0 + b) % RING, :], scalar=W_POW, in1=dst[0],
                                         op0=ALU.mult, op1=ALU.subtract).then_inc(sig("w_lo"), 1)

            def turned_low(i, gains, parts):
                for k in range(KD):
                    if k % 2 == 0:
                        dve.wait_ge(sig("xp_act"), 4 * i + k // 2 + 1)
                    hi, lo = split_chunk(parts, k)
                    ins = dve.scalar_tensor_tensor(out=lo, in0=ps[:, 4 + k // 2, (k % 2) * S:(k % 2) * S + S],
                                                   scalar=pcols(gains, k), in1=hi, op0=ALU.mult, op1=ALU.subtract)
                    if k % 2:
                        ins.then_inc(sig("xp_dve"), 1)

            def banks(s):
                v = ps[:, 4 * (s % 2):4 * (s % 2) + 4, :]
                return v[:, :, 0:S], v[:, :, S:2 * S]

            def both_tiles():
                dve.drain()
                for t in range(T):
                    dve.engine_nop().then_inc(sig(f"xn{t}_ready"), 1)

            def bank_pair(g, cols, o=0):
                return ps[:, (g % 2) * 2:(g % 2) * 2 + 2, o:o + cols]

            def mean_square(src, cols, i, junk):
                for t in range(T):
                    dve.tensor_tensor_reduce(junk[:, t, 0:cols], src[:, t, :], src[:, t, :], 1.0, 0.0, ALU.mult, ALU.add,
                                             ms[:, i + t:i + t + 1])
                dve.drain()
                return dve.tensor_scalar(ms[:, i:i + T], ms[:, i:i + T], 1.0 / cols, EPS, ALU.mult, ALU.add)

            def squares(t, c, part):
                dve.tensor_tensor_reduce(x_norm[:, t, c], x_tok[:, t, c], x_tok[:, t, c], 1.0, 0.0, ALU.mult, ALU.add, part)

            def scale_tile(n, t, mean=None):
                dve.wait_ge(sig("rstd_ready"), norm_count(n, t))
                if mean is None:
                    ins = scaled(x_norm[:, t, :], x_tok[:, t, :], rstd[:, t:t + 1])
                else:
                    ins = dve.tensor_scalar(x_norm[:, t, :], x_tok[:, t, :], mean, rstd[:, t:t + 1],
                                            ALU.subtract, ALU.mult)
                ins.then_inc(sig(f"xn{t}_ready"), 1)

            def rms_tile(n, t):
                dve.drain()
                dve.tensor_scalar(ms[:, t:t + 1], ms[:, t:t + 1], 1.0 / D, EPS, ALU.mult, ALU.add)\
                    .then_inc(sig("ms_ready"), 1)
                scale_tile(n, t)

            def halves_sum(t):
                dve.drain()
                dve.tensor_tensor(ms[:, t:t + 1], ms_part[:, 0, t:t + 1], ms_part[:, 1, t:t + 1], ALU.add)

            def tile_done(i, t, w_used):
                if t == 0:
                    dve.wait_ge(sig("first_tile"), i)
                else:
                    dve.wait_ge(sig("w_used"), w_used)

            junk = gates[:, :, 0:D]
            dve.wait_ge(sig("ld_x"), 16)
            mean_square(x_norm, D, 0, junk).then_inc(sig("ms_ready"), 1)
            dve.wait_ge(sig("rstd_ready"), 1)
            scaled(x_norm[:, 0, :], x_norm[:, 0, :], rstd[:, 0:1]).then_inc(sig("xn0_ready"), 1)
            dve.wait_ge(sig("ld_rows"), 16 * 3)
            dve.tensor_copy(pos_f[:, :], pos_i[:, :])
            dve.drain()
            ang, turns, tmp = (rope_tmp[:, 0, 32 * i:32 * i + 32] for i in range(3))
            for t in range(T):
                dve.tensor_scalar(ang[:, 16 * t:16 * t + 16], inv_freq, pos_f[:, t:t + 1], None, ALU.mult)
            dve.drain()
            dve.tensor_scalar(turns, ang, float(1 / (2 * np.pi)), None, ALU.mult)
            dve.drain()
            dve.tensor_scalar(turns, turns, 12582912.0, None, ALU.add)
            dve.drain()
            dve.tensor_scalar(turns, turns, -12582912.0, None, ALU.add)
            dve.drain()
            c1 = 6.28125
            c2 = round((2 * np.pi - c1) * 2 ** 19) / 2 ** 19
            c3 = 2 * np.pi - c1 - c2
            for c in (c1, c2, c3):
                dve.scalar_tensor_tensor(out=ang, in0=turns, scalar=-c, in1=ang, op0=ALU.mult, op1=ALU.add)
                dve.drain()
            dve.tensor_scalar(ang, ang, 3.1415925, -3.1415925, ALU.min, ALU.max).then_inc(sig("angle"), 1)
            dve.wait_ge(sig("params_T"), 1)
            dve.tensor_copy(pcol[:, :], ps[:, 0, 0:NCOL]).then_inc(sig("pcol"), 1)
            dve.drain()
            turned(dve, scaled, 0, "g_mix", "xp_dve", 1)
            for name in ("g_mlp", "g_final"):
                g8 = pcol[:, PROW[name]:PROW[name] + KD]
                dve.tensor_scalar(g8, g8, A_POW, None, ALU.mult)
            dve.wait_ge(sig("sines"), 1)
            cos, sin = rope_cs[:, 0, :, :], rope_cs[:, 1, :, :]
            dve.tensor_tensor(cos, cos, cos, ALU.mult)
            dve.drain()
            dve.tensor_scalar(cos, cos, -2.0, 1.0, ALU.mult, ALU.add)
            dve.wait_ge(sig("w_used"), 2)
            for t in range(T):
                ins = dve.tensor_copy(u_cqkv[:, T * QL + 288 * t:T * QL + 288 * t + 288], ps[:, 2 + t, 0:288])
            ins.then_inc(sig("out_by_dve"), 1)
            dve.drain()
            dve.wait_ge(sig("out_by_act"), 1)
            mean_square(cq, QL, 0, junk)
            mean_square(ckv[:, :, 0:KVL], KVL, 2, junk).then_inc(sig("ms_ready"), 1)
            dve.wait_ge(sig("rstd_ready"), 2)
            for t in range(T):
                scaled(cq[:, t, :], cq[:, t, :], rstd[:, t:t + 1])
                ins = scaled(ckv[:, t, 0:KVL], ckv[:, t, 0:KVL], rstd[:, 2 + t:3 + t])
            ins.then_inc(sig("mla_normed"), 1)
            dve.wait_ge(sig("pool_d"), 1)
            dve.tensor_copy(u_dT, ps[:, 4:6, :].rearrange("p b s -> p (b s)")).then_inc(sig("dT"), 1)
            dve.wait_ge(sig("w_used"), 5)
            xb_in = xbT[:, :, CONV - 1:]
            dve.tensor_copy(xb_in[:, 0:2, :], ps[:, 0, :].rearrange("p (c s) -> p c s", c=2))
            dve.tensor_copy(xb_in[:, 2, :], ps[:, 1, 0:S]).then_inc(sig("out_by_dve"), 1)
            dve.wait_ge(sig("cT_pe"), 1)
            for k in range(5):
                gain = pcols("q_norm", k) if k < 3 else pcols("kv_norm", k - 3)
                ins = scaled(cT[:, k, :], ps[:, 4 + k // 2, (k % 2) * S:(k % 2) * S + S], gain)
            ins.then_inc(sig("cT"), 1)

            def rope(x, heads, t4):
                def cs(c):
                    return c.unsqueeze(2).broadcast_to([P, T, heads, 16]) if heads > 1 else c
                lo, hi = (x[:, :, :, 0:16], x[:, :, :, 16:32]) if heads > 1 else (x[:, :, 0:16], x[:, :, 16:32])
                dve.tensor_tensor(t4[0], lo, cs(cos), ALU.mult)
                dve.tensor_tensor(t4[1], hi, cs(sin), ALU.mult)
                dve.tensor_tensor(t4[2], hi, cs(cos), ALU.mult)
                dve.tensor_tensor(t4[3], lo, cs(sin), ALU.mult)
                dve.drain()
                dve.tensor_tensor(lo, t4[0], t4[1], ALU.subtract)
                return dve.tensor_tensor(hi, t4[2], t4[3], ALU.add)

            dve.wait_ge(sig("q_out"), 1)
            rope(q_tok[:, :, :, NOPE:], MH, [rope_tmp[:, i, :].rearrange("p (t h f) -> p t h f", t=T, h=MH)
                                             for i in range(4)]).then_inc(sig("q_roped"), 1)
            dve.wait_ge(sig("w_used"), 7)
            dve.tensor_copy(xb_in[:, 3:5, :], ps[:, 2, :].rearrange("p (c s) -> p c s", c=2))
            dve.tensor_copy(xb_in[:, 5, :], ps[:, 3, 0:S])
            dve.tensor_tensor(sp_v[:, 0:16].rearrange("p (t h) -> p t h", t=T),
                              ps[:, 3, S:S + 16].rearrange("p (t h) -> p t h", t=T),
                              brow[:, 0:8].unsqueeze(1).broadcast_to([P, T, MH]), ALU.add)\
                .then_inc(sig("out_by_dve"), 1)
            dve.tensor_scalar(sp_v[:, 16:20], pcol[:, PROW["lru_lambda"]:PROW["lru_lambda"] + 4], -1.0, None, ALU.mult)
            dve.drain()
            dve.scalar_tensor_tensor(out=sp_a[:, :], in0=sp_v[:, :], scalar=-1.0, in1=sp_v[:, :], op0=ALU.mult, op1=ALU.max)\
                .then_inc(sig("sp_abs"), 1)
            rope(ckv[:, :, KVL:288], 1, [rope_tmp[:, i, 0:32].rearrange("p (t f) -> p t f", t=T) for i in range(4)])
            dve.drain()
            dve.wait_ge(sig("kv_out"), 1)
            for t in range(T):
                ins = dve.tensor_copy(k_tok[:, t, :, NOPE:], ckv[:, t:t + 1, KVL:288].broadcast_to([P, MH, ROPE]))
            ins.then_inc(sig("k_roped"), 1)

            def conv(dst, src, chunks, w, b):
                for j in range(CONV):
                    for c in range(chunks):
                        win = src[:, c, j:j + S]
                        if j == 0:
                            ins = dve.tensor_scalar(dst[:, c, :], win, pcols(w, c), pcols(b, c), ALU.mult, ALU.add)
                        else:
                            ins = dve.scalar_tensor_tensor(out=dst[:, c, :], in0=win, scalar=pcols(w, j * chunks + c),
                                                           in1=dst[:, c, :], op0=ALU.mult, op1=ALU.add)
                    if j < CONV - 1:
                        dve.drain()
                return ins

            dve.wait_ge(sig("lru_zeroed"), 1)
            conv(xbS, xbT, KX, "ssd_conv_w", "ssd_conv_b").then_inc(sig("x_conv"), 1)
            dve.wait_ge(sig("w_used"), 10)
            dve.tensor_copy(lxT[:, :, CONV - 1:], ps[:, 2:4, :].rearrange("p b (c s) -> p (b c) s", c=2))\
                .then_inc(sig("out_by_dve"), 1)
            dve.wait_ge(sig("sp_ln"), 1)
            dve.scalar_tensor_tensor(out=sp_v[:, :], in0=sp_v[:, :], scalar=0.0, in1=sp_e[:, :], op0=ALU.max, op1=ALU.add)
            dve.drain()
            dve.tensor_copy(stats[:, 0:16], sp_v[:, 0:16])
            dve.tensor_scalar(decay8[:, :], sp_v[:, 16:20], 8.0, None, ALU.mult)
            dve.drain()
            dve.scalar_tensor_tensor(out=a_tok, in0=dt_tok, scalar=-1.0,
                                     in1=a_head[:, :].unsqueeze(1).broadcast_to([P, T, MH]),
                                     op0=ALU.mult, op1=ALU.mult).then_inc(sig("a_tok"), 1)
            conv(xcT, lxT, KM, "lru_conv_w", "lru_conv_b").then_inc(sig("xcT"), 1)

            def mla_max(h):
                dve.wait_ge(sig("mla_scores"), h + 1)
                if h:
                    dve.wait_ge(sig("mla_pT_pe"), h)
                dve.tensor_tensor_reduce(probs[:, 0:P], ps[:, 4, 0:P], cmask, MLA_SCALE, -3e38, ALU.add, ALU.max,
                                         mx[:, 0:1])
                dve.tensor_tensor_reduce(probs[:, P:384], ps[:, 4, P:384], zc_mask[:, :], MLA_SCALE, -3e38,
                                         ALU.add, ALU.max, mx[:, 1:2])
                dve.drain()
                dve.tensor_scalar(mx, mx, -1.0, None, ALU.mult).then_inc(sig("mla_max"), 1)

            def mla_turned(h):
                dve.wait_ge(sig("mla_pT_pe"), h + 1)
                dve.tensor_copy(probsT, ps[:, 5, 0:384]).then_inc(sig("mla_pT"), 1)
                d = 2 * (h % 2)
                dve.drain()
                dve.reciprocal(den[:, 4 + d:6 + d], den[:, d:d + 2])

            def mla_o(h):
                d = 2 * (h % 2)
                dve.drain()
                dve.wait_ge(sig("mla_pv"), h + 1)
                for t in range(T):
                    ins = scaled(o_mla[:, t, 64 * h:64 * h + 64], ps[:, 5, 384 + 64 * t:448 + 64 * t],
                                 den[:, 4 + d + t:5 + d + t])
                ins.then_inc(sig("mla_o"), 1)

            def cb_mask():
                dve.wait_ge(sig("cb_pe"), 1)
                for gr in range(2):
                    ins = dve.tensor_tensor(cbm[:, gr, :], ps[:, 6 + gr, 0:384], tri3, ALU.mult)
                ins.then_inc(sig("cbm"), 1)

            def ssd_xdt():
                dve.wait_ge(sig("acs_pe"), 1)
                dve.tensor_copy(stats[:, 32:48], ps[:, 6, 0:16]).then_inc(sig("acs"), 1)
                dve.wait_ge(sig("xs_tok"), 1)
                dve.tensor_tensor(xdt.rearrange("p t (h d) -> p (t h) d", d=64),
                                  xs_tok.rearrange("p t (h d) -> p (t h) d", d=64),
                                  stats[:, 0:16].unsqueeze(2).broadcast_to([P, 16, 64]), ALU.mult).then_inc(sig("xdt"), 1)

            def decay(half):
                dve.wait_ge(sig("cum_pe"), half + 1)
                dve.drain()
                for j in range(4):
                    h = 4 * half + j
                    src = ps[:, 6 + j // 2, (j % 2) * S:(j % 2) * S + S]
                    dve.tensor_scalar(dm[:, h, 0:S], src, acs[:, 0, h:h + 1], 0.0, ALU.subtract, ALU.min)
                    ins = dve.tensor_scalar(dm[:, h, S:384], src[:, P:S], acs[:, 1, h:h + 1], 0.0, ALU.subtract, ALU.min)
                ins.then_inc(sig("dm"), 1)

            def decay_cb():
                for half in range(2):
                    dve.wait_ge(sig("dm_exp"), half + 1)
                    for j in range(4):
                        ins = dve.tensor_tensor(dm[:, 4 * half + j, :], dm[:, 4 * half + j, :], cbm[:, half, :], ALU.mult)
                ins.then_inc(sig("dm_cb"), 1)

            def lru_log():
                dve.wait_ge(sig("lru_r"), 1)
                for c in range(KM):
                    ins = scaled(lru_r[:, c, :], lru_r[:, c, :], decay8[:, c:c + 1])
                ins.then_inc(sig("lru_nl"), 1)

            def ssd_out():
                dv = y_ssd.rearrange("p t (h d) -> p t h d", h=MH)
                for t in range(T):
                    dve.tensor_tensor(dv[:, t, :, :], xs_tok[:, t, :].rearrange("p (h d) -> p h d", h=MH),
                                      brow[:, 16:24].unsqueeze(2).broadcast_to([P, MH, 64]), ALU.mult)
                dve.drain()
                dve.wait_ge(sig("ssd_y_pe"), 1)
                dve.tensor_tensor(y_ssd, y_ssd, ps[:, 6:8, :], ALU.add).then_inc(sig("ssd_y"), 1)
                dve.drain()
                dve.tensor_tensor(y_ssd, y_ssd, z_silu, ALU.mult)
                dve.drain()
                mean_square(y_ssd, MIX, 0, xs_tok).then_inc(sig("ms_ready"), 1)
                dve.wait_ge(sig("rstd_ready"), 3)
                for t in range(T):
                    ins = scaled(y_ssd[:, t, :], y_ssd[:, t, :], rstd[:, t:t + 1])
                ins.then_inc(sig("ssd_normed"), 1)

            def lru_input():
                dve.wait_ge(sig("lru_at"), 1)
                sq = xs_tok.rearrange("p t n -> p (t n)").rearrange("p (c s) -> p c s", c=KM)
                dve.drain()
                dve.tensor_tensor(sq, lru_a, lru_a, ALU.mult)
                dve.drain()
                dve.scalar_tensor_tensor(out=lru_t, in0=sq, scalar=1.0, in1=lru_t, op0=ALU.add, op1=ALU.mult)\
                    .then_inc(sig("lru_sq"), 1)
                dve.wait_ge(sig("lru_i"), 1)
                dve.tensor_tensor(lru_i, lru_i, xcT, ALU.mult)

            def pool_out():
                dve.wait_ge(sig("pool_y"), 1)
                for c in range(KM):
                    ins = scaled(ybT[:, c, :], ps[:, 6 + c // 2, (c % 2) * S:(c % 2) * S + S], pcols("pool_scale", c))
                ins.then_inc(sig("ybT"), 1)

            def lru_scan():
                dve.wait_ge(sig("lru_root"), 1)
                dve.drain()
                dve.tensor_tensor(lru_i, lru_i, lru_t, ALU.mult)
                dve.drain()
                for c in range(KM):
                    dve.tensor_tensor_scan(lru_r[:, c, :], lru_a[:, c, :], lru_i[:, c, :], 0.0, ALU.mult, ALU.add)
                dve.drain()
                dve.tensor_tensor(lru_g, lru_g, lru_r, ALU.mult).then_inc(sig("ydT"), 1)

            def ssd_turned():
                dve.wait_ge(sig("ycT_pe"), KM)
                for c in range(KM):
                    ins = scaled(ycT[:, c, :], ps[:, 6 + c // 2, (c % 2) * S:(c % 2) * S + S], pcols("ssd_norm", c))
                ins.then_inc(sig("ycT"), 1)

            extra = {0: [cb_mask], 1: [ssd_xdt], 2: [lambda: decay(0)], 3: [lambda: decay(1), decay_cb],
                     4: [lru_log], 5: [ssd_out], 6: [lru_input, pool_out], 7: [lru_scan, ssd_turned]}
            dve.memset(zc_mask[:, 0:P], 0.0)
            dve.tensor_copy(zc_mask[:, P:S], cmask)
            dve.drain()
            for i in range(8):
                if i >= 2:
                    mla_o(i - 2)
                if i:
                    mla_turned(i - 1)
                mla_max(i)
                for f in extra[i]:
                    f()
            mla_o(MH - 2)
            mla_turned(MH - 1)
            mla_o(MH - 1)
            for i, b in enumerate((1, 0, 3, 2)):
                if i < 3:
                    dve.wait_ge(sig("w_used"), 19 + i)
                if i == 0:
                    dve.wait_ge(sig("out_by_act"), 12)
                for t in range(T):
                    if i == 3 and t == 0:
                        dve.wait_ge(sig("branch_first"), 1)
                    elif i == 3:
                        dve.wait_ge(sig("w_used"), 19 + i)
                    y = ps[:, 4 * (i % 2) + 2 * t:4 * (i % 2) + 2 * t + 2, :].rearrange("p b n -> p (b n)")
                    gt = gates[:, t, D * b:D * b + D]
                    ins = dve.tensor_tensor(gt if i else x_norm[:, t, :], y, gt, ALU.mult)
                    if t == T - 1:
                        ins.then_inc(sig("branch"), 1)
                    dve.drain()
                    if i:
                        ins = dve.tensor_tensor(x_norm[:, t, :], x_norm[:, t, :], gt, ALU.add)
                        if i == 3:
                            ins.then_inc(sig(f"xn{t}_ready"), 1)
            turned(dve, scaled, 1, None, "xp_dve", 1)
            w_low(FF0, 0, ff_w[0])
            dve.wait_ge(sig("ld_x"), 32)
            dve.wait_ge(sig("w_used"), 23)
            dve.tensor_tensor(x_tok[:, :, 0:512], x_tok[:, :, 0:512], ps[:, 0:2, :], ALU.add)
            dve.drain()
            for t in range(T):
                squares(t, slice(0, 512), ms_part[:, 0, t:t + 1])
            for t in range(T):
                tile_done(1, t, 24)
                ins = dve.tensor_tensor(x_tok[:, t, 512:], x_tok[:, t, 512:], ps[:, 2 + t, :], ALU.add)
                if t:
                    ins.then_inc(sig("x_res"), 1)
                dve.drain()
                squares(t, slice(512, D), ms_part[:, 1, t:t + 1])
                halves_sum(t)
                rms_tile(3, t)
            turned_low(2, "g_mlp", ff_parts)
            w_low(FF0, 1, ff_w[1])
            for i in range(14):
                if i < 8:
                    v = hid_tmp[i % 2]
                    v3 = v.rearrange("p (c s) -> p c s", c=4)
                    dve.wait_ge(sig("ff1_low"), i + 1)
                    dve.scalar_tensor_tensor(out=v3, in0=banks(i)[0], scalar=H_POW ** 0.5 / SUM_POW, in1=v3,
                                             op0=ALU.mult, op1=ALU.add).then_inc(sig("ff1_out"), 1)
                    dve.drain()
                    dve.scalar_tensor_tensor(out=v, in0=v, scalar=0.0, in1=v, op0=ALU.max, op1=ALU.mult)\
                        .then_inc(sig("ff1_square"), 1)
                if i == 9:
                    dve.wait_ge(sig("rel_pe"), 1)
                    dve.tensor_copy(rel_row, ps[0:H2, 5, 0:384]).then_inc(sig("rel_row"), 1)
                w_low(FF0, i + 2, ff_w[i % 2])
                if i < 8:
                    dve.wait_ge(sig("hid_hi"), i + 1)
                    dve.drain()
                    dve.tensor_tensor(hid_lo[:, 4 * i:4 * i + 4, :].rearrange("p c s -> p (c s)"), v,
                                      hid_hi[:, 4 * i:4 * i + 4, :].rearrange("p c s -> p (c s)"), ALU.subtract)\
                        .then_inc(sig("hid_lo"), 1)
            for t in range(T):
                tile_done(2, t, 40)
                ins = dve.scalar_tensor_tensor(out=x_tok[:, t, :], in0=ps[:, 2 * t:2 * t + 2, :].rearrange("p b n -> p (b n)"),
                                               scalar=1.0 / (W_POW * H_POW), in1=x_tok[:, t, :],
                                               op0=ALU.mult, op1=ALU.add)
                if t:
                    ins.then_inc(sig("x_res"), 1)
                dve.drain()
                squares(t, slice(0, D), ms[:, t:t + 1])
                rms_tile(4, t)
            turned(dve, scaled, 3, "g_ple", "xp_dve", 1)
            w_low(DIL0, 0, dil_w[0])
            def embedded(t, h):
                ts = slice(0, T) if t is None else slice(t, t + 1)
                xn, xt = (v[:, ts, 512 * h:512 * h + 512] for v in (x_norm, x_tok))
                y = ps[:, 0:4, :].rearrange("p (t h) n -> p t h n", h=2)[:, ts, h, :]
                ins = dve.tensor_tensor(xn, xn, y, ALU.mult)
                dve.drain()
                dve.tensor_tensor(xt, xt, xn, ALU.add)
                dve.drain()
                for u in range(T) if t is None else (t,):
                    squares(u, slice(512 * h, 512 * h + 512), ms_part[:, h, u:u + 1])
                return ins

            dve.wait_ge(sig("ple_gate"), 1)
            embedded(None, 0)
            for t in range(T):
                dve.wait_ge(sig("ple_gate"), 2 + t)
                embedded(t, 1)
                halves_sum(t)
                rms_tile(5, t)
            for _ in range(2):
                dve.engine_nop().then_inc(sig("qkv_out"), 1)
            turned_low(4, "g_final", dil_parts)
            dve.wait_ge(sig("x_full"), 1)
            w_low(DIL0, 1, dil_w[1])

            def qkv(n0, g, bufs, last):
                for s in range(6):
                    if s < 4:
                        d = (q2T, k2T)[s // 2][:, bass.ds(g, 1), 4 * (s % 2):4 * (s % 2) + 4, :]
                        d = d.rearrange("p o c s -> p (o c) s")
                        dve.wait_ge(sig("qkv_low"), (0 if n0 == DIL0 else 12) + s + 1 + g * 4)
                        ins = dve.scalar_tensor_tensor(out=d, in0=banks(s)[0], scalar=(0.125 if s < 2 else 1.0) / SUM_POW,
                                                       in1=d, op0=ALU.mult, op1=ALU.add)
                    else:
                        dve.wait_ge(sig("w_used"), n0 + s + 1 + g * 6)
                        d = v2[:, bass.ds(g, 1), :, 512 * (s % 2):512 * (s % 2) + 512].rearrange("p o t n -> p (o t) n")
                        ins = scaled(d, ps[:, 4 * (s % 2):4 * (s % 2) + T, :], 1.0 / SUM_POW)
                    ins.then_inc(sig("qkv_out"), 1)
                    if s < 4 or not last:
                        w_low(n0, s + 2, bufs[(s + 2) % 6], g)

            with dve.Fori(0, 2) as g:
                qkv(DIL0, g, dil_w, False)
            qkv(DIL0, 2, dil_w, True)

            def dil_max(h):
                dve.wait_ge(sig("dil_scores"), h + 1)
                dve.wait_ge(sig("bm"), h + 1)
                if h >= 2:
                    dve.wait_ge(sig("dil_pT_pe"), h - 1)
                e, m = e_dil[:, h % 2, :], mx4[:, 2 * (h % 2):2 * (h % 2) + 2]
                dve.tensor_tensor_reduce(e[:, 0:384].rearrange("p (g s) -> p g s", g=3),
                                         ps[:, 0, 0:384].rearrange("p (g s) -> p g s", g=3), bm[:, h % 2, :, P:S],
                                         1.0, -3e38, ALU.add, ALU.max, m[:, 0:1])
                dve.tensor_tensor_reduce(e[:, 384:], ps[:, 1:3, :].rearrange("p b n -> p (b n)")[:, 0:768],
                                         bm[:, h % 2, :, :].rearrange("p g s -> p (g s)"),
                                         1.0, -3e38, ALU.add, ALU.max, m[:, 1:2])
                dve.drain()
                dve.tensor_scalar(m, m, -1.0, None, ALU.mult).then_inc(sig("dil_max"), 1)

            def dil_o(h):
                d = 2 * (h % 2)
                dve.wait_ge(sig("dil_pv"), h + 1)
                for t in range(T):
                    ins = scaled(x_norm[:, t, 64 * h:64 * h + 64], ps[:, 6 + h % 2, 64 * t:64 * t + 64],
                                 den[:, 4 + d + t:5 + d + t])
                ins.then_inc(sig("dil_o"), 1)

            dve.wait_ge(sig("x_full"), 1)
            dil_max(0)
            for h in range(H2):
                if h + 1 < H2:
                    dil_max(h + 1)
                dve.wait_ge(sig("dil_pT_pe"), h + 1)
                dve.tensor_copy(eT_two[h % 2][1], ps[:, 4:6, :].rearrange("p b n -> p (b n)")[:, 0:768])\
                    .then_inc(sig("dil_pT_dve"), 1)
                d = 2 * (h % 2)
                dve.drain()
                dve.reciprocal(den[:, 4 + d:6 + d], den[:, d:d + 2])
                if h:
                    dil_o(h - 1)
            dve.drain()
            dil_o(H2 - 1)
            both_tiles()
            turned(dve, scaled, 5, None, "xp_dve", 1)

            def w_split(n0, b, j):
                n = n0 + b
                dve.wait_ge(sig("w_hi"), split_index(n0) + b + 1 + j * 3)
                dve.scalar_tensor_tensor(out=w_lo[:, n % 3, :], in0=w_ring[:, n % RING, :], scalar=W_POW,
                                         in1=w_hi[:, n % 3, :], op0=ALU.mult, op1=ALU.subtract).then_inc(sig("w_lo"), 1)

            def last_tile(t):
                dve.wait_ge(sig("ld_gb"), 16 + 32 * 4)
                dve.scalar_tensor_tensor(out=x_norm[:, t, :], in0=x_tok[:, t, :], scalar=bn_mv[:, t, 0:1],
                                         in1=ln_gb[:, 0, :], op0=ALU.subtract, op1=ALU.mult)
                dve.drain()
                dve.wait_ge(sig("rstd_ready"), norm_count(9, t))
                for h in range(2):
                    c = slice(512 * h, 512 * h + 512)
                    dve.scalar_tensor_tensor(out=x_tok[:, t, c], in0=x_norm[:, t, c], scalar=rstd[:, t:t + 1],
                                             in1=ln_gb[:, 1, c], op0=ALU.mult, op1=ALU.add).then_inc(sig("out_ready"), 1)

            def layer_norm(m):
                after_experts = m % 2
                pow2 = SUM_POW if after_experts else 1.0
                dve.wait_ge(sig("x_full"), m + 1)

                def add(dst, src):
                    dve.scalar_tensor_tensor(out=dst, in0=dst, scalar=ALPHA * pow2, in1=src, op0=ALU.mult, op1=ALU.add)
                    dve.drain()

                def part(t, h):
                    dve.bn_stats(bn_part[:, t, h, :], x_tok[:, t, 512 * h:512 * h + 512])

                if not after_experts:
                    dve.wait_ge(sig("w_used"), (DOUT0, SBO0)[m // 2] + 1)
                    add(x_tok[:, :, 0:512], ps[:, 0:2, :])
                    for t in range(T):
                        part(t, 0)
                for t in range(T):
                    tile_done(4 + m, t, (DOUT0 + 2, MOE0 + 24, SBO0 + 2, MOE1 + 24)[m])
                    if after_experts:
                        add(x_tok[:, t, :], ps[:, 2 * t:2 * t + 2, :].rearrange("p b n -> p (b n)"))
                        part(t, 0)
                    else:
                        add(x_tok[:, t, 512:], ps[:, 2 + t, :])
                    part(t, 1)
                    dve.drain()
                    dve.bn_aggr(bn_mv[:, t, :], bn_part[:, t, :, :])
                    dve.drain()
                    dve.tensor_scalar(ms[:, t:t + 1], bn_mv[:, t, 1:2], LN_EPS * pow2 * pow2, None, ALU.add)\
                        .then_inc(sig("ms_ready"), 1)
                    if m < 3:
                        scale_tile(6 + m, t, bn_mv[:, t, 0:1])
                    else:
                        last_tile(t)

            def rank_of_four(v, rank, tmp, init):
                dve.tensor_copy(rank, init)
                dve.drain()
                for s in (1, 2, 3):
                    c = tmp[:, :, 0:4 - s]
                    dve.tensor_tensor(c, v[:, :, 0:4 - s], v[:, :, s:4], ALU.is_ge)
                    dve.drain()
                    dve.tensor_tensor(rank[:, :, s:4], rank[:, :, s:4], c, ALU.add)
                    dve.drain()
                    dve.tensor_tensor(rank[:, :, 0:4 - s], rank[:, :, 0:4 - s], c, ALU.subtract)
                    dve.drain()

            def experts(layer, n0, turn):
                turned(dve, scaled, turn, None, "xp_dve", 1, 2 * layer)
                dve.wait_ge(sig("xp_act"), 4 * turn + 4)
                dve.drain()
                for t in range(T):
                    c = slice(t * P, (t + 1) * P)
                    dve.wait_ge(sig("aT_hi"), 4 * layer + t + 1)
                    dve.scalar_tensor_tensor(out=aT_lo[:, :, c], in0=actT[:, :, c], scalar=A_POW, in1=aT_hi[:, :, c],
                                             op0=ALU.mult, op1=ALU.subtract).then_inc(sig("aT_lo"), 1)
                w_split(n0, 1, 0)
                g4 = lambda v: v.rearrange("p (g e) -> p g e", e=4)
                tg = lambda v: v.rearrange("p (t e) -> p t e", t=T)
                dve.wait_ge(sig("router_exp"), layer + 1)
                dve.tensor_scalar(score, score, 1.0, None, ALU.add)
                dve.drain()
                dve.reciprocal(score, score)
                dve.drain()
                dve.tensor_tensor(tg(r_v), tg(score), brow[:, 24:40].unsqueeze(1).broadcast_to([P, T, NE]), ALU.add)
                dve.drain()
                rank_of_four(g4(r_v), g4(r_rank), g4(r_cmp), rank0)
                dve.tensor_scalar(r_sel, r_rank, 2.0, None, ALU.is_lt)
                dve.drain()
                dve.tensor_tensor(r_cmp, r_sel, r_v, ALU.mult)
                dve.drain()
                dve.tensor_reduce(r_gs, g4(r_cmp), AX.X, ALU.add)
                dve.drain()
                rank_of_four(g4(r_gs), g4(r_gr), g4(r_best), rank0[:, 0:T, :])
                dve.tensor_scalar(r_best, r_gr, 1.0, None, ALU.is_lt)
                dve.drain()
                dve.tensor_tensor(g4(r_sel), g4(r_sel), r_best.unsqueeze(2).broadcast_to([P, 8, 4]), ALU.mult)
                dve.drain()
                dve.tensor_tensor(r_sel, r_sel, score, ALU.mult)
                dve.drain()
                dve.tensor_reduce(r_den[:, 0:T], tg(r_sel), AX.X, ALU.add)
                dve.drain()
                dve.reciprocal(r_den[:, 2:2 + T], r_den[:, 0:T])
                dve.drain()
                dve.scalar_tensor_tensor(out=tg(r_gate), in0=tg(r_sel), scalar=A_POW / SUM_POW,
                                         in1=r_den[:, 2:2 + T].unsqueeze(2).broadcast_to([P, T, NE]),
                                         op0=ALU.mult, op1=ALU.mult)
                dve.drain()

                def next_split(b, j, last):
                    if not last:
                        w_split(n0 + 3, b, j)
                    elif layer == 0:
                        w_low(SBI0, b, sbq_w[b])

                def weigh(b, j):
                    dve.wait_ge(sig("moe_silu"), NE * layer + b + 1 + j * 2)
                    for t in range(T):
                        ins = dve.scalar_tensor_tensor(out=h_tok[:, b, t, :], in0=ps[:, 4 + 2 * b + t, DE:2 * DE],
                                                       scalar=r_gate[:, bass.ds(2 * j + b + t * NE, 1)],
                                                       in1=e_silu[:, b, t, :], op0=ALU.mult, op1=ALU.mult)
                    ins.then_inc(sig("moe_h"), 1)

                def h_low(b, j):
                    dve.wait_ge(sig("moe_hT_hi"), NE * layer + 1 + b + j * 2)
                    dve.tensor_tensor(hT_lo[:, b, :], ps[:, 4 + 2 * b, :], hT_hi[:, b, :], ALU.subtract)\
                        .then_inc(sig("moe_hT"), 1)

                def pair(j, last):
                    weigh(0, j)
                    w_split(n0, 2, j)
                    h_low(0, j)
                    next_split(0, j, last)
                    weigh(1, j)
                    if not last:
                        next_split(1, j, last)
                    h_low(1, j)

                with dve.Fori(0, NE // 2 - 1) as j:
                    pair(j, False)
                pair(NE // 2 - 1, True)

            w_split(MOE0, 0, 0)
            layer_norm(0)
            experts(0, MOE0, 6)
            layer_norm(1)
            turned(dve, scaled, 7, None, "xp_dve", 1, 1)
            dve.wait_ge(sig("xp_act"), 4 * 7 + 4)
            dve.drain()
            for i in range(2):
                k = slice(4 * i, 4 * i + 4)
                dve.wait_ge(sig("aT_hi"), 3 + i)
                dve.scalar_tensor_tensor(out=sbq_parts[0][:, k, S:2 * S], in0=actT[:, k, :], scalar=A_POW,
                                         in1=sbq_parts[0][:, k, 0:S], op0=ALU.mult, op1=ALU.subtract)\
                    .then_inc(sig("aT_lo"), 1)
            w_low(SBI0, 1, sbq_w[1])
            qkv(SBI0, 0, sbq_w, True)

            mask2 = strict3.unsqueeze(1).broadcast_to([P, 2, 384])

            def sb_clip(m):
                dve.wait_ge(sig("sb_z"), m + 1)
                if m >= SBN:
                    dve.wait_ge(sig("sb_pv"), m - SBN + 1)
                z, b = sb_zt[m % SBN], 2 * (m % 2)
                dve.tensor_scalar(z, ps[:, b:b + 2, 0:384], SB_CLIP, -SB_CLIP, ALU.min, ALU.max)
                dve.drain()
                dve.tensor_scalar(sb_e[m % SBN], z, LN_TOP, None, ALU.min).then_inc(sig("sb_zc"), 1)
                dve.tensor_scalar(sb_h[m % SBN], z, -LN_TOP, 0.0, ALU.add, ALU.max)

            def sb_sp(m):
                dve.wait_ge(sig("sb_ln"), m + 1)
                v = sb_l[m % SBN]
                dve.drain()
                dve.tensor_tensor(v, v, sb_h[m % SBN], ALU.add)
                dve.drain()
                dve.tensor_tensor(v, v, mask2, ALU.mult).then_inc(sig("sb_sp"), 1)

            def sb_att(m):
                dve.wait_ge(sig("sb_r"), m + 1)
                v = sb_e[m % SBN]
                dve.tensor_tensor(v, sb_zt[m % SBN], ps[:, 4:6, 0:384], ALU.subtract).then_inc(sig("sb_d"), 1)

            def sb_mask(m):
                dve.wait_ge(sig("sb_exp"), m + 1)
                v = sb_e[m % SBN]
                dve.tensor_tensor(v, v, mask2, ALU.mult).then_inc(sig("sb_att"), 1)

            def sb_o(m):
                dve.wait_ge(sig("sb_pv"), m + 1)
                dve.tensor_copy(x_norm[:, :, P * m:P * m + P], ps[:, 6 + m % 2, 0:S].rearrange("p (t n) -> p t n", t=T))\
                    .then_inc(sig("sb_o"), 1)

            dve.wait_ge(sig("x_full"), 3)
            for i in range(H2 // 2 + 4):
                staged(i, (sb_att, 2), (sb_sp, 1), (sb_clip, 0), (sb_mask, 3), (sb_o, 4))
            both_tiles()
            turned(dve, scaled, 8, None, "xp_dve", 1)
            w_split(MOE1, 0, 0)
            layer_norm(2)
            experts(1, MOE1, 9)
            layer_norm(3)

_SHAPES_IN = ("x", "p", "positions", "w_in", "w_uq", "w_ukv", "w_pool", "g_final",
              "lru_w_a", "lru_w_i", "w_branch", "w_out", "w_ff1", "w_ff2", "w_ple_gate", "w_ple",
              "rel_table_2", "router_w_2", "ln1_g_2", "ln1_b_2", "ln2_g_2", "ln2_b_2",
              "exp_w_gate_2", "exp_w_up_2", "exp_w_down_2", "dil_w_in_2", "dil_w_out_2", "sb_w_in_2",
              "sb_w_out_2")


def kernel(**inputs):
    import concourse.bacc as bacc
    from concourse.bass_utils import run_bass_kernel_spmd

    nc = bacc.Bacc("TRN2", target_bir_lowering=False, num_devices=1)
    arrays, aps = {}, {}
    named = [(n, inputs[n]) for n in _SHAPES_IN] + list(constants().items())
    rows = [np.asarray(inputs[n]).reshape(-1, P) for n, _ in PARAM_ROWS]
    rows += [np.asarray(inputs[n])[layer].reshape(-1, P) for n, layer in LN_ROWS]
    flat = [np.asarray(inputs[n]).reshape(-1) for n in ("ssd_dt_bias", "ssd_a_log", "ssd_d", "router_b_2")]
    named += [("p_rows", np.concatenate(rows, 0)), ("p_brow", np.concatenate(flat))]
    for name, value in named:
        if name == "positions":
            value = np.asarray(value).reshape(T, P).T
        v = np.ascontiguousarray(value)
        arrays["in_" + name] = v
        aps[name] = nc.dram_tensor("in_" + name, v.shape, mybir.dt.from_np(v.dtype), kind="ExternalInput").ap()
    out = nc.dram_tensor("out_0", (1, S, D), F32, kind="ExternalOutput").ap()
    build(nc, aps, out)
    r = run_bass_kernel_spmd(nc, [arrays], core_ids=[0])
    return r.results[0]["out_0"]
```
